# Optimizing a Trainium2 kernel written in Bass

```python
import jax, jax.numpy as jnp
from jax import lax
import numpy as np

D_MODEL = 1024
BATCH = 1
SEQ = 1024
DEPTH = 2
DEC_BATCH = 8
DEC_SEQ = 16
PAST_LEN = 128

CHUNK = 64
N_HEADS = 16
HEAD_DIM = D_MODEL // N_HEADS
N_A_LAYERS = DEPTH // 2
N_B_LAYERS = DEPTH - N_A_LAYERS
BAND_CHUNKS = 8
BAND_PAST = BAND_CHUNKS * CHUNK
REL_CLIP = 128
N_REL = 2 * REL_CLIP + 1
D_FF = ((8 * D_MODEL // 3 + 255) // 256) * 256
Q_BLOCK = 128
EPS = 1e-6
NEG_INF = -1e30

kernel_name = "fox_yoco_chunkband_stream_step"

def rms_norm(x, g):
    xf = x.astype(jnp.float32)
    y = xf * lax.rsqrt(jnp.mean(xf * xf, axis=-1, keepdims=True) + EPS)
    return (y * g.astype(jnp.float32)).astype(x.dtype)

def swiglu(x, w_gate_up, w_down):
    gate, up = jnp.split(x @ w_gate_up, 2, axis=-1)
    return (jax.nn.silu(gate) * up) @ w_down

def split_heads(t):
    return t.reshape(t.shape[0], t.shape[1], N_HEADS, HEAD_DIM)

def merge_heads(t):
    return t.reshape(t.shape[0], t.shape[1], D_MODEL)

def fox_project(h, w_in, b_f):
    proj = h @ w_in
    q, k, v, f = jnp.split(proj, [D_MODEL, 2 * D_MODEL, 3 * D_MODEL], axis=-1)
    logf = jax.nn.log_sigmoid((f + b_f).astype(jnp.float32))
    return split_heads(q), split_heads(k), split_heads(v), logf

def fox_attention_prompt(q, k, v, logf):
    bsz, s_len = q.shape[0], q.shape[1]
    scale = HEAD_DIM ** -0.5
    cum = jnp.transpose(jnp.cumsum(logf, axis=1), (0, 2, 1))
    key_pos = jnp.arange(s_len)

    def block(i):
        start = i * Q_BLOCK
        qb = lax.dynamic_slice_in_dim(q, start, Q_BLOCK, axis=1)
        cq = lax.dynamic_slice_in_dim(cum, start, Q_BLOCK, axis=2)
        s = jnp.einsum('bqhd,bkhd->bhqk', qb, k).astype(jnp.float32) * scale
        s = s + cq[..., :, None] - cum[..., None, :]
        qpos = start + jnp.arange(Q_BLOCK)
        s = jnp.where(key_pos[None, :] <= qpos[:, None], s, NEG_INF)
        p = jax.nn.softmax(s, axis=-1).astype(v.dtype)
        return jnp.einsum('bhqk,bkhd->bqhd', p, v)

    out = lax.map(block, jnp.arange(s_len // Q_BLOCK))
    return jnp.moveaxis(out, 0, 1).reshape(bsz, s_len, N_HEADS, HEAD_DIM)

def fox_attention_sample(q, k_all, v_all, logf_all, past):
    t_len = q.shape[1]
    scale = HEAD_DIM ** -0.5
    cum = jnp.transpose(jnp.cumsum(logf_all, axis=1), (0, 2, 1))
    s = jnp.einsum('bqhd,bkhd->bhqk', q, k_all).astype(jnp.float32) * scale
    s = s + cum[..., past:, None] - cum[..., None, :]
    qpos = past + jnp.arange(t_len)
    kpos = jnp.arange(k_all.shape[1])
    s = jnp.where(kpos[None, :] <= qpos[:, None], s, NEG_INF)
    p = jax.nn.softmax(s, axis=-1).astype(v_all.dtype)
    return jnp.einsum('bhqk,bkhd->bqhd', p, v_all)

def rel_index(dist):
    return jnp.clip(dist, -REL_CLIP, REL_CLIP) + REL_CLIP

def band_attention_prompt(q, k, v, rel_bias):
    bsz, s_len = q.shape[0], q.shape[1]
    scale = HEAD_DIM ** -0.5
    band = BAND_PAST + CHUNK
    pad = ((0, 0), (BAND_PAST, 0), (0, 0), (0, 0))
    kp = jnp.pad(k, pad)
    vp = jnp.pad(v, pad)
    qi = jnp.arange(CHUNK)
    kj = jnp.arange(band)
    bias = rel_bias[:, rel_index(qi[:, None] + BAND_PAST - kj[None, :])].astype(jnp.float32)

    def chunk(c):
        qs = lax.dynamic_slice_in_dim(q, c * CHUNK, CHUNK, axis=1)
        ks = lax.dynamic_slice_in_dim(kp, c * CHUNK, band, axis=1)
        vs = lax.dynamic_slice_in_dim(vp, c * CHUNK, band, axis=1)
        s = jnp.einsum('bqhd,bkhd->bhqk', qs, ks).astype(jnp.float32) * scale + bias
        key_pos = c * CHUNK - BAND_PAST + kj
        s = jnp.where((key_pos >= 0)[None, :], s, NEG_INF)
        p = jax.nn.softmax(s, axis=-1).astype(vs.dtype)
        return jnp.einsum('bhqk,bkhd->bqhd', p, vs)

    out = lax.map(chunk, jnp.arange(s_len // CHUNK))
    return jnp.moveaxis(out, 0, 1).reshape(bsz, s_len, N_HEADS, HEAD_DIM)

def band_attention_sample(q, k_all, v_all, rel_bias, past):
    t_len, l_len = q.shape[1], k_all.shape[1]
    w_len = l_len - t_len
    scale = HEAD_DIM ** -0.5
    qpos = past + jnp.arange(t_len)
    kpos = past - w_len + jnp.arange(l_len)
    qc = qpos // CHUNK
    kc = kpos // CHUNK
    mask = (kc[None, :] <= qc[:, None]) & (kc[None, :] >= qc[:, None] - BAND_CHUNKS)
    bias = rel_bias[:, rel_index(qpos[:, None] - kpos[None, :])].astype(jnp.float32)
    s = jnp.einsum('bqhd,bkhd->bhqk', q, k_all).astype(jnp.float32) * scale + bias
    s = jnp.where(mask, s, NEG_INF)
    p = jax.nn.softmax(s, axis=-1).astype(v_all.dtype)
    return jnp.einsum('bhqk,bkhd->bqhd', p, v_all)

def shared_kv(h, g_kv, w_kv):
    kb, vb = jnp.split(rms_norm(h, g_kv) @ w_kv, 2, axis=-1)
    return split_heads(kb), split_heads(vb)

def setup_inputs(seed: int = 0) -> dict:
    key = jax.random.key(seed)
    ks = jax.random.split(key, 24)
    f32 = jnp.float32
    d_in = D_MODEL ** -0.5
    b_len = min(BAND_PAST, PAST_LEN)
    nrm = lambda k, shape, s: jax.random.normal(k, shape, f32) * s
    return {
        "x_prompt": nrm(ks[0], (BATCH, SEQ, D_MODEL), 1.0),
        "x_sample": nrm(ks[1], (DEC_BATCH, DEC_SEQ, D_MODEL), 1.0),
        "cache_a_k": nrm(ks[2], (N_A_LAYERS, DEC_BATCH, PAST_LEN, N_HEADS, HEAD_DIM), 1.0),
        "cache_a_v": nrm(ks[3], (N_A_LAYERS, DEC_BATCH, PAST_LEN, N_HEADS, HEAD_DIM), 1.0),
        "cache_a_logf": jax.nn.log_sigmoid(3.0 + nrm(ks[4], (N_A_LAYERS, DEC_BATCH, PAST_LEN, N_HEADS), 1.0)),
        "cache_b_k": nrm(ks[5], (DEC_BATCH, b_len, N_HEADS, HEAD_DIM), 1.0),
        "cache_b_v": nrm(ks[6], (DEC_BATCH, b_len, N_HEADS, HEAD_DIM), 1.0),
        "g_attn": 1.0 + nrm(ks[7], (DEPTH, D_MODEL), 0.02),
        "w_a_in": nrm(ks[8], (N_A_LAYERS, D_MODEL, 3 * D_MODEL + N_HEADS), d_in),
        "b_a_f": 3.0 + nrm(ks[9], (N_A_LAYERS, N_HEADS), 0.5),
        "w_a_out": nrm(ks[10], (N_A_LAYERS, D_MODEL, D_MODEL), d_in),
        "w_b_q": nrm(ks[11], (N_B_LAYERS, D_MODEL, D_MODEL), d_in),
        "rel_bias": nrm(ks[12], (N_B_LAYERS, N_HEADS, N_REL), 0.5),
        "w_b_out": nrm(ks[13], (N_B_LAYERS, D_MODEL, D_MODEL), d_in),
        "g_kv": 1.0 + nrm(ks[14], (D_MODEL,), 0.02),
        "w_kv": nrm(ks[15], (D_MODEL, 2 * D_MODEL), d_in),
        "g_ffn": 1.0 + nrm(ks[16], (DEPTH, D_MODEL), 0.02),
        "w_gate_up": nrm(ks[17], (DEPTH, D_MODEL, 2 * D_FF), d_in),
        "w_down": nrm(ks[18], (DEPTH, D_FF, D_MODEL), D_FF ** -0.5),
        "g_final": 1.0 + nrm(ks[19], (D_MODEL,), 0.02),
    }

def reference(x_prompt, x_sample, cache_a_k, cache_a_v, cache_a_logf, cache_b_k, cache_b_v,
              g_attn, w_a_in, b_a_f, w_a_out, w_b_q, rel_bias, w_b_out, g_kv, w_kv,
              g_ffn, w_gate_up, w_down, g_final):
    past = cache_a_k.shape[2]

    h = x_prompt
    ak_p, av_p, alf_p = [], [], []
    kb_p = vb_p = None
    for l in range(DEPTH):
        if l < N_A_LAYERS:
            q, k, v, lf = fox_project(rms_norm(h, g_attn[l]), w_a_in[l], b_a_f[l])
            h = h + merge_heads(fox_attention_prompt(q, k, v, lf)) @ w_a_out[l]
            ak_p.append(k); av_p.append(v); alf_p.append(lf)
        else:
            j = l - N_A_LAYERS
            if j == 0:
                kb_p, vb_p = shared_kv(h, g_kv, w_kv)
            q = split_heads(rms_norm(h, g_attn[l]) @ w_b_q[j])
            h = h + merge_heads(band_attention_prompt(q, kb_p, vb_p, rel_bias[j])) @ w_b_out[j]
        h = h + swiglu(rms_norm(h, g_ffn[l]), w_gate_up[l], w_down[l])
    y_prompt = rms_norm(h, g_final)
    keep_p = min(BAND_PAST, kb_p.shape[1])
    new_b_k_p = kb_p[:, kb_p.shape[1] - keep_p:]
    new_b_v_p = vb_p[:, vb_p.shape[1] - keep_p:]

    h = x_sample
    ak_s, av_s, alf_s = [], [], []
    kb_all = vb_all = None
    for l in range(DEPTH):
        if l < N_A_LAYERS:
            q, k, v, lf = fox_project(rms_norm(h, g_attn[l]), w_a_in[l], b_a_f[l])
            k_all = jnp.concatenate([cache_a_k[l].astype(k.dtype), k], axis=1)
            v_all = jnp.concatenate([cache_a_v[l].astype(v.dtype), v], axis=1)
            lf_all = jnp.concatenate([cache_a_logf[l].astype(jnp.float32), lf], axis=1)
            h = h + merge_heads(fox_attention_sample(q, k_all, v_all, lf_all, past)) @ w_a_out[l]
            ak_s.append(k); av_s.append(v); alf_s.append(lf)
        else:
            j = l - N_A_LAYERS
            if j == 0:
                kb_new, vb_new = shared_kv(h, g_kv, w_kv)
                kb_all = jnp.concatenate([cache_b_k.astype(kb_new.dtype), kb_new], axis=1)
                vb_all = jnp.concatenate([cache_b_v.astype(vb_new.dtype), vb_new], axis=1)
            q = split_heads(rms_norm(h, g_attn[l]) @ w_b_q[j])
            h = h + merge_heads(band_attention_sample(q, kb_all, vb_all, rel_bias[j], past)) @ w_b_out[j]
        h = h + swiglu(rms_norm(h, g_ffn[l]), w_gate_up[l], w_down[l])
    y_sample = rms_norm(h, g_final)
    keep_s = cache_b_k.shape[1]
    new_b_k_s = kb_all[:, kb_all.shape[1] - keep_s:]
    new_b_v_s = vb_all[:, vb_all.shape[1] - keep_s:]

    return (y_prompt, y_sample,
            jnp.stack(ak_p, 0), jnp.stack(av_p, 0), jnp.stack(alf_p, 0), new_b_k_p, new_b_v_p,
            jnp.stack(ak_s, 0), jnp.stack(av_s, 0), jnp.stack(alf_s, 0), new_b_k_s, new_b_v_s)


_drawn_inputs = setup_inputs


def setup_inputs(seed=0):
    import zlib

    import numpy as np

    out = dict(_drawn_inputs(seed))
    spreads = {}
    factors = {'g_attn': 2.803, 'g_kv': 2.877, 'g_ffn': 2.837, 'g_final': 2.835}
    for name, (base, spread) in spreads.items():
        noise = np.random.default_rng([zlib.crc32(name.encode()), seed]).standard_normal(out[name].shape)
        drawn = base * np.exp(spread * noise) if base else spread * noise
        out[name] = __import__('jax').numpy.asarray(drawn.astype(out[name].dtype))
    for name, factor in factors.items():
        out[name] = (out[name] * factor).astype(out[name].dtype)
    return out
```

```python
from contextlib import ExitStack

import concourse.bass as bass
from concourse import mybir

F32 = mybir.dt.float32
F32R = mybir.dt.float32r
ALU = mybir.AluOpType
ACT = mybir.ActivationFunctionType

P = 128
D = 1024
KC = D // P
HEADS = 16
HD = 64
PAIRS = HEADS // 2
QT = 8
NT = QT + 1
TOK = NT * P
STREAMS = 8
NEW = 16
CACHED = 128
KT = QT + STREAMS + 1
DFF = 2816
GW = 256
GROUPS = DFF // GW
GC = GW // P
WC = 512
EPS = 1e-6
NEG = -1e30
BIG = 3.0e38
SCALE = HD ** -0.5
BAND_TILES = 4
REL = 128
NREL = 2 * REL + 1
TOEP = (BAND_TILES + 1) * P + P


def f32(ap):
    return ap.bitcast(F32)


class Phase:

    def __init__(self, nc, name):
        self.nc, self.name, self.ctx, self.sems = nc, name, ExitStack(), []

    def sem(self, what):
        self.sems.append(self.nc.alloc_semaphore(f"{self.name}_{what}"))
        return self.sems[-1]

    def sb(self, what, shape, dt=F32):
        return self.ctx.enter_context(self.nc.sbuf_tensor(f"{self.name}_{what}", shape, dt))

    def ps(self, what, shape):
        return self.ctx.enter_context(self.nc.psum_tensor(f"{self.name}_{what}", shape, F32))

    def __enter__(self):
        return self

    def __exit__(self, *e):
        if self.sems and not any(e):
            self.nc.clear_and_free_semaphores(self.sems)
            self.nc.all_engine_barrier()
        return self.ctx.__exit__(*e)


def setup_block(nc, ident, half, ms):
    with Phase(nc, "setup") as ph:
        made = ph.sem("made")
        with nc.Block() as block:
            @block.gpsimd
            def _(pool):
                pool.memset(half[:], -0.5).then_inc(made, 1)
                pool.memset(ident[:], 0.0).then_inc(made, 1)
                pool.memset(ms[:], 0.0).then_inc(made, 1)
                pool.wait_ge(made, 3)
                pool.affine_select(out=ident[:], in_=ident[:], compare_op=ALU.not_equal, fill=1.0,
                                   base=0, pattern=[[-1, P]], channel_multiplier=1).then_inc(made, 1)
                cached = ms[:, 0:STREAMS * CACHED].rearrange("p (b k) -> p b k", b=STREAMS)
                fresh = ms[:, STREAMS * CACHED:].rearrange("p (b k) -> p b k", b=STREAMS)
                n = 4
                for view, width in ((cached, CACHED), (fresh, NEW)):
                    pool.wait_ge(made, n)
                    pool.affine_select(out=view, in_=view, compare_op=ALU.is_ge, fill=NEG, base=0,
                                       pattern=[[-NEW, STREAMS], [0, width]],
                                       channel_multiplier=1).then_inc(made, 1)
                    pool.wait_ge(made, n + 1)
                    pool.affine_select(out=view, in_=view, compare_op=ALU.is_ge, fill=NEG, base=NEW - 1,
                                       pattern=[[NEW, STREAMS], [0, width]],
                                       channel_multiplier=-1).then_inc(made, 1)
                    n += 2


class Norm:

    def __init__(self, ph, h, g_ap, ident, half, xh, xl, ptr, x_in=None):
        self.ph, self.h, self.g_ap, self.ident, self.half = ph, h, g_ap, ident, half
        self.xh, self.xl, self.ptr, self.x_in = xh, xl, ptr, x_in
        self.g = ph.sb("g", [P, D])
        self.sq = ph.sb("sq", [P, D])
        self.ss = ph.sb("ss", [P, NT])
        self.ms = ph.sb("ms", [P, NT])
        self.rs = ph.sb("rs", [P, NT])
        self.xn = ph.sb("xn", [P, 2, D])
        self.g_loaded = ph.sem("g_loaded")
        self.squared, self.mean_ready, self.rs_ready = ph.sem("squared"), ph.sem("mean_ready"), ph.sem("rs_ready")
        self.xn_ready, self.turned = ph.sem("xn_ready"), ph.sem("turned")
        self.high_ready, self.low_ready = ph.sem("high_ready"), ph.sem("low_ready")

    def load(self, sp):
        sp.dma_start(self.g[:], self.g_ap.partition_broadcast(P)).then_inc(self.g_loaded, 16)

    def squares(self, act, t):
        if self.x_in:
            act.wait_ge(self.x_in[t], 16)
        if t:
            act.wait_ge(self.squared, t)
        act.activation(self.sq[:], self.h[:, t, :], ACT.Square,
                       accum_out=self.ss[:, t:t + 1]).then_inc(self.squared, 1)

    def rsqrt(self, pool, t):
        pool.wait_ge(self.squared, t + 1)
        pool.tensor_scalar(self.ms[:, t:t + 1], self.ss[:, t:t + 1], 1.0 / D, EPS,
                           ALU.mult, ALU.add).then_inc(self.mean_ready, 1)
        pool.wait_ge(self.mean_ready, t + 1)
        pool.tensor_tensor(out=self.rs[:, t:t + 1], in0=self.ms[:, t:t + 1], in1=self.half[:],
                           op=ALU.pow).then_inc(self.rs_ready, 1)

    def scaled(self, dve, t):
        if t == 0:
            dve.wait_ge(self.g_loaded, 16)
        dve.wait_ge(self.rs_ready, t + 1)
        if t >= 2:
            dve.wait_ge(self.turned, 2 * (t - 1))
        dve.scalar_tensor_tensor(self.xn[:, t % 2, :], self.h[:, t, :], self.rs[:, t:t + 1], self.g[:],
                                 ALU.mult, ALU.mult).then_inc(self.xn_ready, 1)

    def turn(self, pe, t):
        pe.wait_ge(self.xn_ready, t + 1)
        if t:
            pe.wait_ge(self.low_ready, 2 * t)
        for half in range(2):
            for j in range(4):
                c = 4 * half + j
                last = pe.transpose(self.ptr[:, half, j * P:(j + 1) * P],
                                    self.xn[:, t % 2, c * P:(c + 1) * P], self.ident[:])
            last.then_inc(self.turned, 1)

    def views(self, half, t):
        cols = slice(t * P, (t + 1) * P)
        src = self.ptr[:, half, :].rearrange("p (c n) -> p c n", c=4)
        return self.xh[:, 4 * half:4 * half + 4, cols], self.xl[:, 4 * half:4 * half + 4, cols], src

    def high(self, act, t):
        for half in range(2):
            xh, _, src = self.views(half, t)
            act.wait_ge(self.turned, 2 * t + half + 1)
            act.activation(xh, src, ACT.Copy).then_inc(self.high_ready, 1)

    def low(self, dve, t):
        for half in range(2):
            xh, xl, src = self.views(half, t)
            dve.wait_ge(self.high_ready, 2 * t + half + 1)
            dve.tensor_tensor(xl, src, f32(xh), ALU.subtract).then_inc(self.low_ready, 1)

    def ready(self, pe, t):
        pe.wait_ge(self.low_ready, 2 * t + 2)


class Turned:

    def __init__(self, ph, src, xh, xl):
        self.src, self.xh, self.xl = src, xh, xl
        self.raw = ph.sb("at", [P, 2, KC, P])
        self.loaded = [ph.sem(f"at_loaded{i}") for i in range(2)]
        self.high_ready, self.low_ready = ph.sem("high_ready"), ph.sem("low_ready")

    def load(self, sp):
        pass

    def squares(self, act, t):
        pass

    def rsqrt(self, pool, t):
        pass

    def scaled(self, dve, t):
        pass

    def turn(self, pe, t):
        pass

    def fetch(self, sp, t):
        if t >= 2:
            sp.wait_ge(self.low_ready, t - 1)
        sp.dma_start(self.raw[:, t % 2], self.src[:, t * P:(t + 1) * P].rearrange("(c p) n -> p c n", p=P)
                     ).then_inc(self.loaded[t % 2], 16)

    def high(self, act, t):
        act.wait_ge(self.loaded[t % 2], 16 * (t // 2 + 1))
        act.activation(self.xh[:, :, t * P:(t + 1) * P], self.raw[:, t % 2], ACT.Copy).then_inc(self.high_ready, 1)

    def low(self, dve, t):
        dve.wait_ge(self.high_ready, t + 1)
        dve.tensor_tensor(self.xl[:, :, t * P:(t + 1) * P], self.raw[:, t % 2],
                          f32(self.xh[:, :, t * P:(t + 1) * P]), ALU.subtract).then_inc(self.low_ready, 1)

    def ready(self, pe, t):
        pe.wait_ge(self.low_ready, t + 1)


def product(pe, out, xh, xl, wh, wl, first, last):
    pe.matmul(out, xh, wh, start=first, stop=False)
    pe.matmul(out, xh, wl, start=False, stop=False)
    return pe.matmul(out, xl, wh, start=False, stop=last)


def dense_block(nc, name, h, ident, half, w_of, chunks, g_ap=None, turned_src=None, stores=None,
                x_in=None, load_x=None, gate=None):
    with Phase(nc, name) as ph:
        xh = ph.sb("xh", [P, KC, TOK], F32R)
        xl = ph.sb("xl", [P, KC, TOK], F32R)
        with Phase(nc, name + "w") as pw:
            wraw = pw.sb("raw", [P, KC, WC])
            wh = pw.sb("h", [P, KC, WC], F32R)
            wl = pw.sb("l", [P, KC, WC], F32R)
            acc = pw.ps("acc", [P, 3, WC])
            ptr = pw.ps("ptr", [P, 2, WC])
            if turned_src is not None:
                src = Turned(pw, turned_src, xh, xl)
            else:
                src = Norm(pw, h, g_ap, ident, half, xh, xl, ptr, x_in)
            stage = pw.sb("stage", [P, 3, WC]) if stores else None
            raw_loaded = pw.sem("raw_loaded")
            wh_ready, wl_ready, w_used = pw.sem("wh_ready"), pw.sem("wl_ready"), pw.sem("w_used")
            acc_ready, acc_used = pw.sem("acc_ready"), pw.sem("acc_used")
            stored = [pw.sem(f"stored{i}") for i in range(3)] if stores else None

            def split_high(act, n):
                act.wait_ge(raw_loaded, 16 * (n + 1))
                for c in range(KC):
                    if not (isinstance(n, int) and n == 0):
                        if c < KC - 1:
                            act.wait_ge(w_used, (KC - 1) * (n - 1) + c + 1)
                        else:
                            act.wait_ge(acc_ready, NT * n)
                    act.activation(wh[:, c, :], wraw[:, c, :], ACT.Copy).then_inc(wh_ready, 1)

            def split_low(dve, n):
                for c in range(KC):
                    dve.wait_ge(wh_ready, KC * n + c + 1)
                    dve.tensor_tensor(wl[:, c, :], wraw[:, c, :], f32(wh[:, c, :]),
                                      ALU.subtract).then_inc(wl_ready, 1)

            def multiply(pe, n, t):
                if t >= 3 or not (isinstance(n, int) and n == 0):
                    pe.wait_ge(acc_used, NT * n + t - 2)
                rows = slice(t * P, (t + 1) * P)
                for c in range(KC):
                    if t == 0:
                        pe.wait_ge(wl_ready, KC * n + c + 1)
                    last = product(pe, acc[:, t % 3, :], xh[:, c, rows], xl[:, c, rows],
                                   wh[:, c, :], wl[:, c, :], c == 0, c == KC - 1)
                    if t == NT - 1 and c < KC - 1:
                        last.then_inc(w_used, 1)
                last.then_inc(acc_ready, 1)

            def empty(eng, n, t):
                eng.wait_ge(acc_ready, NT * n + t + 1)
                if stores:
                    if t >= 3 or not (isinstance(n, int) and n == 0):
                        eng.wait_ge(stored[t % 3], 32 * (3 * n + t // 3))
                    eng.activation(stage[:, t % 3, :], acc[:, t % 3, :], ACT.Copy).then_inc(acc_used, 1)
                else:
                    part = h[:, t, n * WC:(n + 1) * WC]
                    eng.tensor_tensor(part, acc[:, t % 3, :], part, ALU.add).then_inc(acc_used, 1)

            def store(sp, n, t, dest):
                sp.wait_ge(acc_used, NT * n + t + 1)
                pairs = dest(t, stage[:, t % 3, :])
                assert len(pairs) == 2
                for dst, s in pairs:
                    sp.dma_start(dst, s).then_inc(stored[t % 3], 16)

            with nc.Block() as block:
                @block.sync
                def _(sp):
                    if load_x:
                        load_x(sp, 0, 2)
                    src.load(sp)
                    sp.dma_start(wraw[:], w_of(0)).then_inc(raw_loaded, 16)
                    if load_x:
                        load_x(sp, 2, NT)
                    if turned_src is not None:
                        for t in range(NT):
                            src.fetch(sp, t)
                    n = 0
                    segments = stores if stores else [(chunks, None)]
                    for count, dest in segments:
                        def one(i, more):
                            if more:
                                sp.wait_ge(wl_ready, KC * (n + i + 1))
                                sp.dma_start(wraw[:], w_of(n + i + 1)).then_inc(raw_loaded, 16)
                            if dest:
                                for t in range(NT):
                                    store(sp, n + i, t, lambda tt, s: dest(tt, s, i))
                        for i in range(count):
                            one(i, n + i + 1 < chunks)
                        n += count
                    if stores:
                        for i in range(3):
                            sp.wait_ge(stored[i], 32 * 3 * chunks)

                @block.gpsimd
                def _(pool):
                    for t in range(NT):
                        src.rsqrt(pool, t)

                @block.scalar
                def _(act):
                    src.squares(act, 0)
                    src.squares(act, 1)
                    split_high(act, 0)
                    for t in range(NT):
                        src.high(act, t)
                        if t + 2 < NT:
                            src.squares(act, t + 2)
                        if stores and t:
                            empty(act, 0, t - 1)
                    def rest(n, more):
                        if stores:
                            for t in range(NT - 1):
                                empty(act, n, t)
                        if more:
                            split_high(act, n + 1)
                        if stores:
                            empty(act, n, NT - 1)
                    split_high(act, 1)
                    if stores:
                        empty(act, 0, NT - 1)
                    if chunks > 2:
                        with act.Fori(1, chunks - 1) as n:
                            rest(n, True)
                    rest(chunks - 1, False)

                @block.vector
                def _(dve):
                    src.scaled(dve, 0)
                    src.scaled(dve, 1)
                    split_low(dve, 0)
                    for t in range(NT):
                        src.low(dve, t)
                        if t + 2 < NT:
                            src.scaled(dve, t + 2)
                        if not stores and t:
                            empty(dve, 0, t - 1)
                    split_low(dve, 1)
                    if not stores:
                        empty(dve, 0, NT - 1)
                    if chunks > 2:
                        with dve.Fori(1, chunks - 1) as n:
                            split_low(dve, n + 1)
                    if not stores:
                        for t in range(NT):
                            empty(dve, chunks - 1, t)

                @block.tensor
                def _(pe):
                    src.turn(pe, 0)
                    for t in range(NT):
                        if t + 1 < NT:
                            src.turn(pe, t + 1)
                        src.ready(pe, t)
                        multiply(pe, 0, t)
                    if chunks > 2:
                        with pe.Fori(1, chunks - 1) as n:
                            for t in range(NT):
                                multiply(pe, n, t)
                    for t in range(NT):
                        multiply(pe, chunks - 1, t)
        if gate:
            gate(xh, xl)


def gate_block(nc, xh, xl, ident, wf_ap, bf_ap, clf_ap, lf_p, lf_s, negcum, cq):
    with Phase(nc, "gate") as ph:
        wraw = ph.sb("wraw", [P, KC, HEADS])
        wh = ph.sb("wh", [P, KC, HEADS], F32R)
        wl = ph.sb("wl", [P, KC, HEADS], F32R)
        bf = ph.sb("bf", [HEADS, 1])
        clf = ph.sb("clf", [P, STREAMS, HEADS])
        tri = ph.sb("tri", [P, P])
        trib = ph.sb("trib", [P, P])
        z = ph.sb("z", [HEADS, TOK])
        u = ph.sb("u", [HEADS, TOK])
        w = ph.sb("w", [HEADS, TOK])
        e = ph.sb("e", [HEADS, TOK])
        lf = ph.sb("lf", [P, NT, HEADS])
        cum = ph.sb("cum", [HEADS, KT * P])
        ncum = ph.sb("ncum", [HEADS, KT * P])
        pf = ph.ps("pf", [P, 3, WC])
        pc = ph.ps("pc", [P, 5, WC])
        loaded, split, made = ph.sem("loaded"), ph.sem("split"), ph.sem("made")
        f_ready, chain, lnd = ph.sem("f_ready"), ph.sem("chain"), ph.sem("lnd")
        turned, lf_ready, summed, cq_turned, cq_ready = (ph.sem(s) for s in
            ("turned", "lf_ready", "summed", "cq_turned", "cq_ready"))
        stored = ph.sem("stored")
        spans = [(0, WC), (WC, WC), (2 * WC, TOK - 2 * WC)]
        with nc.Block() as block:
            @block.sync
            def _(sp):
                with nc.allow_non_contiguous_dma("small"):
                    sp.dma_start(wraw[:], wf_ap.rearrange("(c p) n -> p c n", p=P)).then_inc(loaded, 16)
                    sp.dma_start(bf[:], bf_ap.rearrange("(h o) -> h o", o=1)).then_inc(loaded, 16)
                    sp.dma_start(clf[:], clf_ap.rearrange("b k h -> k b h")).then_inc(loaded, 16)
                    sp.wait_ge(lf_ready, 1)
                    sp.dma_start(lf_p.rearrange("(t p) h -> p t h", p=P), lf[:, 0:QT, :]).then_inc(stored, 16)
                    sp.dma_start(lf_s, lf[:, QT, :]).then_inc(stored, 16)
                    sp.wait_ge(chain, 7 + QT + 3)
                    sp.dma_start(negcum, ncum[:]).then_inc(stored, 16)
                    sp.wait_ge(stored, 48)

            @block.gpsimd
            def _(pool):
                pool.memset(tri[:], 1.0).then_inc(made, 1)
                pool.wait_ge(made, 1)
                pool.affine_select(out=tri[:], in_=tri[:], compare_op=ALU.is_ge, fill=0.0, base=0,
                                   pattern=[[1, P]], channel_multiplier=-1).then_inc(made, 1)
                pool.wait_ge(made, 2)
                pool.affine_select(out=trib[:].rearrange("p (b n) -> p b n", b=STREAMS),
                                   in_=tri[:].rearrange("p (b n) -> p b n", b=STREAMS),
                                   compare_op=ALU.is_ge, fill=0.0, base=0,
                                   pattern=[[-NEW, STREAMS], [0, NEW]], channel_multiplier=1).then_inc(made, 1)

            @block.scalar
            def _(act):
                act.wait_ge(loaded, 48)
                act.activation(wh[:], wraw[:], ACT.Copy).then_inc(split, 1)
                act.wait_ge(chain, 2)
                act.activation(u[:], u[:], ACT.Exp, scale=-1.0).then_inc(lnd, 1)
                act.wait_ge(chain, 3)
                act.activation(w[:], w[:], ACT.Ln).then_inc(lnd, 1)
                act.wait_ge(turned, 1)
                act.activation(lf[:], pf[:, 0, 0:NT * HEADS].rearrange("p (t h) -> p t h", t=NT),
                               ACT.Copy).then_inc(lf_ready, 1)
                act.wait_ge(cq_turned, 1)
                act.activation(cq[:], pf[:, 1, 0:NT * HEADS].rearrange("p (t h) -> p t h", t=NT),
                               ACT.Copy).then_inc(cq_ready, 1)

            @block.vector
            def _(dve):
                steps = [0]

                def link(ins):
                    steps[0] += 1
                    ins.then_inc(chain, 1)
                    dve.wait_ge(chain, steps[0])

                dve.wait_ge(split, 1)
                dve.tensor_tensor(wl[:], wraw[:], f32(wh[:]), ALU.subtract).then_inc(split, 1)
                dve.wait_ge(f_ready, 1)
                link(dve.tensor_scalar(z[:], pf[0:HEADS, :, :].rearrange("p a n -> p (a n)")[:, 0:TOK],
                                       bf[:, 0:1], None, ALU.add))
                link(dve.scalar_tensor_tensor(u[:], z[:], -1.0, z[:], ALU.mult, ALU.max))
                dve.wait_ge(lnd, 1)
                link(dve.tensor_scalar(w[:], u[:], 1.0, None, ALU.add))
                link(dve.tensor_scalar(e[:], u[:], 1.0, None, ALU.add))
                link(dve.scalar_tensor_tensor(e[:], e[:], 1.0, u[:], ALU.subtract, ALU.subtract))
                dve.wait_ge(lnd, 2)
                link(dve.scalar_tensor_tensor(z[:], z[:], 0.0, w[:], ALU.min, ALU.subtract))
                link(dve.tensor_tensor(z[:], z[:], e[:], ALU.add))
                dve.wait_ge(summed, 1)
                for t in range(QT):
                    cols = slice(t * P, (t + 1) * P)
                    src = pc[0:HEADS, t // 4, (t % 4) * P:(t % 4 + 1) * P]
                    if t == 0:
                        link(dve.tensor_copy(cum[:, cols], src))
                    else:
                        link(dve.tensor_scalar(cum[:, cols], src, cum[:, t * P - 1:t * P], None, ALU.add))
                link(dve.tensor_copy(cum[:, QT * P:(KT - 1) * P],
                                     pc[0:HEADS, 2:4, :].rearrange("p a n -> p (a n)")))
                past = cum[:, QT * P:(KT - 1) * P].rearrange("p (b k) -> p b k", b=STREAMS)
                link(dve.tensor_tensor(cum[:, (KT - 1) * P:].rearrange("p (b n) -> p b n", b=STREAMS),
                                       pc[0:HEADS, 4, 0:P].rearrange("p (b n) -> p b n", b=STREAMS),
                                       past[:, :, CACHED - 1:CACHED].to_broadcast([HEADS, STREAMS, NEW]), ALU.add))
                link(dve.tensor_scalar(ncum[:], cum[:], -1.0, None, ALU.mult))

            @block.tensor
            def _(pe):
                pe.wait_ge(split, 2)
                for s, (at, width) in enumerate(spans):
                    for c in range(KC):
                        last = product(pe, pf[0:HEADS, s, 0:width], wh[:, c, :], wl[:, c, :],
                                       xh[:, c, at:at + width], xl[:, c, at:at + width], c == 0, c == KC - 1)
                last.then_inc(f_ready, 1)
                pe.wait_ge(chain, 7)
                for t in range(NT):
                    last = pe.transpose(pf[:, 0, t * HEADS:(t + 1) * HEADS], z[:, t * P:(t + 1) * P],
                                        ident[0:HEADS, 0:HEADS])
                last.then_inc(turned, 1)
                pe.wait_ge(made, 3)
                pe.wait_ge(lf_ready, 1)
                for t in range(QT):
                    pe.matmul(pc[0:HEADS, t // 4, (t % 4) * P:(t % 4 + 1) * P], lf[:, t, :], tri[:],
                              start=True, stop=True)
                for b in range(STREAMS):
                    pe.matmul(pc[0:HEADS, 2 + b // 4, (b % 4) * P:(b % 4 + 1) * P], clf[:, b, :], tri[:],
                              start=True, stop=True)
                pe.matmul(pc[0:HEADS, 4, 0:P], lf[:, QT, :], trib[:], start=True, stop=True).then_inc(summed, 1)
                pe.wait_ge(chain, 7 + QT + 2)
                for t in range(NT):
                    at = t * P if t < QT else (KT - 1) * P
                    last = pe.transpose(pf[:, 1, t * HEADS:(t + 1) * HEADS], cum[:, at:at + P],
                                        ident[0:HEADS, 0:HEADS])
                last.then_inc(cq_turned, 1)


def attention_block(nc, name, ident, ms, q_d, k_parts, v_parts, out_d, cq=None, negcum=None, toep=None):
    fox = negcum is not None
    S = QT

    def width(i):
        return STREAMS + 1 if i == S else (i + 1 if fox else min(i, BAND_TILES) + 1)

    def first_key(i):
        return QT if i == S else i + 1 - width(i)

    order = [(0, S)] + [(0, i) for i in range(QT)] + [(1, 0), (1, S)] + [(1, i) for i in range(1, QT)]
    U = len(order)
    groups = []
    for hh in (0, 1):
        gs = [(hh, (i, i + 1)) for i in range(0, QT, 2)]
        groups += [(hh, (S,))] + gs
    G = len(groups)
    last_unit = [max(order.index((hh, i)) for i in tiles) for hh, tiles in groups]
    assert last_unit == sorted(last_unit) and G % 2 == 0
    group_of = {(hh, i): g for g, (hh, tiles) in enumerate(groups) for i in tiles}

    k_rounds = [(j, min(4, KT - j)) for j in range(0, KT, 4)]
    q_rounds = [(j, min(4, 2 * NT - j)) for j in range(0, 2 * NT, 4)]
    PREP = len(k_rounds) + len(q_rounds)
    rounds_of, r = [], PREP
    for hh, i in order:
        mine = [(j, min(4, width(i) - j)) for j in range(0, width(i), 4)]
        rounds_of.append((r, mine))
        r += len(mine)
    R = r
    assert R % 2 == 0 and U % 6 == 0

    def rounds_through(n):
        return rounds_of[n][0] + len(rounds_of[n][1])

    with Phase(nc, name) as ph:
        kraw = ph.sb("kraw", [P, KT, P])
        vraw = ph.sb("vraw", [P, KT, P])
        qraw = ph.sb("qraw", [P, 2 * NT, P])
        ks = [ph.sb(f"ks{i}", [P, KT * P], F32R) for i in range(2)]
        vs = [ph.sb(f"vs{i}", [P, KT, P], F32R) for i in range(2)]
        qh = ph.sb("qh", [P, 2 * TOK], F32R)
        ql = ph.sb("ql", [P, 2 * TOK], F32R)
        pth = ph.sb("pth", [P, 2, QT * 2 * P], F32R)
        ptl = ph.sb("ptl", [P, 2, QT * 2 * P], F32R)
        wide = (STREAMS + 1) * P
        pr = [ph.sb(f"pr{i}", [P, wide]) for i in range(3)]
        mneg = ph.sb("mneg", [P, 3])
        rowsum = ph.sb("rowsum", [P, 3])
        inv = ph.sb("inv", [P, 3])
        half_out = ph.sb("half_out", [HD, 2 * P])
        att = ph.sb("att", [P, TOK])
        if fox:
            ncb = ph.sb("ncb", [P, 2, KT * P])
            diag = ph.sb("diag", [P, QT, P])
            bias = [ph.sb(f"bias{i}", [P, wide]) for i in range(2)]
            cqh = [ph.sb(f"cqh{i}", [P, NT]) for i in range(2)]
            cq_done, samp_chain = ph.sem("cq_done"), ph.sem("samp_chain")
        else:
            toe = ph.sb("toe", [P, 2, TOEP - P])
            toes = ph.sb("toes", [P, 2, CACHED + NEW])
            bs = [ph.sb(f"bs{i}", [P, wide]) for i in range(2)]
        sp_wide = ph.ps("sp_wide", [P, 3 * WC])
        sp_slim = ph.ps("sp_slim", [P, 2 * WC])
        tp = ph.ps("tp", [P, 2, WC])
        op = ph.ps("op", [P, WC])
        scores = [sp_wide, sp_slim]

        k_loaded, v_loaded, q_loaded, b_loaded = (ph.sem(s) for s in ("k_loaded", "v_loaded", "q_loaded", "b_loaded"))
        t_done, th_done, tl_done = ph.sem("t_done"), ph.sem("th_done"), ph.sem("tl_done")
        vh_done, vl_done = ph.sem("vh_done"), ph.sem("vl_done")
        qk_done, max_done, exp_done, inv_done, norm_done = (ph.sem(s) for s in
            ("qk_done", "max_done", "exp_done", "inv_done", "norm_done"))
        bias_done, pool_chain = ph.sem("bias_done"), ph.sem("pool_chain")
        pv_done, half_done, o_done, att_stored = (ph.sem(s) for s in ("pv_done", "half_done", "o_done", "att_stored"))

        waited = {e: ph.sem(e + "_waited") for e in ("pool", "dve")}

        def settle(eng, which="pool"):
            eng.sem_inc(waited[which], 1)

        with nc.Block() as block:
            @block.sync
            def _(sp):
                with sp.Fori(0, PAIRS) as p:
                    cols = bass.ds(p * P, P)
                    sp.wait_ge(tl_done, p * R)
                    for raw, parts, done in ((kraw, k_parts, k_loaded), (vraw, v_parts, v_loaded)):
                        for at, n, src in parts:
                            sp.dma_start(raw[:, at:at + n, :], src(cols)).then_inc(done, 16)
                    for i in range(2):
                        sp.dma_start(qraw[:, i * NT:(i + 1) * NT, :],
                                     q_d[:, bass.ds(p * 2 * P + i * P, P)].rearrange("(t p) n -> p t n", p=P)
                                     ).then_inc(q_loaded, 16)
                    sp.wait_ge(o_done, p * G)
                    if fox:
                        for i in range(2):
                            sp.dma_start(ncb[:, i, :], negcum[bass.ds(p * 2 + i, 1), :].to_broadcast([P, KT * P])
                                         ).then_inc(b_loaded, 16)
                    else:
                        for buf, src in ((toe, toep[0]), (toes, toep[1])):
                            sp.dma_start(buf[:], src[bass.ds(p * 2, 2)].rearrange("h p n -> p h n")
                                         ).then_inc(b_loaded, 16)
                    sp.wait_ge(o_done, p * G + G)
                    sp.dma_start(out_d[bass.ds(p * P, P), :], att[:]).then_inc(att_stored, 16)
                sp.wait_ge(att_stored, 16 * PAIRS)

            @block.gpsimd
            def _(pool):
                with pool.Fori(0, PAIRS) as p:
                    pool.wait_ge(o_done, p * G)
                    pool.wait_ge(v_loaded, (p + 1) * 16 * len(v_parts))
                    for hh in range(2):
                        settle(pool)
                        pool.tensor_copy(vs[hh][:, :, 0:HD], vraw[:, :, hh * HD:(hh + 1) * HD]).then_inc(vh_done, 1)
                    pool.wait_ge(b_loaded, (p + 1) * 32)

                    def head_bias(hh):
                        settle(pool)
                        if fox:
                            if hh:
                                pool.wait_ge(bias_done, p * U + order.index((0, QT - 1)) + 1)
                                settle(pool)
                            pool.affine_select(
                                out=diag[:], in_=ncb[:, hh, 0:QT * P].rearrange("p (t k) -> p t k", t=QT),
                                compare_op=ALU.is_ge, fill=NEG, base=0, pattern=[[0, QT], [-1, P]],
                                channel_multiplier=1).then_inc(pool_chain, 1)
                        else:
                            for cols, base, mult in ((slice(TOEP - P - HD, TOEP - P), -HD, 1), (slice(0, HD), HD - 1, -1)):
                                pool.affine_select(out=toe[:, hh, cols], in_=toe[:, hh, cols], compare_op=ALU.is_ge,
                                                   fill=NEG, base=base, pattern=[[0, HD]], channel_multiplier=mult)
                            out = bs[hh][:, 0:STREAMS * CACHED].rearrange("p (b k) -> p b k", b=STREAMS)
                            pool.tensor_tensor(out=out, in0=ms[:, 0:STREAMS * CACHED].rearrange("p (b k) -> p b k", b=STREAMS),
                                               in1=toes[:, hh:hh + 1, 0:CACHED].to_broadcast([P, STREAMS, CACHED]),
                                               op=ALU.add)
                            out = bs[hh][:, STREAMS * CACHED:].rearrange("p (b k) -> p b k", b=STREAMS)
                            pool.tensor_tensor(out=out, in0=ms[:, STREAMS * CACHED:wide].rearrange("p (b k) -> p b k", b=STREAMS),
                                               in1=toes[:, hh:hh + 1, CACHED:].to_broadcast([P, STREAMS, NEW]),
                                               op=ALU.add).then_inc(bias_done, 1)

                    def unit_bias(n):
                        hh, i = order[n]
                        if n >= 2:
                            pool.wait_ge(max_done, p * U + n - 1)
                        settle(pool)
                        slot = bias[n % 2]
                        cqs = cqh[hh]
                        if i == S:
                            pool.tensor_tensor(out=slot[:, 0:wide], in0=ncb[:, hh, QT * P:], in1=ms[:, 0:wide],
                                               op=ALU.add).then_inc(samp_chain, 1)
                            pool.wait_ge(samp_chain, 4 * p + 2 * hh + 1)
                            settle(pool)
                            new = slot[:, STREAMS * P:wide]
                            pool.affine_select(out=new, in_=new, compare_op=ALU.is_ge, fill=NEG, base=0,
                                               pattern=[[-1, P]], channel_multiplier=1).then_inc(samp_chain, 1)
                            pool.wait_ge(samp_chain, 4 * p + 2 * hh + 2)
                            settle(pool)
                            pool.tensor_scalar(slot[:, 0:wide], slot[:, 0:wide], cqs[:, i:i + 1], 1.0,
                                               ALU.add, ALU.mult).then_inc(bias_done, 1)
                        else:
                            if i:
                                pool.tensor_scalar(slot[:, 0:i * P], ncb[:, hh, 0:i * P], cqs[:, i:i + 1], 1.0,
                                                   ALU.add, ALU.mult)
                            if i == 0:
                                pool.wait_ge(pool_chain, 2 * p + hh + 1)
                                settle(pool)
                            pool.tensor_scalar(slot[:, i * P:(i + 1) * P], diag[:, i, :], cqs[:, i:i + 1], 1.0,
                                               ALU.add, ALU.mult).then_inc(bias_done, 1)

                    if fox:
                        settle(pool)
                        for hh in range(2):
                            pool.tensor_copy(cqh[hh][:], cq[:, :, bass.ds(p * 2 + hh, 1)].rearrange("p t o -> p (t o)")).then_inc(cq_done, 1)
                        pool.wait_ge(cq_done, 2 * p + 2)
                        head_bias(0)
                        unit_bias(0)
                    else:
                        head_bias(0)
                        head_bias(1)
                    for n in range(U + 1):
                        if fox and n + 1 < U:
                            if order[n + 1] == (1, 0):
                                head_bias(1)
                            unit_bias(n + 1)
                        if n >= 1:
                            w = width(order[n - 1][1]) * P
                            s = (n - 1) % 3
                            pool.wait_ge(inv_done, p * U + n)
                            settle(pool)
                            pool.tensor_scalar(pr[s][:, 0:w], pr[s][:, 0:w], inv[:, s:s + 1], 1.0,
                                               ALU.mult, ALU.mult).then_inc(norm_done, 1)

            def evac(n):
                hh, i = order[n]
                g = group_of[(hh, i)]
                tiles = groups[g][1]
                base, mine = rounds_of[n]
                for k, (j, cnt) in enumerate(mine):
                    out = []
                    for buf in (pth, ptl):
                        if i == S:
                            v = buf[:, g % 2, j * P:(j + cnt) * P].rearrange("p (k q) -> p k q", q=P)
                        else:
                            kb = first_key(i) - first_key(tiles[0]) + j
                            off = (i - tiles[0]) * P
                            v = buf[:, g % 2, :].rearrange("p (k q) -> p k q", q=2 * P)[:, kb:kb + cnt, off:off + P]
                        out.append(v)
                    yield base + k, cnt, g, out[0], out[1]

            @block.scalar
            def _(act):
                with act.Fori(0, PAIRS) as p:
                    act.wait_ge(o_done, p * G)
                    for r, (j, cnt) in enumerate(k_rounds):
                        act.wait_ge(t_done, p * R + r + 1)
                        for hh in range(2):
                            last = act.activation(ks[hh][0:HD, j * P:(j + cnt) * P],
                                                  tp[hh * HD:(hh + 1) * HD, r % 2, 0:cnt * P], ACT.Copy)
                        last.then_inc(th_done, 1)
                    for r, (j, cnt) in enumerate(q_rounds, len(k_rounds)):
                        act.wait_ge(t_done, p * R + r + 1)
                        act.activation(qh[:, j * P:(j + cnt) * P], tp[:, r % 2, 0:cnt * P], ACT.Copy,
                                       scale=SCALE).then_inc(th_done, 1)
                    for n in range(U + 3):
                        if 1 <= n <= U:
                            w = width(order[n - 1][1]) * P
                            s = (n - 1) % 3
                            act.wait_ge(max_done, p * U + n)
                            act.activation(pr[s][:, 0:w], pr[s][:, 0:w], ACT.Exp, bias=mneg[:, s:s + 1],
                                           scale=-1.0, accum_out=rowsum[:, s:s + 1]).then_inc(exp_done, 1)
                        if 2 <= n < U + 2:
                            for r, cnt, g, hi, _lo in evac(n - 2):
                                act.wait_ge(t_done, p * R + r + 1)
                                if g >= 2:
                                    act.wait_ge(pv_done, p * G + g - 1)
                                act.activation(hi, tp[:, r % 2, 0:cnt * P].rearrange("p (k q) -> p k q", q=P),
                                               ACT.Copy).then_inc(th_done, 1)
                        if n - 3 in last_unit:
                            g = last_unit.index(n - 3)
                            w = P * len(groups[g][1])
                            act.wait_ge(pv_done, p * G + g + 1)
                            if g:
                                act.wait_ge(o_done, p * G + g)
                            act.activation(half_out[:, 0:w], op[HD:P, 0:w], ACT.Copy).then_inc(half_done, 1)

            @block.vector
            def _(dve):
                with dve.Fori(0, PAIRS) as p:
                    dve.wait_ge(o_done, p * G)
                    for r, (j, cnt) in enumerate(k_rounds):
                        dve.wait_ge(th_done, p * R + r + 1)
                        for hh in range(2):
                            last = dve.tensor_tensor(ks[hh][HD:P, j * P:(j + cnt) * P],
                                                     tp[hh * HD:(hh + 1) * HD, r % 2, 0:cnt * P],
                                                     f32(ks[hh][0:HD, j * P:(j + cnt) * P]), ALU.subtract)
                        last.then_inc(tl_done, 1)
                    for r, (j, cnt) in enumerate(q_rounds, len(k_rounds)):
                        dve.wait_ge(th_done, p * R + r + 1)
                        dve.scalar_tensor_tensor(ql[:, j * P:(j + cnt) * P], tp[:, r % 2, 0:cnt * P], SCALE,
                                                 f32(qh[:, j * P:(j + cnt) * P]), ALU.mult,
                                                 ALU.subtract).then_inc(tl_done, 1)
                    for n in range(U + 3):
                        if n < U:
                            hh, i = order[n]
                            w = width(i) * P
                            s = n % 3
                            dve.wait_ge(qk_done, p * U + n + 1)
                            if fox:
                                dve.wait_ge(bias_done, p * U + n + 1)
                                b = bias[n % 2][:, 0:w]
                            else:
                                dve.wait_ge(bias_done, p * 2 + hh + 1)
                                b = bs[hh][:, 0:w] if i == S else toe[:, hh, TOEP - P - w:TOEP - P]
                            if n >= 3:
                                dve.wait_ge(t_done, p * R + rounds_through(n - 3))
                            settle(dve, "dve")
                            dve.tensor_tensor_reduce(out=pr[s][:, 0:w], in0=scores[n % 2][:, 0:w], in1=b,
                                                     scale=-1.0, scalar=BIG, op0=ALU.add, op1=ALU.min,
                                                     accum_out=mneg[:, s:s + 1]).then_inc(max_done, 1)
                        if 1 <= n <= U:
                            s = (n - 1) % 3
                            dve.wait_ge(exp_done, p * U + n)
                            dve.reciprocal(inv[:, s:s + 1], rowsum[:, s:s + 1]).then_inc(inv_done, 1)
                        if n == 0:
                            for hh in range(2):
                                dve.wait_ge(vh_done, p * 2 + hh + 1)
                                dve.tensor_tensor(vs[hh][:, :, HD:P], vraw[:, :, hh * HD:(hh + 1) * HD],
                                                  f32(vs[hh][:, :, 0:HD]), ALU.subtract).then_inc(vl_done, 1)
                        if 2 <= n < U + 2:
                            for r, cnt, g, hi, lo in evac(n - 2):
                                dve.wait_ge(th_done, p * R + r + 1)
                                dve.tensor_tensor(lo, tp[:, r % 2, 0:cnt * P].rearrange("p (k q) -> p k q", q=P),
                                                  f32(hi), ALU.subtract).then_inc(tl_done, 1)
                        if n - 3 in last_unit:
                            g = last_unit.index(n - 3)
                            hh, tiles = groups[g]
                            w = P * len(tiles)
                            dve.wait_ge(half_done, p * G + g + 1)
                            if g == 0:
                                dve.wait_ge(att_stored, 16 * p)
                            dve.tensor_tensor(att[hh * HD:(hh + 1) * HD, tiles[0] * P:tiles[0] * P + w],
                                              op[0:HD, 0:w], half_out[:, 0:w], ALU.add).then_inc(o_done, 1)

            @block.tensor
            def _(pe):
                with pe.Fori(0, PAIRS) as p:
                    pe.wait_ge(o_done, p * G)
                    pe.wait_ge(k_loaded, (p + 1) * 16 * len(k_parts))
                    for r, (j, cnt) in enumerate(k_rounds):
                        if r >= 2:
                            pe.wait_ge(tl_done, p * R + r - 1)
                        for k in range(cnt):
                            last = pe.transpose(tp[:, r % 2, k * P:(k + 1) * P], kraw[:, j + k, :], ident[:])
                        last.then_inc(t_done, 1)
                    pe.wait_ge(q_loaded, (p + 1) * 32)
                    for r, (j, cnt) in enumerate(q_rounds, len(k_rounds)):
                        pe.wait_ge(tl_done, p * R + r - 1)
                        for k in range(cnt):
                            last = pe.transpose(tp[:, r % 2, k * P:(k + 1) * P], qraw[:, j + k, :], ident[:])
                        last.then_inc(t_done, 1)
                    pe.wait_ge(tl_done, p * R + PREP)
                    for n in range(U + 3):
                        if n < U:
                            hh, i = order[n]
                            if n >= 2:
                                pe.wait_ge(max_done, p * U + n - 1)
                            q = slice((hh * NT + i) * P, (hh * NT + i + 1) * P)
                            for j in range(0, width(i), 4):
                                cnt = min(4, width(i) - j)
                                keys = slice((first_key(i) + j) * P, (first_key(i) + j + cnt) * P)
                                out = scores[n % 2][:, j * P:(j + cnt) * P]
                                pe.matmul(out, qh[:, q], ks[hh][:, keys], start=True, stop=False)
                                last = pe.matmul(out, ql[:, q], ks[hh][:, keys], start=False, stop=True)
                            last.then_inc(qk_done, 1)
                        if 2 <= n < U + 2:
                            m = n - 2
                            base, mine = rounds_of[m]
                            pe.wait_ge(norm_done, p * U + m + 1)
                            for k, (j, cnt) in enumerate(mine):
                                pe.wait_ge(tl_done, p * R + base + k - 1)
                                for b in range(cnt):
                                    last = pe.transpose(tp[:, (base + k) % 2, b * P:(b + 1) * P],
                                                        pr[m % 3][:, (j + b) * P:(j + b + 1) * P], ident[:])
                                last.then_inc(t_done, 1)
                        if n - 3 in last_unit:
                            g = last_unit.index(n - 3)
                            hh, tiles = groups[g]
                            if g == 0:
                                pe.wait_ge(vl_done, 2 * p + 2)
                            else:
                                pe.wait_ge(o_done, p * G + g)
                            pe.wait_ge(tl_done, p * R + rounds_through(last_unit[g]))
                            k0 = first_key(tiles[0])
                            steps = []
                            for kb in range(k0, first_key(tiles[-1]) + width(tiles[-1])):
                                inside = [x for x in range(len(tiles))
                                          if first_key(tiles[x]) <= kb < first_key(tiles[x]) + width(tiles[x])]
                                steps.append((len(inside) < len(tiles), kb, inside[0] * P, len(inside) * P))
                            steps.sort()
                            step = P * len(tiles)
                            for x, (_, kb, off, w) in enumerate(steps):
                                at = (kb - k0) * step + off
                                for y, buf in enumerate((pth, ptl)):
                                    last = pe.matmul(op[:, off:off + w], vs[hh][:, kb, :], buf[:, g % 2, at:at + w],
                                                     start=x == 0 and y == 0, stop=x == len(steps) - 1 and y == 1)
                            last.then_inc(pv_done, 1)


def slid(rows_ap, start, rows, cols):
    return bass.AP(tensor=rows_ap.tensor, offset=start, ap=[[rows_ap.shape[1], rows_ap.shape[0]], [-1, rows], [1, cols]])


def distances_block(nc, rel_ap, line, toep):
    with Phase(nc, "dist") as ph:
        rb = ph.sb("rb", [HEADS, NREL])
        row = ph.sb("row", [HEADS, TOEP])
        loaded, made, stored = ph.sem("loaded"), ph.sem("made"), ph.sem("stored")
        far = TOEP - NREL
        with nc.Block() as block:
            @block.sync
            def _(sp):
                sp.dma_start(rb[:], rel_ap).then_inc(loaded, 16)
                sp.wait_ge(made, 2)
                sp.dma_start(line, row[:]).then_inc(stored, 16)
                sp.wait_ge(stored, 16)
                sp.dma_start(toep[0], slid(line, P - 1, P, TOEP - P)).then_inc(stored, 16)
                for b in range(STREAMS):
                    sp.dma_start(toep[1][:, b * NEW:(b + 1) * NEW, :],
                                 slid(line, 4 * P - 1, NEW, CACHED + NEW)).then_inc(stored, 16)
                sp.wait_ge(stored, 32 + 16 * STREAMS)

            @block.vector
            def _(dve):
                dve.wait_ge(loaded, 16)
                dve.tensor_copy(row[:, far:], rb[:, ::-1]).then_inc(made, 1)
                dve.tensor_copy(row[:, 0:far], rb[:, NREL - 1:NREL].to_broadcast([HEADS, far])).then_inc(made, 1)


def ffn_block(nc, name, h, ident, half, g_ap, wgu, wdn):
    with Phase(nc, name) as ph:
        xh = ph.sb("xh", [P, KC, TOK], F32R)
        xl = ph.sb("xl", [P, KC, TOK], F32R)
        graw = ph.sb("graw", [P, KC, 2, GW])
        gh = ph.sb("gh", [P, KC, 2 * GW], F32R)
        gl = ph.sb("gl", [P, KC, 2 * GW], F32R)
        draw = ph.sb("draw", [P, GC, D])
        dh = ph.sb("dh", [P, GC, D], F32R)
        dl = ph.sb("dl", [P, GC, D], F32R)
        gu = ph.ps("gu", [P, 2, WC])
        ptr = ph.ps("ptr", [P, 2, WC])
        tps = ph.ps("tps", [P, WC])
        dn = ph.ps("dn", [P, 2, WC])
        gate = ph.sb("gate", [P, GW])
        hid = ph.sb("hid", [P, GW])
        hidh = ph.sb("hidh", [P, GC, P], F32R)
        hidl = ph.sb("hidl", [P, GC, P], F32R)
        src = Norm(ph, h, g_ap, ident, half, xh, xl, ptr)
        g_loaded, d_loaded = ph.sem("gu_loaded"), ph.sem("dn_loaded")
        gh_ready, gl_ready, g_used = ph.sem("gh_ready"), ph.sem("gl_ready"), ph.sem("g_used")
        dh_ready, dl_ready = ph.sem("dh_ready"), ph.sem("dl_ready")
        gu_ready, gate_ready, hid_ready = ph.sem("gu_ready"), ph.sem("gate_ready"), ph.sem("hid_ready")
        hid_turned, hidh_ready, hidl_ready = ph.sem("hid_turned"), ph.sem("hidh_ready"), ph.sem("hidl_ready")
        dn_ready, dn_used = ph.sem("dn_ready"), ph.sem("dn_used")
        wg_v = wgu.rearrange("(c p) (u n) -> p c u n", p=P, u=2)
        wd_v = wdn.rearrange("(c p) n -> p c n", p=P)
        DS = GC * D // WC

        def is_first(g):
            return isinstance(g, int) and g == 0

        def split_gu_high(act, g):
            act.wait_ge(g_loaded, 16 * 2 * (g + 1))
            for c in range(KC):
                if not is_first(g):
                    if c < KC - 1:
                        act.wait_ge(g_used, (KC - 1) * (g - 1) + c + 1)
                    else:
                        act.wait_ge(gu_ready, NT * g)
                act.activation(gh[:, c, :], graw[:, c].rearrange("p u n -> p (u n)"), ACT.Copy).then_inc(gh_ready, 1)

        def split_gu_low(dve, g):
            for c in range(KC):
                dve.wait_ge(gh_ready, KC * g + c + 1)
                dve.tensor_tensor(gl[:, c, :], graw[:, c].rearrange("p u n -> p (u n)"), f32(gh[:, c, :]),
                                  ALU.subtract).then_inc(gl_ready, 1)

        def piece(buf, s):
            return buf[:, s // 2, (s % 2) * WC:(s % 2 + 1) * WC]

        def split_dn_high(act, g):
            act.wait_ge(d_loaded, 16 * (g + 1))
            if not is_first(g):
                act.wait_ge(dn_ready, NT * g)
            for s in range(DS):
                act.activation(piece(dh, s), piece(draw, s), ACT.Copy).then_inc(dh_ready, 1)

        def split_dn_low(dve, g):
            for s in range(DS):
                dve.wait_ge(dh_ready, DS * g + s + 1)
                dve.tensor_tensor(piece(dl, s), piece(draw, s), f32(piece(dh, s)),
                                  ALU.subtract).then_inc(dl_ready, 1)

        def up(pe, g, t):
            k = NT * g + t
            if not (is_first(g) and t < 2):
                pe.wait_ge(hid_ready, k - 1 if t else k)
            rows = slice(t * P, (t + 1) * P)
            for c in range(KC):
                if t == 0:
                    pe.wait_ge(gl_ready, KC * g + c + 1)
                last = product(pe, gu[:, t % 2, :], xh[:, c, rows], xl[:, c, rows], gh[:, c, :], gl[:, c, :],
                               c == 0, c == KC - 1)
                if t == NT - 1 and c < KC - 1:
                    last.then_inc(g_used, 1)
            last.then_inc(gu_ready, 1)

        def turn(pe, g, t):
            k = NT * g + t
            pe.wait_ge(hid_ready, k + 1)
            if not (is_first(g) and t == 0):
                pe.wait_ge(hidl_ready, k)
            for c in range(GC):
                last = pe.transpose(tps[:, c * P:(c + 1) * P], hid[:, c * P:(c + 1) * P], ident[:])
            last.then_inc(hid_turned, 1)

        def down(pe, g, t):
            k = NT * g + t
            pe.wait_ge(hidl_ready, k + 1)
            if t == 0:
                pe.wait_ge(dl_ready, DS * (g + 1))
            if not (is_first(g) and t == 0):
                pe.wait_ge(dn_used, k)
            for half_ in range(2):
                for c in range(GC):
                    w = slice(half_ * WC, (half_ + 1) * WC)
                    last = product(pe, dn[:, half_, :], hidh[:, c, :], hidl[:, c, :], dh[:, c, w], dl[:, c, w],
                                   c == 0, c == GC - 1)
            last.then_inc(dn_ready, 1)

        def silu(act, g, t):
            k = NT * g + t
            act.wait_ge(gu_ready, k + 1)
            if not (is_first(g) and t == 0):
                act.wait_ge(hid_ready, k)
            act.activation(gate[:], gu[:, t % 2, 0:GW], ACT.Silu).then_inc(gate_ready, 1)

        def hidden(dve, g, t):
            k = NT * g + t
            dve.wait_ge(gate_ready, k + 1)
            if not (is_first(g) and t == 0):
                dve.wait_ge(hid_turned, k)
            dve.tensor_tensor(hid[:], gu[:, t % 2, GW:2 * GW], gate[:], ALU.mult).then_inc(hid_ready, 1)

        def hid_high(act, g, t):
            k = NT * g + t
            act.wait_ge(hid_turned, k + 1)
            if not (is_first(g) and t == 0):
                act.wait_ge(dn_ready, k)
            act.activation(hidh[:].rearrange("p c n -> p (c n)"), tps[:, 0:GW], ACT.Copy).then_inc(hidh_ready, 1)

        def hid_low(dve, g, t):
            dve.wait_ge(hidh_ready, NT * g + t + 1)
            dve.tensor_tensor(hidl[:].rearrange("p c n -> p (c n)"), tps[:, 0:GW],
                              f32(hidh[:].rearrange("p c n -> p (c n)")), ALU.subtract).then_inc(hidl_ready, 1)

        def residual(dve, g, t):
            dve.wait_ge(dn_ready, NT * g + t + 1)
            dve.tensor_tensor(h[:, t, :], dn[:].rearrange("p a n -> p (a n)"), h[:, t, :],
                              ALU.add).then_inc(dn_used, 1)

        with nc.Block() as block:
            @block.sync
            def _(sp):
                def load_gu(g):
                    for u in range(2):
                        sp.dma_start(graw[:, :, u, :], wg_v[:, :, u, bass.ds(g * GW, GW)]).then_inc(g_loaded, 16)

                def load_dn(g):
                    sp.dma_start(draw[:], wd_v[:, bass.ds(g * GC, GC), :]).then_inc(d_loaded, 16)

                src.load(sp)
                load_gu(0)
                load_dn(0)
                with sp.Fori(1, GROUPS) as g:
                    sp.wait_ge(gl_ready, KC * g)
                    load_gu(g)
                    sp.wait_ge(dl_ready, DS * g)
                    load_dn(g)

            @block.gpsimd
            def _(pool):
                for t in range(NT):
                    src.rsqrt(pool, t)

            @block.scalar
            def _(act):
                def tile(g, t, more):
                    if t == NT - 1 and more:
                        split_gu_high(act, g + 1)
                    silu(act, g, t)
                    if t == 0:
                        split_dn_high(act, g)
                    hid_high(act, g, t)

                src.squares(act, 0)
                src.squares(act, 1)
                split_gu_high(act, 0)
                src.high(act, 0)
                for t in range(NT):
                    if t + 2 < NT:
                        src.squares(act, t + 2)
                    if t + 1 < NT:
                        src.high(act, t + 1)
                    tile(0, t, True)
                with act.Fori(1, GROUPS - 1) as g:
                    for t in range(NT):
                        tile(g, t, True)
                for t in range(NT):
                    tile(GROUPS - 1, t, False)

            @block.vector
            def _(dve):
                def tile(g, t, more, first):
                    if t == NT - 1 and more:
                        split_gu_low(dve, g + 1)
                    hidden(dve, g, t)
                    if not first:
                        if t:
                            residual(dve, g, t - 1)
                        else:
                            residual(dve, g - 1, NT - 1)
                    if t == 0:
                        split_dn_low(dve, g)
                    hid_low(dve, g, t)

                src.scaled(dve, 0)
                src.scaled(dve, 1)
                split_gu_low(dve, 0)
                src.low(dve, 0)
                for t in range(NT):
                    if t + 2 < NT:
                        src.scaled(dve, t + 2)
                    if t + 1 < NT:
                        src.low(dve, t + 1)
                    tile(0, t, True, t == 0)
                with dve.Fori(1, GROUPS - 1) as g:
                    for t in range(NT):
                        tile(g, t, True, False)
                for t in range(NT):
                    tile(GROUPS - 1, t, False, False)
                residual(dve, GROUPS - 1, NT - 1)

            @block.tensor
            def _(pe):
                src.turn(pe, 0)
                for t in range(NT):
                    if t + 1 < NT:
                        src.turn(pe, t + 1)
                    src.ready(pe, t)
                    up(pe, 0, t)
                    if t:
                        down(pe, 0, t - 1)
                    turn(pe, 0, t)

                def group(g):
                    for t in range(NT):
                        up(pe, g, t)
                        if t:
                            down(pe, g, t - 1)
                        else:
                            down(pe, g - 1, NT - 1)
                        turn(pe, g, t)
                with pe.Fori(1, GROUPS - 1) as g:
                    group(g)
                group(GROUPS - 1)
                down(pe, GROUPS - 1, NT - 1)


def final_block(nc, h, half, g_ap, y_of):
    with Phase(nc, "final") as ph:
        src = Norm(ph, h, g_ap, None, half, None, None, None)
        y = ph.sb("y", [P, 3, D])
        y_ready = ph.sem("y_ready")
        stored = [ph.sem(f"stored{i}") for i in range(3)]
        with nc.Block() as block:
            @block.sync
            def _(sp):
                src.load(sp)
                for t in range(NT):
                    sp.wait_ge(y_ready, t + 1)
                    sp.dma_start(y_of(t), y[:, t % 3, :]).then_inc(stored[t % 3], 16)
                for i in range(3):
                    sp.wait_ge(stored[i], 16 * (NT // 3))

            @block.gpsimd
            def _(pool):
                for t in range(NT):
                    src.rsqrt(pool, t)

            @block.scalar
            def _(act):
                for t in range(NT):
                    src.squares(act, t)

            @block.vector
            def _(dve):
                dve.wait_ge(src.g_loaded, 16)
                for t in range(NT):
                    dve.wait_ge(src.rs_ready, t + 1)
                    if t >= 3:
                        dve.wait_ge(stored[t % 3], 16 * (t // 3))
                    dve.scalar_tensor_tensor(y[:, t % 3, :], h[:, t, :], src.rs[:, t:t + 1], src.g[:],
                                             ALU.mult, ALU.mult).then_inc(y_ready, 1)


def build(nc, a, o):
    (y_p, y_s, ak_p, av_p, lf_p, bk_p, bv_p, ak_s, av_s, lf_s, bk_s, bv_s) = o

    def flat(ap, pattern):
        return ap.rearrange(pattern)

    x_p = a["x_prompt"][0]
    x_s = flat(a["x_sample"], "b t d -> (b t) d")
    y_p, y_s = y_p[0], flat(y_s, "b t d -> (b t) d")
    akp, avp = (flat(x[0, 0], "t h d -> t (h d)") for x in (ak_p, av_p))
    aks, avs = (flat(x[0], "b t h d -> (b t) (h d)") for x in (ak_s, av_s))
    lfp, lfs = lf_p[0, 0], flat(lf_s[0], "b t h -> (b t) h")
    bkp, bvp = (flat(x[0], "t h d -> t (h d)") for x in (bk_p, bv_p))
    bks, bvs = (flat(x, "b t h d -> b t (h d)") for x in (bk_s, bv_s))
    cak, cav = (flat(a[n][0], "b t h d -> b t (h d)") for n in ("cache_a_k", "cache_a_v"))
    cbk, cbv = (flat(a[n], "b t h d -> b t (h d)") for n in ("cache_b_k", "cache_b_v"))

    def scratch(name, shape):
        return nc.dram_tensor(name, shape, F32, kind="Internal").ap()

    q_d = scratch("q_doubled", (TOK, 2 * D))
    kb_d, vb_d = scratch("band_k", (TOK, D)), scratch("band_v", (TOK, D))
    at_d = scratch("attn_turned", (D, TOK))
    negcum = scratch("negcum", (HEADS, KT * P))
    line = scratch("distances", (HEADS, TOEP))
    toep = scratch("band_bias", (HEADS, P, TOEP - P)), scratch("stream_bias", (HEADS, P, CACHED + NEW))

    def weights(w, at=0):
        v = w.rearrange("(c p) n -> p c n", p=P)
        return lambda n: v[:, :, bass.ds(n * WC + at, WC)]

    def q_dest(t, s, i):
        v = q_d[t * P:(t + 1) * P, bass.ds(i * 2 * WC, 2 * WC)].rearrange("p (h u d) -> p h u d", u=2, d=HD)
        s = s.rearrange("p (h d) -> p h d", d=HD)
        return [(v[:, :, 0, :], s), (v[:, :, 1, :], s)]

    def kv_dest(prompt, sample):
        def dest(t, s, i):
            dst = prompt[t * P:(t + 1) * P] if t < QT else sample
            return [(dst[:, bass.ds(i * WC + j * (WC // 2), WC // 2)], s[:, j * (WC // 2):(j + 1) * (WC // 2)])
                    for j in range(2)]
        return dest

    def band_dest(full, kept_p, kept_s):
        def dest(t, s, i):
            cols = bass.ds(i * WC, WC)
            row = full[t * P:(t + 1) * P]
            if t == QT:
                return [(row[:, cols], s), (kept_s[:, CACHED - NEW:, cols], s)]
            if t >= QT // 2:
                return [(row[:, cols], s), (kept_p[(t - QT // 2) * P:(t - QT // 2 + 1) * P, cols], s)]
            return [(row[:, bass.ds(i * WC + j * (WC // 2), WC // 2)], s[:, j * (WC // 2):(j + 1) * (WC // 2)])
                    for j in range(2)]
        return dest

    def parts(prompt, cached, new):
        return [(0, QT, lambda c: prompt[:, c].rearrange("(t p) n -> p t n", p=P)),
                (QT, STREAMS, lambda c: cached[:, :, c].rearrange("b p n -> p b n")),
                (QT + STREAMS, 1, lambda c: new[:, c].rearrange("(o p) n -> p o n", o=1))]

    with Phase(nc, "all") as al:
        h = al.sb("h", [P, NT, D])
        ident = al.sb("ident", [P, P])
        half = al.sb("half", [P, 1])
        ms = al.sb("mask", [P, (STREAMS + 1) * P])
        cq = al.sb("cq", [P, NT, HEADS])
        x_in = [al.sem(f"x_in{t}") for t in range(NT)]
        kept = al.sem("kept")

        def load_x(sp, t0, t1):
            for t in range(t0, t1):
                sp.dma_start(h[:, t, :], x_p[t * P:(t + 1) * P, :] if t < QT else x_s).then_inc(x_in[t], 16)
            if t0:
                for dst, src in ((bks, cbk), (bvs, cbv)):
                    sp.dma_start(dst[:, 0:CACHED - NEW, :], src[:, NEW:, :]).then_inc(kept, 16)

        setup_block(nc, ident, half, ms)
        w_in = a["w_a_in"][0]
        dense_block(nc, "qkv", h, ident, half, weights(w_in), 3 * D // WC, g_ap=a["g_attn"][0],
                    stores=[(2, q_dest), (2, kv_dest(akp, aks)), (2, kv_dest(avp, avs))],
                    x_in=x_in, load_x=load_x,
                    gate=lambda xh, xl: gate_block(nc, xh, xl, ident, w_in[:, 3 * D:], a["b_a_f"][0],
                                                   a["cache_a_logf"][0], lfp, lfs, negcum, cq))
        attention_block(nc, "fox", ident, ms, q_d, parts(akp, cak, aks), parts(avp, cav, avs), at_d,
                        cq=cq, negcum=negcum)
        dense_block(nc, "aout", h, ident, half, weights(a["w_a_out"][0]), 2, turned_src=at_d)
        ffn_block(nc, "ffn0", h, ident, half, a["g_ffn"][0], a["w_gate_up"][0], a["w_down"][0])
        dense_block(nc, "kv", h, ident, half, weights(a["w_kv"]), 4, g_ap=a["g_kv"],
                    stores=[(2, band_dest(kb_d, bkp, bks)), (2, band_dest(vb_d, bvp, bvs))])
        dense_block(nc, "bq", h, ident, half, weights(a["w_b_q"][0]), 2, g_ap=a["g_attn"][1],
                    stores=[(2, q_dest)])
        distances_block(nc, a["rel_bias"][0], line, toep)
        attention_block(nc, "band", ident, ms, q_d, parts(kb_d[0:QT * P], cbk, kb_d[QT * P:]),
                        parts(vb_d[0:QT * P], cbv, vb_d[QT * P:]), at_d, toep=toep)
        dense_block(nc, "bout", h, ident, half, weights(a["w_b_out"][0]), 2, turned_src=at_d)
        ffn_block(nc, "ffn1", h, ident, half, a["g_ffn"][1], a["w_gate_up"][1], a["w_down"][1])
        final_block(nc, h, half, a["g_final"], lambda t: y_p[t * P:(t + 1) * P, :] if t < QT else y_s)
        with nc.Block() as block:
            @block.sync
            def _(sp):
                sp.wait_ge(kept, 32)


OUTPUTS = [(1, 1024, 1024), (8, 16, 1024), (1, 1, 1024, 16, 64), (1, 1, 1024, 16, 64), (1, 1, 1024, 16),
           (1, 512, 16, 64), (1, 512, 16, 64), (1, 8, 16, 16, 64), (1, 8, 16, 16, 64), (1, 8, 16, 16),
           (8, 128, 16, 64), (8, 128, 16, 64)]
INPUTS = ["x_prompt", "x_sample", "cache_a_k", "cache_a_v", "cache_a_logf", "cache_b_k", "cache_b_v", "g_attn",
          "w_a_in", "b_a_f", "w_a_out", "w_b_q", "rel_bias", "w_b_out", "g_kv", "w_kv", "g_ffn", "w_gate_up",
          "w_down", "g_final"]


def kernel(**inputs):
    import numpy as np
    import concourse.bacc as bacc
    from concourse.bass_utils import run_bass_kernel_spmd

    nc = bacc.Bacc("TRN2", target_bir_lowering=False, num_devices=1)
    arrays, aps = {}, {}
    for name in INPUTS:
        x = np.ascontiguousarray(inputs[name])
        arrays[f"in_{name}"] = x
        aps[name] = nc.dram_tensor(f"in_{name}", x.shape, F32, kind="ExternalInput").ap()
    outs = [nc.dram_tensor(f"out_{i}", s, F32, kind="ExternalOutput").ap() for i, s in enumerate(OUTPUTS)]
    build(nc, aps, outs)
    r = run_bass_kernel_spmd(nc, [arrays], core_ids=[0])
    return tuple(r.results[0][f"out_{i}"] for i in range(len(OUTPUTS)))
```

```python
from contextlib import ExitStack

import concourse.bass as bass
from concourse import mybir

F32 = mybir.dt.float32
F32R = mybir.dt.float32r
ALU = mybir.AluOpType
ACT = mybir.ActivationFunctionType

P = 128
D = 1024
KC = D // P
HEADS = 16
HD = 64
PAIRS = HEADS // 2
QT = 8
NT = QT + 1
TOK = NT * P
STREAMS = 8
NEW = 16
CACHED = 128
KT = QT + STREAMS + 1
DFF = 2816
GW = 256
GROUPS = DFF // GW
GC = GW // P
WC = 512
EPS = 1e-6
NEG = -1e30
BIG = 3.0e38
SCALE = HD ** -0.5
BAND_TILES = 4
REL = 128
NREL = 2 * REL + 1
TOEP = (BAND_TILES + 1) * P + P


def f32(ap):
    return ap.bitcast(F32)


def wait(eng, sem, count):
    if isinstance(count, int) and count <= 0:
        return
    eng.wait_ge(sem, count)


class Phase:

    def __init__(self, nc, name):
        self.nc, self.name, self.ctx, self.sems = nc, name, ExitStack(), []

    def sem(self, what):
        self.sems.append(self.nc.alloc_semaphore(f"{self.name}_{what}"))
        return self.sems[-1]

    def sb(self, what, shape, dt=F32):
        return self.ctx.enter_context(self.nc.sbuf_tensor(f"{self.name}_{what}", shape, dt))

    def ps(self, what, shape):
        return self.ctx.enter_context(self.nc.psum_tensor(f"{self.name}_{what}", shape, F32))

    def __enter__(self):
        return self

    def __exit__(self, *e):
        if self.sems and not any(e):
            self.nc.clear_and_free_semaphores(self.sems)
            self.nc.all_engine_barrier()
        return self.ctx.__exit__(*e)


def setup_block(nc, ident, half):
    with Phase(nc, "setup") as ph:
        made = ph.sem("made")
        with nc.Block() as block:
            @block.gpsimd
            def _(pool):
                pool.memset(half[:], -0.5).then_inc(made, 1)
                pool.memset(ident[:], 0.0).then_inc(made, 1)
                pool.wait_ge(made, 2)
                pool.affine_select(out=ident[:], in_=ident[:], compare_op=ALU.not_equal, fill=1.0,
                                   base=0, pattern=[[-1, P]], channel_multiplier=1).then_inc(made, 1)


def stream_mask(pool, ms, made):
    pool.memset(ms[:], 0.0).then_inc(made, 1)
    n = 1
    for view, width in ((ms[:, 0:STREAMS * CACHED].rearrange("p (b k) -> p b k", b=STREAMS), CACHED),
                        (ms[:, STREAMS * CACHED:].rearrange("p (b k) -> p b k", b=STREAMS), NEW)):
        pool.wait_ge(made, n)
        pool.affine_select(out=view, in_=view, compare_op=ALU.is_ge, fill=NEG, base=0,
                           pattern=[[-NEW, STREAMS], [0, width]], channel_multiplier=1).then_inc(made, 1)
        pool.wait_ge(made, n + 1)
        pool.affine_select(out=view, in_=view, compare_op=ALU.is_ge, fill=NEG, base=NEW - 1,
                           pattern=[[NEW, STREAMS], [0, width]], channel_multiplier=-1).then_inc(made, 1)
        n += 2
    pool.wait_ge(made, n)


class Norm:

    def __init__(self, ph, h, g_ap, ident, half, xh, xl, ptr, x_in=None):
        self.ph, self.h, self.g_ap, self.ident, self.half = ph, h, g_ap, ident, half
        self.xh, self.xl, self.ptr, self.x_in = xh, xl, ptr, x_in
        self.g = ph.sb("g", [P, D])
        self.sq = ph.sb("sq", [P, D], mybir.dt.bfloat16)
        self.ss = ph.sb("ss", [P, NT])
        self.ms = ph.sb("ms", [P, NT])
        self.rs = ph.sb("rs", [P, NT])
        self.xn = ph.sb("xn", [P, 2, D])
        self.g_loaded = ph.sem("g_loaded")
        self.squared, self.mean_ready, self.rs_ready = ph.sem("squared"), ph.sem("mean_ready"), ph.sem("rs_ready")
        self.xn_ready, self.turned = ph.sem("xn_ready"), ph.sem("turned")
        self.high_ready, self.low_ready = ph.sem("high_ready"), ph.sem("low_ready")

    def load(self, sp):
        sp.dma_start(self.g[:], self.g_ap.partition_broadcast(P)).then_inc(self.g_loaded, 16)

    def squares(self, act, t):
        if self.x_in:
            act.wait_ge(self.x_in[t], 16)
        if t:
            act.wait_ge(self.squared, t)
        act.activation(self.sq[:], self.h[:, t, :], ACT.Square,
                       accum_out=self.ss[:, t:t + 1]).then_inc(self.squared, 1)

    def rsqrt(self, pool, t):
        pool.wait_ge(self.squared, t + 1)
        pool.tensor_scalar(self.ms[:, t:t + 1], self.ss[:, t:t + 1], 1.0 / D, EPS,
                           ALU.mult, ALU.add).then_inc(self.mean_ready, 1)
        pool.wait_ge(self.mean_ready, t + 1)
        pool.tensor_tensor(out=self.rs[:, t:t + 1], in0=self.ms[:, t:t + 1], in1=self.half[:],
                           op=ALU.pow).then_inc(self.rs_ready, 1)

    def scaled(self, dve, t):
        if t == 0:
            dve.wait_ge(self.g_loaded, 16)
        dve.wait_ge(self.rs_ready, t + 1)
        if t >= 2:
            dve.wait_ge(self.turned, 2 * (t - 1))
        dve.scalar_tensor_tensor(self.xn[:, t % 2, :], self.h[:, t, :], self.rs[:, t:t + 1], self.g[:],
                                 ALU.mult, ALU.mult).then_inc(self.xn_ready, 1)

    def turn(self, pe, t):
        pe.wait_ge(self.xn_ready, t + 1)
        if t:
            pe.wait_ge(self.low_ready, 2 * t)
        for half in range(2):
            for j in range(4):
                c = 4 * half + j
                last = pe.transpose(self.ptr[:, half, j * P:(j + 1) * P],
                                    self.xn[:, t % 2, c * P:(c + 1) * P], self.ident[:])
            last.then_inc(self.turned, 1)

    def views(self, half, t):
        cols = slice(t * P, (t + 1) * P)
        src = self.ptr[:, half, :].rearrange("p (c n) -> p c n", c=4)
        return self.xh[:, 4 * half:4 * half + 4, cols], self.xl[:, 4 * half:4 * half + 4, cols], src

    def high(self, act, t):
        for half in range(2):
            xh, _, src = self.views(half, t)
            act.wait_ge(self.turned, 2 * t + half + 1)
            act.activation(xh, src, ACT.Copy).then_inc(self.high_ready, 1)

    def low(self, dve, t):
        for half in range(2):
            xh, xl, src = self.views(half, t)
            dve.wait_ge(self.high_ready, 2 * t + half + 1)
            dve.tensor_tensor(xl, src, f32(xh), ALU.subtract).then_inc(self.low_ready, 1)

    def ready(self, pe, t):
        pe.wait_ge(self.low_ready, 2 * t + 2)


class Turned:

    def __init__(self, ph, src, xh, xl):
        self.src, self.xh, self.xl = src, xh, xl
        self.raw = ph.sb("at", [P, 2, KC, P])
        self.loaded = [ph.sem(f"at_loaded{i}") for i in range(2)]
        self.high_ready, self.low_ready = ph.sem("high_ready"), ph.sem("low_ready")

    def load(self, sp):
        pass

    def squares(self, act, t):
        pass

    def rsqrt(self, pool, t):
        pass

    def scaled(self, dve, t):
        pass

    def turn(self, pe, t):
        pass

    def fetch(self, sp, t):
        if t >= 2:
            sp.wait_ge(self.low_ready, t - 1)
        sp.dma_start(self.raw[:, t % 2], self.src[:, t * P:(t + 1) * P].rearrange("(c p) n -> p c n", p=P)
                     ).then_inc(self.loaded[t % 2], 16)

    def high(self, act, t):
        act.wait_ge(self.loaded[t % 2], 16 * (t // 2 + 1))
        act.activation(self.xh[:, :, t * P:(t + 1) * P], self.raw[:, t % 2], ACT.Copy).then_inc(self.high_ready, 1)

    def low(self, dve, t):
        dve.wait_ge(self.high_ready, t + 1)
        dve.tensor_tensor(self.xl[:, :, t * P:(t + 1) * P], self.raw[:, t % 2],
                          f32(self.xh[:, :, t * P:(t + 1) * P]), ALU.subtract).then_inc(self.low_ready, 1)

    def ready(self, pe, t):
        pe.wait_ge(self.low_ready, t + 1)


def product(pe, out, xh, xl, wh, wl, first, last):
    pe.matmul(out, xh, wh, start=first, stop=False)
    pe.matmul(out, xh, wl, start=False, stop=False)
    return pe.matmul(out, xl, wh, start=False, stop=last)


class Chunk:

    def __init__(self, n, kind, before):
        self.n, self.kind, self.before = n, kind, before


def dense_block(nc, name, h, ident, half, w_of, kinds, g_ap=None, turned_src=None, stage_stores=None,
                turned_stores=None, cached=None, cached_stores=None, x_in=None, load_x=None, gate=None):
    chunks = len(kinds)
    NS, NTS, NCS = 3, 3, 2

    def dmas_of(kind):
        stage = [0] * NS
        turned = [0] * NTS
        cach = [0] * NCS
        for t in range(NT):
            if kind in ("v", "k"):
                stage[t % NS] += len(stage_stores(kind, 0, t, None))
            if kind in ("q", "k"):
                turned[t % NTS] += len(turned_stores(kind, 0, t, None, None))
            if kind == "k" and t < STREAMS:
                cach[t % NCS] += len(cached_stores(0, t, None, None))
        return {"stage": stage, "turned": turned, "cached": cach, "craw": [STREAMS // 2] * 2 if kind == "k" else [0, 0],
                "turns": [NT if kind in ("q", "k") else 0], "cturns": [STREAMS if kind == "k" else 0]}

    def chunks_of(eng, body):
        before = {k: [0] * len(v) for k, v in dmas_of("add").items()}
        for n, kind in enumerate(kinds):
            per = dmas_of(kind)
            body(Chunk(n, kind, before))
            before = {k: [b + per[k][x] for x, b in enumerate(v)] for k, v in before.items()}

    storing = "add" not in kinds
    turning = "q" in kinds or "k" in kinds
    with Phase(nc, name) as ph:
        xh = ph.sb("xh", [P, KC, TOK], F32R)
        xl = ph.sb("xl", [P, KC, TOK], F32R)
        with Phase(nc, name + "w") as pw:
            wraw = pw.sb("raw", [P, KC, WC])
            wh = pw.sb("h", [P, KC, WC], F32R)
            wl = pw.sb("l", [P, KC, WC], F32R)
            acc = pw.ps("acc", [P, 3, WC])
            ptr = pw.ps("ptr", [P, 2, WC])
            if turned_src is not None:
                src = Turned(pw, turned_src, xh, xl)
            else:
                src = Norm(pw, h, g_ap, ident, half, xh, xl, ptr, x_in)
            raw_loaded = pw.sem("raw_loaded")
            wh_ready, wl_ready, w_used = pw.sem("wh_ready"), pw.sem("wl_ready"), pw.sem("w_used")
            acc_ready, acc_used = pw.sem("acc_ready"), pw.sem("acc_used")
            if storing:
                stage = pw.sb("stage", [P, NS, WC])
                stored = [pw.sem(f"stored{i}") for i in range(NS)]
            if turning:
                kt = pw.ps("kt", [P, WC])
                th = pw.sb("th", [P, NTS, WC])
                tl = pw.sb("tl", [P, NTS, WC])
                t_done, th_done, tl_done = pw.sem("t_done"), pw.sem("th_done"), pw.sem("tl_done")
                t_stored = [pw.sem(f"t_stored{i}") for i in range(NTS)]
            if "k" in kinds:
                ct = pw.ps("ct", [P, WC])
                craw = pw.sb("craw", [P, NCS, WC])
                ch = pw.sb("ch", [P, NCS, WC])
                cl = pw.sb("cl", [P, NCS, WC])
                c_loaded = [pw.sem(f"c_loaded{i}") for i in range(NCS)]
                c_done, ch_done, cl_done = pw.sem("c_done"), pw.sem("ch_done"), pw.sem("cl_done")
                c_stored = [pw.sem(f"c_stored{i}") for i in range(NCS)]

            def split_high(act, n):
                act.wait_ge(raw_loaded, 16 * (n + 1))
                for c in range(KC):
                    if n:
                        if c < KC - 1:
                            act.wait_ge(w_used, (KC - 1) * (n - 1) + c + 1)
                        else:
                            act.wait_ge(acc_ready, NT * n)
                    act.activation(wh[:, c, :], wraw[:, c, :], ACT.Copy).then_inc(wh_ready, 1)

            def split_low(dve, n):
                for c in range(KC):
                    dve.wait_ge(wh_ready, KC * n + c + 1)
                    dve.tensor_tensor(wl[:, c, :], wraw[:, c, :], f32(wh[:, c, :]),
                                      ALU.subtract).then_inc(wl_ready, 1)

            def multiply(pe, n, t):
                if t >= 3 or n:
                    pe.wait_ge(acc_used, NT * n + t - 2)
                rows = slice(t * P, (t + 1) * P)
                for c in range(KC):
                    if t == 0:
                        pe.wait_ge(wl_ready, KC * n + c + 1)
                    last = product(pe, acc[:, t % 3, :], xh[:, c, rows], xl[:, c, rows],
                                   wh[:, c, :], wl[:, c, :], c == 0, c == KC - 1)
                    if t == NT - 1 and c < KC - 1:
                        last.then_inc(w_used, 1)
                last.then_inc(acc_ready, 1)

            def empty(eng, ck, t):
                n = ck.n
                eng.wait_ge(acc_ready, NT * n + t + 1)
                if storing:
                    before = ck.before["stage"][t % NS]
                    here = 0
                    if ck.kind in ("v", "k"):
                        here = sum(len(stage_stores(ck.kind, 0, u, None)) for u in range(t % NS, t, NS))
                    wait(eng, stored[t % NS], 16 * (before + here))
                    if turning:
                        before = ck.before["turns"][0]
                        wait(eng, t_done, before + (t - NS + 1 if ck.kind != "v" else 0))
                    eng.activation(stage[:, t % NS, :], acc[:, t % 3, :], ACT.Copy,
                                   scale=SCALE if ck.kind == "q" else 1.0).then_inc(acc_used, 1)
                else:
                    part = h[:, t, n * WC:(n + 1) * WC]
                    eng.tensor_tensor(part, acc[:, t % 3, :], part, ALU.add).then_inc(acc_used, 1)

            def turn_tile(pe, ck, t):
                before = ck.before["turns"][0]
                pe.wait_ge(acc_used, NT * ck.n + t + 1)
                wait(pe, tl_done, before + t)
                for j in range(4):
                    last = pe.transpose(kt[:, j * P:(j + 1) * P], stage[:, t % NS, j * P:(j + 1) * P], ident[:])
                last.then_inc(t_done, 1)

            def turned_high(act, ck, t):
                before = ck.before["turns"][0]
                wait(act, t_done, before + t + 1)
                wait_turned_slot(act, ck, t)
                act.activation(th[:, t % NTS, :].bitcast(F32R), kt[:], ACT.Copy).then_inc(th_done, 1)

            def wait_turned_slot(eng, ck, t):
                before = ck.before["turned"][t % NTS]
                if t >= 0:
                    here = sum(len(turned_stores(ck.kind, 0, u, None, None)) for u in range(t % NTS, t, NTS))
                else:
                    here = -len(turned_stores(kinds[ck.n - 1], 0, NT - 1, None, None))
                wait(eng, t_stored[t % NTS], 16 * (before + here))

            def turned_low(dve, ck, t):
                before = ck.before["turns"][0]
                wait(dve, th_done, before + t + 1)
                dve.tensor_tensor(tl[:, t % NTS, :].bitcast(F32R), kt[:], th[:, t % NTS, :],
                                  ALU.subtract).then_inc(tl_done, 1)

            def turn_cached(pe, ck, t):
                before = ck.before["cturns"][0]
                craw_before = ck.before["craw"][t % NCS]
                pe.wait_ge(c_loaded[t % NCS], 16 * (craw_before + t // NCS + 1))
                wait(pe, cl_done, before + t)
                for j in range(4):
                    last = pe.transpose(ct[:, j * P:(j + 1) * P], craw[:, t % NCS, j * P:(j + 1) * P], ident[:])
                last.then_inc(c_done, 1)

            def cached_high(act, ck, t):
                before = ck.before["cturns"][0]
                wait(act, c_done, before + t + 1)
                before = ck.before["cached"][t % NCS]
                here = sum(len(cached_stores(0, u, None, None)) for u in range(t % NCS, t, NCS))
                wait(act, c_stored[t % NCS], 16 * (before + here))
                act.activation(ch[:, t % NCS, :].bitcast(F32R), ct[:], ACT.Copy).then_inc(ch_done, 1)

            def cached_low(dve, ck, t):
                before = ck.before["cturns"][0]
                wait(dve, ch_done, before + t + 1)
                dve.tensor_tensor(cl[:, t % NCS, :].bitcast(F32R), ct[:], ch[:, t % NCS, :],
                                  ALU.subtract).then_inc(cl_done, 1)

            def turned_before(ck):
                return ck.n > 0 and kinds[ck.n - 1] in ("q", "k")

            def after_tile(eng, ck, t, turned_part, cached_part):
                if t == 0:
                    if turned_before(ck):
                        turned_part(eng, ck, -1)
                elif ck.kind in ("q", "k"):
                    turned_part(eng, ck, t - 1)
                    if ck.kind == "k":
                        cached_part(eng, ck, t - 1)

            def leftover(eng, turned_part):
                if kinds[-1] in ("q", "k"):
                    before = {k: [sum(dmas_of(x)[k][i] for x in kinds) for i in range(len(v))]
                              for k, v in dmas_of("add").items()}
                    turned_part(eng, Chunk(chunks, "v", before), -1)

            with nc.Block() as block:
                @block.sync
                def _(sp):
                    if load_x:
                        load_x(sp, 0, 2)
                    src.load(sp)
                    sp.dma_start(wraw[:], w_of(0)).then_inc(raw_loaded, 16)
                    if load_x:
                        load_x(sp, 2, NT)
                    if turned_src is not None:
                        for t in range(NT):
                            src.fetch(sp, t)
                    seen = {}

                    def store_turned(kind, i, t, turns):
                        sp.wait_ge(tl_done, turns)
                        for dst, s in turned_stores(kind, i, t, th[:, t % NTS, :], tl[:, t % NTS, :]):
                            sp.dma_start(dst, s).then_inc(t_stored[t % NTS], 16)

                    turns = cturns = 0
                    pending = None
                    for n, kind in enumerate(kinds):
                        i = seen.setdefault(kind, 0)
                        seen[kind] += 1
                        if n + 1 < chunks:
                            sp.wait_ge(wl_ready, KC * (n + 1))
                            sp.dma_start(wraw[:], w_of(n + 1)).then_inc(raw_loaded, 16)
                        if kind == "k":
                            for t in range(NCS):
                                sp.dma_start(craw[:, t, :], cached(i, t)).then_inc(c_loaded[t], 16)
                        for t in range(NT):
                            if kind in ("v", "k"):
                                sp.wait_ge(acc_used, NT * n + t + 1)
                                for dst, s in stage_stores(kind, i, t, stage[:, t % NS, :]):
                                    sp.dma_start(dst, s).then_inc(stored[t % NS], 16)
                            if pending:
                                turns += 1
                                store_turned(*pending, turns)
                                pending = None
                            if kind == "k" and t:
                                u = t - 1
                                cturns += 1
                                sp.wait_ge(cl_done, cturns)
                                for dst, s in cached_stores(i, u, ch[:, u % NCS, :], cl[:, u % NCS, :]):
                                    sp.dma_start(dst, s).then_inc(c_stored[u % NCS], 16)
                                if u + NCS < STREAMS:
                                    sp.dma_start(craw[:, u % NCS, :], cached(i, u + NCS)).then_inc(c_loaded[u % NCS], 16)
                            if kind in ("q", "k"):
                                pending = (kind, i, t)
                    if pending:
                        turns += 1
                        store_turned(*pending, turns)
                    totals = {k: [sum(dmas_of(x)[k][i] for x in kinds) for i in range(len(v))]
                              for k, v in dmas_of("add").items()}
                    if storing:
                        for i in range(NS):
                            if totals["stage"][i]:
                                sp.wait_ge(stored[i], 16 * totals["stage"][i])
                    if turning:
                        for i in range(NTS):
                            sp.wait_ge(t_stored[i], 16 * totals["turned"][i])
                    if "k" in kinds:
                        for i in range(NCS):
                            sp.wait_ge(c_stored[i], 16 * totals["cached"][i])

                @block.gpsimd
                def _(pool):
                    for t in range(NT):
                        src.rsqrt(pool, t)

                @block.scalar
                def _(act):
                    src.squares(act, 0)
                    src.squares(act, 1)
                    split_high(act, 0)

                    def chunk(ck):
                        first = ck.n == 0
                        for t in range(NT):
                            if first:
                                src.high(act, t)
                                if t + 2 < NT:
                                    src.squares(act, t + 2)
                            if t == NT - 1 and ck.n < chunks - 1:
                                split_high(act, ck.n + 1)
                            if storing and not (first and t == 0):
                                empty(act, ck, t - 1 if first else t)
                                if first and t == NT - 1:
                                    after_tile(act, ck, t - 1, turned_high, cached_high)
                                    empty(act, ck, t)
                                after_tile(act, ck, t - 1 if first and t < NT - 1 else t, turned_high, cached_high)

                    chunks_of(act, chunk)
                    leftover(act, turned_high)

                @block.vector
                def _(dve):
                    src.scaled(dve, 0)
                    src.scaled(dve, 1)
                    split_low(dve, 0)

                    def chunk(ck):
                        first = ck.n == 0
                        for t in range(NT):
                            if first:
                                src.low(dve, t)
                                if t + 2 < NT:
                                    src.scaled(dve, t + 2)
                            if t == NT - 1 and ck.n < chunks - 1:
                                split_low(dve, ck.n + 1)
                            if not storing:
                                empty(dve, ck, t)
                            elif first:
                                if t:
                                    after_tile(dve, ck, t - 1, turned_low, cached_low)
                                if t == NT - 1:
                                    after_tile(dve, ck, t, turned_low, cached_low)
                            else:
                                after_tile(dve, ck, t, turned_low, cached_low)

                    chunks_of(dve, chunk)
                    leftover(dve, turned_low)

                @block.tensor
                def _(pe):
                    def chunk(ck):
                        first = ck.n == 0
                        for t in range(NT):
                            if first:
                                if t == 0:
                                    src.turn(pe, 0)
                                if t + 1 < NT:
                                    src.turn(pe, t + 1)
                                src.ready(pe, t)
                            multiply(pe, ck.n, t)
                            if first and storing:
                                if t:
                                    after_tile(pe, ck, t - 1, turn_tile, turn_cached)
                                if t == NT - 1:
                                    after_tile(pe, ck, t, turn_tile, turn_cached)
                            elif storing:
                                after_tile(pe, ck, t, turn_tile, turn_cached)

                    chunks_of(pe, chunk)
                    leftover(pe, turn_tile)
        if gate:
            gate(xh, xl)


def gate_block(nc, xh, xl, ident, wf_ap, bf_ap, clf_ap, lf_p, lf_s, negcum, cq):
    with Phase(nc, "gate") as ph:
        wraw = ph.sb("wraw", [P, KC, HEADS])
        wh = ph.sb("wh", [P, KC, HEADS], F32R)
        wl = ph.sb("wl", [P, KC, HEADS], F32R)
        bf = ph.sb("bf", [HEADS, 1])
        clf = ph.sb("clf", [P, STREAMS, HEADS])
        tri = ph.sb("tri", [P, P])
        trib = ph.sb("trib", [P, P])
        z = ph.sb("z", [HEADS, TOK])
        u = ph.sb("u", [HEADS, TOK])
        w = ph.sb("w", [HEADS, TOK])
        e = ph.sb("e", [HEADS, TOK])
        lf = ph.sb("lf", [P, NT, HEADS])
        cum = ph.sb("cum", [HEADS, KT * P])
        ncum = ph.sb("ncum", [HEADS, KT * P])
        pf = ph.ps("pf", [P, 3, WC])
        pc = ph.ps("pc", [P, 5, WC])
        loaded, split, made = ph.sem("loaded"), ph.sem("split"), ph.sem("made")
        f_ready, chain, lnd = ph.sem("f_ready"), ph.sem("chain"), ph.sem("lnd")
        turned, lf_ready, summed, cq_turned, cq_ready = (ph.sem(s) for s in
            ("turned", "lf_ready", "summed", "cq_turned", "cq_ready"))
        stored = ph.sem("stored")
        spans = [(0, WC), (WC, WC), (2 * WC, TOK - 2 * WC)]
        with nc.Block() as block:
            @block.sync
            def _(sp):
                with nc.allow_non_contiguous_dma("small"):
                    sp.dma_start(wraw[:], wf_ap.rearrange("(c p) n -> p c n", p=P)).then_inc(loaded, 16)
                    sp.dma_start(bf[:], bf_ap.rearrange("(h o) -> h o", o=1)).then_inc(loaded, 16)
                    sp.dma_start(clf[:], clf_ap.rearrange("b k h -> k b h")).then_inc(loaded, 16)
                    sp.wait_ge(lf_ready, 1)
                    sp.dma_start(lf_p.rearrange("(t p) h -> p t h", p=P), lf[:, 0:QT, :]).then_inc(stored, 16)
                    sp.dma_start(lf_s, lf[:, QT, :]).then_inc(stored, 16)
                    sp.wait_ge(chain, 7 + QT + 3)
                    sp.dma_start(negcum, ncum[:]).then_inc(stored, 16)
                    sp.wait_ge(stored, 48)

            @block.gpsimd
            def _(pool):
                pool.memset(tri[:], 1.0).then_inc(made, 1)
                pool.wait_ge(made, 1)
                pool.affine_select(out=tri[:], in_=tri[:], compare_op=ALU.is_ge, fill=0.0, base=0,
                                   pattern=[[1, P]], channel_multiplier=-1).then_inc(made, 1)
                pool.wait_ge(made, 2)
                pool.affine_select(out=trib[:].rearrange("p (b n) -> p b n", b=STREAMS),
                                   in_=tri[:].rearrange("p (b n) -> p b n", b=STREAMS),
                                   compare_op=ALU.is_ge, fill=0.0, base=0,
                                   pattern=[[-NEW, STREAMS], [0, NEW]], channel_multiplier=1).then_inc(made, 1)

            @block.scalar
            def _(act):
                act.wait_ge(loaded, 48)
                act.activation(wh[:], wraw[:], ACT.Copy).then_inc(split, 1)
                act.wait_ge(chain, 2)
                act.activation(u[:], u[:], ACT.Exp, scale=-1.0).then_inc(lnd, 1)
                act.wait_ge(chain, 3)
                act.activation(w[:], w[:], ACT.Ln).then_inc(lnd, 1)
                act.wait_ge(turned, 1)
                act.activation(lf[:], pf[:, 0, 0:NT * HEADS].rearrange("p (t h) -> p t h", t=NT),
                               ACT.Copy).then_inc(lf_ready, 1)
                act.wait_ge(cq_turned, 1)
                act.activation(cq[:], pf[:, 1, 0:NT * HEADS].rearrange("p (t h) -> p t h", t=NT),
                               ACT.Copy).then_inc(cq_ready, 1)

            @block.vector
            def _(dve):
                steps = [0]

                def link(ins):
                    steps[0] += 1
                    ins.then_inc(chain, 1)
                    dve.wait_ge(chain, steps[0])

                dve.wait_ge(split, 1)
                dve.tensor_tensor(wl[:], wraw[:], f32(wh[:]), ALU.subtract).then_inc(split, 1)
                dve.wait_ge(f_ready, 1)
                link(dve.tensor_scalar(z[:], pf[0:HEADS, :, :].rearrange("p a n -> p (a n)")[:, 0:TOK],
                                       bf[:, 0:1], None, ALU.add))
                link(dve.scalar_tensor_tensor(u[:], z[:], -1.0, z[:], ALU.mult, ALU.max))
                dve.wait_ge(lnd, 1)
                link(dve.tensor_scalar(w[:], u[:], 1.0, None, ALU.add))
                link(dve.tensor_scalar(e[:], u[:], 1.0, None, ALU.add))
                link(dve.scalar_tensor_tensor(e[:], e[:], 1.0, u[:], ALU.subtract, ALU.subtract))
                dve.wait_ge(lnd, 2)
                link(dve.scalar_tensor_tensor(z[:], z[:], 0.0, w[:], ALU.min, ALU.subtract))
                link(dve.tensor_tensor(z[:], z[:], e[:], ALU.add))
                dve.wait_ge(summed, 1)
                for t in range(QT):
                    cols = slice(t * P, (t + 1) * P)
                    src = pc[0:HEADS, t // 4, (t % 4) * P:(t % 4 + 1) * P]
                    if t == 0:
                        link(dve.tensor_copy(cum[:, cols], src))
                    else:
                        link(dve.tensor_scalar(cum[:, cols], src, cum[:, t * P - 1:t * P], None, ALU.add))
                link(dve.tensor_copy(cum[:, QT * P:(KT - 1) * P],
                                     pc[0:HEADS, 2:4, :].rearrange("p a n -> p (a n)")))
                past = cum[:, QT * P:(KT - 1) * P].rearrange("p (b k) -> p b k", b=STREAMS)
                link(dve.tensor_tensor(cum[:, (KT - 1) * P:].rearrange("p (b n) -> p b n", b=STREAMS),
                                       pc[0:HEADS, 4, 0:P].rearrange("p (b n) -> p b n", b=STREAMS),
                                       past[:, :, CACHED - 1:CACHED].to_broadcast([HEADS, STREAMS, NEW]), ALU.add))
                link(dve.tensor_scalar(ncum[:], cum[:], -1.0, None, ALU.mult))

            @block.tensor
            def _(pe):
                pe.wait_ge(split, 2)
                for s, (at, width) in enumerate(spans):
                    for c in range(KC):
                        last = product(pe, pf[0:HEADS, s, 0:width], wh[:, c, :], wl[:, c, :],
                                       xh[:, c, at:at + width], xl[:, c, at:at + width], c == 0, c == KC - 1)
                last.then_inc(f_ready, 1)
                pe.wait_ge(chain, 7)
                for t in range(NT):
                    last = pe.transpose(pf[:, 0, t * HEADS:(t + 1) * HEADS], z[:, t * P:(t + 1) * P],
                                        ident[0:HEADS, 0:HEADS])
                last.then_inc(turned, 1)
                pe.wait_ge(made, 3)
                pe.wait_ge(lf_ready, 1)
                for t in range(QT):
                    pe.matmul(pc[0:HEADS, t // 4, (t % 4) * P:(t % 4 + 1) * P], lf[:, t, :], tri[:],
                              start=True, stop=True)
                for b in range(STREAMS):
                    pe.matmul(pc[0:HEADS, 2 + b // 4, (b % 4) * P:(b % 4 + 1) * P], clf[:, b, :], tri[:],
                              start=True, stop=True)
                pe.matmul(pc[0:HEADS, 4, 0:P], lf[:, QT, :], trib[:], start=True, stop=True).then_inc(summed, 1)
                pe.wait_ge(chain, 7 + QT + 2)
                for t in range(NT):
                    at = t * P if t < QT else (KT - 1) * P
                    last = pe.transpose(pf[:, 1, t * HEADS:(t + 1) * HEADS], cum[:, at:at + P],
                                        ident[0:HEADS, 0:HEADS])
                last.then_inc(cq_turned, 1)


def attention_block(nc, name, ident, ks_d, qh_d, ql_d, v_parts, out_d, cq=None, negcum=None, toep=None):
    fox = negcum is not None
    S = QT

    def width(i):
        return STREAMS + 1 if i == S else (i + 1 if fox else min(i, BAND_TILES) + 1)

    def first_key(i):
        return QT if i == S else i + 1 - width(i)

    order = [(0, S)] + [(0, i) for i in range(QT)] + [(1, 0), (1, S)] + [(1, i) for i in range(1, QT)]
    U = len(order)
    groups = []
    for hh in (0, 1):
        groups += [(hh, (S,))] + [(hh, (i, i + 1)) for i in range(0, QT, 2)]
    G = len(groups)
    GH = G // 2
    last_unit = [max(order.index((hh, i)) for i in tiles) for hh, tiles in groups]
    group_of = {(hh, i): g for g, (hh, tiles) in enumerate(groups) for i in tiles}
    last_of_head = [max(n for n, (hh, _) in enumerate(order) if hh == x) for x in (0, 1)]
    first_of_head = [min(n for n, (hh, _) in enumerate(order) if hh == x) for x in (0, 1)]

    rounds_of, r = [], 0
    for hh, i in order:
        mine = [(j, min(4, width(i) - j)) for j in range(0, width(i), 4)]
        rounds_of.append((r, mine))
        r += len(mine)
    R = r
    TB = 3
    SMALL = 6
    VSLICES = [(0, 6), (6, 12), (12, KT)]
    NV = len(VSLICES)
    vslice_at = {step + k: (hh, k) for hh, step in ((0, 2), (1, 7)) for k in range(NV)}
    assert last_unit == sorted(last_unit) and G % 2 == 0 and R % TB == 0 and U % SMALL == 0
    assert all(n % 2 == 0 for n, (_, i) in enumerate(order) if i == S)

    def rounds_through(n):
        return rounds_of[n][0] + len(rounds_of[n][1])

    MAX, EXP, NORM, TURN, FIRST, OTHERS, VALUES, OUT = 1, 2, 3, 4, 4, 5, 6, 7
    wide = (STREAMS + 1) * P
    fives = U % 4
    slot_of = [x for run in [4] * ((U - 5 * fives) // 4) + [5] * fives for x in range(run)]
    assert len(slot_of) == U
    prompt_groups = [g for g, (_, tiles) in enumerate(groups) if tiles != (S,)]
    sample_groups = [g for g, (_, tiles) in enumerate(groups) if tiles == (S,)]
    assert len(prompt_groups) % 2 == 0

    def through_before(g):
        kin, apart = (prompt_groups, 2) if g in prompt_groups else (sample_groups, 1)
        k = kin.index(g) - apart
        return kin[k] + 1 if k >= 0 else kin[k] + 1 - G
    samples = [n for n, (_, i) in enumerate(order) if i == S]
    values_step = [n + VALUES + ((n + VALUES) % U in samples) for n in last_unit]
    out_step = [v + OUT - VALUES for v in values_step]
    assert all(b > a for a, b in zip(values_step, values_step[1:])) and values_step[-1] < values_step[0] + U

    with Phase(nc, name) as ph:
        vraw = ph.sb("vraw", [P, KT, P])
        ks = [ph.sb(f"ks{i}", [P, KT * P], F32R) for i in range(2)]
        vs = [ph.sb(f"vs{i}", [P, KT, P], F32R) for i in range(2)]
        qh = [ph.sb(f"qh{i}", [P, TOK], F32R) for i in range(2)]
        ql = [ph.sb(f"ql{i}", [P, TOK], F32R) for i in range(2)]
        group_wide = 2 * P * (QT if fox else BAND_TILES + 2)
        pth = ph.sb("pth", [P, 2, group_wide], F32R)
        ptl = ph.sb("ptl", [P, 2, group_wide], F32R)
        sth = ph.sb("sth", [P, wide], F32R)
        stl = ph.sb("stl", [P, wide], F32R)
        pr = [ph.sb(f"pr{i}", [P, wide]) for i in range(5 if fives else 4)]
        mneg = ph.sb("mneg", [P, SMALL])
        rowsum = ph.sb("rowsum", [P, SMALL])
        inv = ph.sb("inv", [P, SMALL])
        half_out = ph.sb("half_out", [HD, 2 * P])
        att = ph.sb("att", [P, TOK])
        ms = ph.sb("mask", [P, wide])
        if fox:
            ncb = [ph.sb(f"ncb{i}", [P, KT * P]) for i in range(2)]
            diag = ph.sb("diag", [P, QT, P])
            bias = [ph.sb(f"bias{i}", [P, wide]) for i in range(2)]
            cqh = [ph.sb(f"cqh{i}", [P, NT]) for i in range(2)]
            cq_done, samp_chain = ph.sem("cq_done"), ph.sem("samp_chain")
        else:
            toe = [ph.sb(f"toe{i}", [P, TOEP - P]) for i in range(2)]
            toes = [ph.sb(f"toes{i}", [P, CACHED + NEW]) for i in range(2)]
            bs = [ph.sb(f"bs{i}", [P, wide]) for i in range(2)]
        sp_wide = ph.ps("sp_wide", [P, 3 * WC])
        sp_slim = ph.ps("sp_slim", [P, 2 * WC])
        tp = ph.ps("tp", [P, TB, WC])
        scores = [sp_wide, sp_slim]
        op = sp_wide[:, 3 * WC - 2 * P:3 * WC]

        kq_loaded = [ph.sem(f"kq_loaded{i}") for i in range(2)]
        b_loaded = [ph.sem(f"b_loaded{i}") for i in range(2)]
        v_loaded = ph.sem("v_loaded")
        t_done, th_done, tl_done = ph.sem("t_done"), ph.sem("th_done"), ph.sem("tl_done")
        vh_done, vl_done = ph.sem("vh_done"), ph.sem("vl_done")
        qk_done, max_done, exp_done, inv_done, norm_done = (ph.sem(s) for s in
            ("qk_done", "max_done", "exp_done", "inv_done", "norm_done"))
        bias_done, pool_chain, masked = ph.sem("bias_done"), ph.sem("pool_chain"), ph.sem("masked")
        pv_done, half_done, o_done = (ph.sem(s) for s in ("pv_done", "half_done", "o_done"))
        att_stored = [ph.sem(f"att_stored{i}") for i in range(2)]
        waited = {e: ph.sem(e + "_waited") for e in ("pool", "dve")}

        def settle(eng, which="pool"):
            eng.sem_inc(waited[which], 1)

        def stage_units(p, first, step, lag):
            n = step - lag
            if n >= U:
                return
            if n >= 0:
                yield n, p
            elif not first:
                yield n + U, p - 1

        def pairs_loop(eng, steps):
            steps(0, range(U), True)
            with eng.Fori(1, PAIRS) as p:
                steps(p, range(U), False)
            steps(PAIRS - 1, range(U, out_step[-1] + 1), False)

        def groups_at(p, first, step, steps_of):
            for g, s in enumerate(steps_of):
                if s == step:
                    yield g, p
                elif s == step + U and not first:
                    yield g, p - 1

        def group_slots(g):
            if g in sample_groups:
                return sth[:], stl[:]
            k = prompt_groups.index(g) % 2
            return pth[:, k, :], ptl[:, k, :]

        def splits(n, part):
            hh, i = order[n]
            g = group_of[(hh, i)]
            tiles = groups[g][1]
            base, mine = rounds_of[n]
            for k, (j, cnt) in enumerate(mine):
                if (k == 0) != (part == FIRST):
                    continue
                out = []
                for buf in group_slots(g):
                    if i == S:
                        v = buf[:, j * P:(j + cnt) * P].rearrange("p (k q) -> p k q", q=P)
                    else:
                        kb = first_key(i) - first_key(tiles[0]) + j
                        off = (i - tiles[0]) * P
                        v = buf.rearrange("p (k q) -> p k q", q=2 * P)[:, kb:kb + cnt, off:off + P]
                    out.append(v)
                yield base + k, cnt, g, out[0], out[1]

        with nc.Block() as block:
            @block.sync
            def _(sp):
                def load_head(p, hh):
                    wait(sp, qk_done, (p - 1) * U + last_of_head[hh] + 1)
                    head = bass.ds(p * 2 + hh, 1)
                    for buf, src in ((ks, ks_d), (qh, qh_d), (ql, ql_d)):
                        sp.dma_start(f32(buf[hh][:]), src[head].rearrange("o p n -> (o p) n")
                                     ).then_inc(kq_loaded[hh], 16)
                    if fox:
                        wait(sp, bias_done, (p - 1) * U + last_of_head[hh] + 1)
                        sp.dma_start(ncb[hh][:], negcum[head, :].to_broadcast([P, KT * P])).then_inc(b_loaded[hh], 16)
                    else:
                        wait(sp, max_done, (p - 1) * U + last_of_head[hh] + 1)
                        for buf, src in ((toe, toep[0]), (toes, toep[1])):
                            sp.dma_start(buf[hh][:], src[head].rearrange("o p n -> (o p) n")
                                         ).then_inc(b_loaded[hh], 16)

                def load_values(p):
                    wait(sp, vl_done, 2 * NV * p)
                    for at, n, src in v_parts:
                        sp.dma_start(vraw[:, at:at + n, :], src(bass.ds(p * P, P))).then_inc(v_loaded, 16)

                def store_head(p, hh):
                    sp.wait_ge(o_done, p * G + (hh + 1) * GH)
                    sp.dma_start(out_d[bass.ds(p * P + hh * HD, HD), :], att[hh * HD:(hh + 1) * HD, :]
                                 ).then_inc(att_stored[hh], 16)

                load_head(0, 0)
                load_values(0)
                load_head(0, 1)
                with sp.Fori(0, PAIRS - 1) as p:
                    load_head(p + 1, 0)
                    store_head(p, 0)
                    load_values(p + 1)
                    load_head(p + 1, 1)
                    store_head(p, 1)
                store_head(PAIRS - 1, 0)
                store_head(PAIRS - 1, 1)
                for hh in range(2):
                    sp.wait_ge(att_stored[hh], 16 * PAIRS)

            @block.gpsimd
            def _(pool):
                def values_low(p, step):
                    if step - 1 in vslice_at:
                        hh, k = vslice_at[step - 1]
                        k0, k1 = VSLICES[k]
                        pool.wait_ge(vh_done, (2 * p + hh) * NV + k + 1)
                        settle(pool)
                        pool.tensor_tensor(out=vs[hh][:, k0:k1, HD:P], in0=vraw[:, k0:k1, hh * HD:(hh + 1) * HD],
                                           in1=f32(vs[hh][:, k0:k1, 0:HD]), op=ALU.subtract).then_inc(vl_done, 1)

                def diagonal(p, hh):
                    pool.wait_ge(b_loaded[hh], (p + 1) * 16)
                    wait(pool, bias_done, p * U + (first_of_head[1] if hh else 0))
                    settle(pool)
                    pool.affine_select(out=diag[:], in_=ncb[hh][:, 0:QT * P].rearrange("p (t k) -> p t k", t=QT),
                                       compare_op=ALU.is_ge, fill=NEG, base=0, pattern=[[0, QT], [-1, P]],
                                       channel_multiplier=1).then_inc(pool_chain, 1)
                    pool.tensor_copy(cqh[hh][:], cq[:, :, bass.ds(p * 2 + hh, 1)].rearrange("p t o -> p (t o)")
                                     ).then_inc(cq_done, 1)
                    pool.wait_ge(cq_done, 2 * p + hh + 1)
                    pool.wait_ge(pool_chain, 2 * p + hh + 1)

                def unit_bias(p, n):
                    hh, i = order[n]
                    wait(pool, max_done, p * U + n - 1)
                    settle(pool)
                    slot, cqs = bias[n % 2], cqh[hh]
                    if i == S:
                        pool.tensor_tensor(out=slot[:, 0:wide], in0=ncb[hh][:, QT * P:], in1=ms[:],
                                           op=ALU.add).then_inc(samp_chain, 1)
                        pool.wait_ge(samp_chain, 4 * p + 2 * hh + 1)
                        settle(pool)
                        new = slot[:, STREAMS * P:wide]
                        pool.affine_select(out=new, in_=new, compare_op=ALU.is_ge, fill=NEG, base=0,
                                           pattern=[[-1, P]], channel_multiplier=1).then_inc(samp_chain, 1)
                        pool.wait_ge(samp_chain, 4 * p + 2 * hh + 2)
                        settle(pool)
                        pool.tensor_scalar(slot[:, 0:wide], slot[:, 0:wide], cqs[:, i:i + 1], 1.0,
                                           ALU.add, ALU.mult).then_inc(bias_done, 1)
                    else:
                        if i:
                            pool.tensor_scalar(slot[:, 0:i * P], ncb[hh][:, 0:i * P], cqs[:, i:i + 1], 1.0,
                                               ALU.add, ALU.mult)
                        pool.tensor_scalar(slot[:, i * P:(i + 1) * P], diag[:, i, :], cqs[:, i:i + 1], 1.0,
                                           ALU.add, ALU.mult).then_inc(bias_done, 1)

                def band_bias(p, hh):
                    pool.wait_ge(b_loaded[hh], (p + 1) * 32)
                    wait(pool, max_done, (p - 1) * U + last_of_head[hh] + 1)
                    settle(pool)
                    for cols, base, mult in ((slice(TOEP - P - HD, TOEP - P), -HD, 1), (slice(0, HD), HD - 1, -1)):
                        pool.affine_select(out=toe[hh][:, cols], in_=toe[hh][:, cols], compare_op=ALU.is_ge,
                                           fill=NEG, base=base, pattern=[[0, HD]], channel_multiplier=mult)
                    for at, k0, k1 in ((0, 0, CACHED), (STREAMS * CACHED, CACHED, CACHED + NEW)):
                        view = slice(at, at + STREAMS * (k1 - k0))
                        last = pool.tensor_tensor(
                            out=bs[hh][:, view].rearrange("p (b k) -> p b k", b=STREAMS),
                            in0=ms[:, view].rearrange("p (b k) -> p b k", b=STREAMS),
                            in1=toes[hh][:, k0:k1].rearrange("p (o k) -> p o k", o=1).to_broadcast([P, STREAMS, k1 - k0]),
                            op=ALU.add)
                    last.then_inc(bias_done, 1)

                def normalise(p, n):
                    w, s, m = width(order[n][1]) * P, slot_of[n], n % SMALL
                    pool.wait_ge(inv_done, p * U + n + 1)
                    settle(pool)
                    pool.tensor_scalar(pr[s][:, 0:w], pr[s][:, 0:w], inv[:, m:m + 1], 1.0,
                                       ALU.mult, ALU.mult).then_inc(norm_done, 1)

                stream_mask(pool, ms, masked)

                def fox_pair(p, last=False):
                    for n in range(U):
                        hh = order[n][0]
                        if n in first_of_head:
                            diagonal(p, hh)
                        unit_bias(p, n)
                        values_low(p, n)

                def band_pair(p, last=False):
                    for n in range(U):
                        if n == first_of_head[1] - 4:
                            band_bias(p, 1)
                        if n == U - 4 and not last:
                            band_bias(p + 1, 0)
                        values_low(p, n + NORM)
                        normalise(p, n)

                pair = fox_pair if fox else band_pair
                if not fox:
                    band_bias(0, 0)
                pair(0)
                with pool.Fori(1, PAIRS - 1) as p:
                    pair(p)
                pair(PAIRS - 1, last=True)

            @block.scalar
            def _(act):
                def high(p, first, step, part):
                    for n, pp in stage_units(p, first, step, part):
                        for r, cnt, g, hi, _ in splits(n, part):
                            act.wait_ge(t_done, pp * R + r + 1)
                            wait(act, pv_done, pp * G + through_before(g))
                            act.activation(hi, tp[:, r % TB, 0:cnt * P].rearrange("p (k q) -> p k q", q=P),
                                           ACT.Copy).then_inc(th_done, 1)

                def values_high(p, step):
                    if step in vslice_at:
                        hh, k = vslice_at[step]
                        k0, k1 = VSLICES[k]
                        if (hh, k) == (0, 0):
                            act.wait_ge(v_loaded, (p + 1) * 16 * len(v_parts))
                        if k == 0:
                            wait(act, pv_done, (p - 1) * G + (hh + 1) * GH)
                        act.activation(vs[hh][:, k0:k1, 0:HD], vraw[:, k0:k1, hh * HD:(hh + 1) * HD], ACT.Copy
                                       ).then_inc(vh_done, 1)

                def steps(p, rng, first):
                    for step in rng:
                        high(p, first, step, OTHERS)
                        for n, pp in stage_units(p, first, step, EXP):
                            w, s, m = width(order[n][1]) * P, slot_of[n], n % SMALL
                            act.wait_ge(max_done, pp * U + n + 1)
                            act.activation(pr[s][:, 0:w], pr[s][:, 0:w], ACT.Exp, bias=mneg[:, m:m + 1],
                                           scale=-1.0, accum_out=rowsum[:, m:m + 1]).then_inc(exp_done, 1)
                        for g, pp in groups_at(p, first, step, out_step):
                            w = P * len(groups[g][1])
                            act.wait_ge(pv_done, pp * G + g + 1)
                            wait(act, o_done, pp * G + g)
                            act.activation(half_out[:, 0:w], op[HD:P, 0:w], ACT.Copy).then_inc(half_done, 1)
                        high(p, first, step, FIRST)
                        values_high(p, step)

                pairs_loop(act, steps)

            @block.vector
            def _(dve):
                def low(p, first, step, part):
                    for n, pp in stage_units(p, first, step, part):
                        for r, cnt, g, hi, lo in splits(n, part):
                            dve.wait_ge(th_done, pp * R + r + 1)
                            dve.tensor_tensor(lo, tp[:, r % TB, 0:cnt * P].rearrange("p (k q) -> p k q", q=P),
                                              f32(hi), ALU.subtract).then_inc(tl_done, 1)

                def steps(p, rng, first):
                    for step in rng:
                        for n, pp in stage_units(p, first, step, NORM):
                            w, s, m = width(order[n][1]) * P, slot_of[n], n % SMALL
                            dve.wait_ge(exp_done, pp * U + n + 1)
                            dve.reciprocal(inv[:, m:m + 1], rowsum[:, m:m + 1]).then_inc(inv_done, 1)
                            if fox:
                                dve.wait_ge(inv_done, pp * U + n + 1)
                                dve.tensor_scalar(pr[s][:, 0:w], pr[s][:, 0:w], inv[:, m:m + 1], None,
                                                  ALU.mult).then_inc(norm_done, 1)
                        low(p, first, step, OTHERS)
                        for n, pp in stage_units(p, first, step, MAX):
                            hh, i = order[n]
                            w, s, m = width(i) * P, slot_of[n], n % SMALL
                            dve.wait_ge(qk_done, pp * U + n + 1)
                            if fox:
                                dve.wait_ge(bias_done, pp * U + n + 1)
                                b = bias[n % 2][:, 0:w]
                            else:
                                dve.wait_ge(bias_done, pp * 2 + hh + 1)
                                b = bs[hh][:, 0:w] if i == S else toe[hh][:, TOEP - P - w:TOEP - P]
                            wait(dve, t_done, pp * R + (rounds_through(n - 4) if n >= 4 else rounds_through(n - 4 + U) - R))
                            if not isinstance(pp, int):
                                settle(dve, "dve")
                            dve.tensor_tensor_reduce(out=pr[s][:, 0:w], in0=scores[n % 2][:, 0:w], in1=b,
                                                     scale=-1.0, scalar=BIG, op0=ALU.add, op1=ALU.min,
                                                     accum_out=mneg[:, m:m + 1]).then_inc(max_done, 1)
                        for g, pp in groups_at(p, first, step, out_step):
                            hh, tiles = groups[g]
                            w = P * len(tiles)
                            dve.wait_ge(half_done, pp * G + g + 1)
                            if g % GH == 0:
                                wait(dve, att_stored[hh], 16 * pp)
                            dve.tensor_tensor(att[hh * HD:(hh + 1) * HD, tiles[0] * P:tiles[0] * P + w],
                                              op[0:HD, 0:w], half_out[:, 0:w], ALU.add).then_inc(o_done, 1)
                        low(p, first, step, FIRST)

                pairs_loop(dve, steps)

            @block.tensor
            def _(pe):
                def score(p, n):
                    hh, i = order[n]
                    if n in first_of_head:
                        pe.wait_ge(kq_loaded[hh], (p + 1) * 48)
                    wait(pe, max_done, p * U + n - 1)
                    if i == S:
                        wait(pe, o_done, p * G + sum(v < n for v in values_step)
                             - sum(v >= U + n for v in values_step))
                    q = slice(i * P, (i + 1) * P)
                    for j in range(0, width(i), 4):
                        cnt = min(4, width(i) - j)
                        keys = slice((first_key(i) + j) * P, (first_key(i) + j + cnt) * P)
                        out = scores[n % 2][:, j * P:(j + cnt) * P]
                        pe.matmul(out, qh[hh][:, q], ks[hh][:, keys], start=True, stop=False)
                        last = pe.matmul(out, ql[hh][:, q], ks[hh][:, keys], start=False, stop=True)
                    last.then_inc(qk_done, 1)

                def values(p, g, scored):
                    hh, tiles = groups[g]
                    if g % GH == 0:
                        pe.wait_ge(vl_done, (2 * p + hh + 1) * NV)
                    wait(pe, o_done, p * G + g)
                    if scored is not None:
                        pe.wait_ge(max_done, scored)
                    pe.wait_ge(tl_done, p * R + rounds_through(last_unit[g]))
                    k0 = first_key(tiles[0])
                    todo = []
                    for kb in range(k0, first_key(tiles[-1]) + width(tiles[-1])):
                        inside = [x for x in range(len(tiles))
                                  if first_key(tiles[x]) <= kb < first_key(tiles[x]) + width(tiles[x])]
                        todo.append((len(inside) < len(tiles), kb, inside[0] * P, len(inside) * P))
                    todo.sort()
                    step = P * len(tiles)
                    for x, (_, kb, off, w) in enumerate(todo):
                        at = (kb - k0) * step + off
                        for y, buf in enumerate(group_slots(g)):
                            last = pe.matmul(op[:, off:off + w], vs[hh][:, kb, :], buf[:, at:at + w],
                                             start=x == 0 and y == 0, stop=x == len(todo) - 1 and y == 1)
                    last.then_inc(pv_done, 1)

                def turn(p, first, step):
                    for n, pp in stage_units(p, first, step, TURN):
                        base, mine = rounds_of[n]
                        pe.wait_ge(norm_done, pp * U + n + 1)
                        for k, (j, cnt) in enumerate(mine):
                            wait(pe, tl_done, pp * R + base + k - TB + 1)
                            for b in range(cnt):
                                last = pe.transpose(tp[:, (base + k) % TB, b * P:(b + 1) * P],
                                                    pr[slot_of[n]][:, (j + b) * P:(j + b + 1) * P], ident[:])
                            last.then_inc(t_done, 1)

                def steps(p, rng, first):
                    scored = None
                    for step in rng:
                        turn(p, first, step)
                        for n, pp in stage_units(p, first, step, 0):
                            score(pp, n)
                            if n in samples:
                                scored = pp * U + n + 1
                        for g, pp in groups_at(p, first, step, values_step):
                            values(pp, g, scored)
                            scored = None
                    assert scored is None

                pairs_loop(pe, steps)


def slid(rows_ap, start, rows, cols):
    return bass.AP(tensor=rows_ap.tensor, offset=start, ap=[[rows_ap.shape[1], rows_ap.shape[0]], [-1, rows], [1, cols]])


def distances_block(nc, rel_ap, line, toep):
    with Phase(nc, "dist") as ph:
        rb = ph.sb("rb", [HEADS, NREL])
        row = ph.sb("row", [HEADS, TOEP])
        loaded, made, stored = ph.sem("loaded"), ph.sem("made"), ph.sem("stored")
        far = TOEP - NREL
        with nc.Block() as block:
            @block.sync
            def _(sp):
                sp.dma_start(rb[:], rel_ap).then_inc(loaded, 16)
                sp.wait_ge(made, 2)
                sp.dma_start(line, row[:]).then_inc(stored, 16)
                sp.wait_ge(stored, 16)
                sp.dma_start(toep[0], slid(line, P - 1, P, TOEP - P)).then_inc(stored, 16)
                for b in range(STREAMS):
                    sp.dma_start(toep[1][:, b * NEW:(b + 1) * NEW, :],
                                 slid(line, 4 * P - 1, NEW, CACHED + NEW)).then_inc(stored, 16)
                sp.wait_ge(stored, 32 + 16 * STREAMS)

            @block.vector
            def _(dve):
                dve.wait_ge(loaded, 16)
                dve.tensor_copy(row[:, far:], rb[:, ::-1]).then_inc(made, 1)
                dve.tensor_copy(row[:, 0:far], rb[:, NREL - 1:NREL].to_broadcast([HEADS, far])).then_inc(made, 1)


def ffn_block(nc, name, h, ident, half, g_ap, wgu, wdn):
    with Phase(nc, name) as ph:
        xh = ph.sb("xh", [P, KC, TOK], F32R)
        xl = ph.sb("xl", [P, KC, TOK], F32R)
        graw = ph.sb("graw", [P, KC, 2, GW])
        gh = ph.sb("gh", [P, KC, 2 * GW], F32R)
        gl = ph.sb("gl", [P, KC, 2 * GW], F32R)
        draw = ph.sb("draw", [P, GC, D])
        dh = ph.sb("dh", [P, GC, D], F32R)
        dl = ph.sb("dl", [P, GC, D], F32R)
        gu = ph.ps("gu", [P, 2, WC])
        ptr = ph.ps("ptr", [P, 2, WC])
        tps = ph.ps("tps", [P, WC])
        dn = ph.ps("dn", [P, 2, WC])
        gate = ph.sb("gate", [P, GW])
        hid = ph.sb("hid", [P, GW])
        hidh = ph.sb("hidh", [P, GC, P], F32R)
        hidl = ph.sb("hidl", [P, GC, P], F32R)
        src = Norm(ph, h, g_ap, ident, half, xh, xl, ptr)
        g_loaded, d_loaded = ph.sem("gu_loaded"), ph.sem("dn_loaded")
        gh_ready, gl_ready, g_used = ph.sem("gh_ready"), ph.sem("gl_ready"), ph.sem("g_used")
        dh_ready, dl_ready = ph.sem("dh_ready"), ph.sem("dl_ready")
        gu_ready, gate_ready, hid_ready = ph.sem("gu_ready"), ph.sem("gate_ready"), ph.sem("hid_ready")
        hid_turned, hidh_ready, hidl_ready = ph.sem("hid_turned"), ph.sem("hidh_ready"), ph.sem("hidl_ready")
        dn_ready, dn_used = ph.sem("dn_ready"), ph.sem("dn_used")
        wg_v = wgu.rearrange("(c p) (u n) -> p c u n", p=P, u=2)
        wd_v = wdn.rearrange("(c p) n -> p c n", p=P)
        DS = GC * D // WC

        def is_first(g):
            return isinstance(g, int) and g == 0

        def split_gu_high(act, g):
            act.wait_ge(g_loaded, 16 * 2 * (g + 1))
            for c in range(KC):
                if not is_first(g):
                    if c < KC - 1:
                        act.wait_ge(g_used, (KC - 1) * (g - 1) + c + 1)
                    else:
                        act.wait_ge(gu_ready, NT * g)
                act.activation(gh[:, c, :], graw[:, c].rearrange("p u n -> p (u n)"), ACT.Copy).then_inc(gh_ready, 1)

        def split_gu_low(dve, g):
            for c in range(KC):
                dve.wait_ge(gh_ready, KC * g + c + 1)
                dve.tensor_tensor(gl[:, c, :], graw[:, c].rearrange("p u n -> p (u n)"), f32(gh[:, c, :]),
                                  ALU.subtract).then_inc(gl_ready, 1)

        def piece(buf, s):
            return buf[:, s // 2, (s % 2) * WC:(s % 2 + 1) * WC]

        def split_dn_high(act, g):
            act.wait_ge(d_loaded, 16 * (g + 1))
            if not is_first(g):
                act.wait_ge(dn_ready, NT * g)
            for s in range(DS):
                act.activation(piece(dh, s), piece(draw, s), ACT.Copy).then_inc(dh_ready, 1)

        def split_dn_low(dve, g):
            for s in range(DS):
                dve.wait_ge(dh_ready, DS * g + s + 1)
                dve.tensor_tensor(piece(dl, s), piece(draw, s), f32(piece(dh, s)),
                                  ALU.subtract).then_inc(dl_ready, 1)

        def up(pe, g, t):
            k = NT * g + t
            if not (is_first(g) and t < 2):
                pe.wait_ge(hid_ready, k - 1 if t else k)
            rows = slice(t * P, (t + 1) * P)
            for c in range(KC):
                if t == 0:
                    pe.wait_ge(gl_ready, KC * g + c + 1)
                last = product(pe, gu[:, t % 2, :], xh[:, c, rows], xl[:, c, rows], gh[:, c, :], gl[:, c, :],
                               c == 0, c == KC - 1)
                if t == NT - 1 and c < KC - 1:
                    last.then_inc(g_used, 1)
            last.then_inc(gu_ready, 1)

        def turn(pe, g, t):
            k = NT * g + t
            pe.wait_ge(hid_ready, k + 1)
            if not (is_first(g) and t == 0):
                pe.wait_ge(hidl_ready, k)
            for c in range(GC):
                last = pe.transpose(tps[:, c * P:(c + 1) * P], hid[:, c * P:(c + 1) * P], ident[:])
            last.then_inc(hid_turned, 1)

        def down(pe, g, t):
            k = NT * g + t
            pe.wait_ge(hidl_ready, k + 1)
            if t == 0:
                pe.wait_ge(dl_ready, DS * (g + 1))
            if not (is_first(g) and t == 0):
                pe.wait_ge(dn_used, k)
            for half_ in range(2):
                for c in range(GC):
                    w = slice(half_ * WC, (half_ + 1) * WC)
                    last = product(pe, dn[:, half_, :], hidh[:, c, :], hidl[:, c, :], dh[:, c, w], dl[:, c, w],
                                   c == 0, c == GC - 1)
            last.then_inc(dn_ready, 1)

        def silu(act, g, t):
            k = NT * g + t
            act.wait_ge(gu_ready, k + 1)
            if not (is_first(g) and t == 0):
                act.wait_ge(hid_ready, k)
            act.activation(gate[:], gu[:, t % 2, 0:GW], ACT.Silu).then_inc(gate_ready, 1)

        def hidden(dve, g, t):
            k = NT * g + t
            dve.wait_ge(gate_ready, k + 1)
            if not (is_first(g) and t == 0):
                dve.wait_ge(hid_turned, k)
            dve.tensor_tensor(hid[:], gu[:, t % 2, GW:2 * GW], gate[:], ALU.mult).then_inc(hid_ready, 1)

        def hid_high(act, g, t):
            k = NT * g + t
            act.wait_ge(hid_turned, k + 1)
            if not (is_first(g) and t == 0):
                act.wait_ge(dn_ready, k)
            act.activation(hidh[:].rearrange("p c n -> p (c n)"), tps[:, 0:GW], ACT.Copy).then_inc(hidh_ready, 1)

        def hid_low(dve, g, t):
            dve.wait_ge(hidh_ready, NT * g + t + 1)
            dve.tensor_tensor(hidl[:].rearrange("p c n -> p (c n)"), tps[:, 0:GW],
                              f32(hidh[:].rearrange("p c n -> p (c n)")), ALU.subtract).then_inc(hidl_ready, 1)

        def residual(dve, g, t):
            dve.wait_ge(dn_ready, NT * g + t + 1)
            dve.tensor_tensor(h[:, t, :], dn[:].rearrange("p a n -> p (a n)"), h[:, t, :],
                              ALU.add).then_inc(dn_used, 1)

        with nc.Block() as block:
            @block.sync
            def _(sp):
                def load_gu(g):
                    for u in range(2):
                        sp.dma_start(graw[:, :, u, :], wg_v[:, :, u, bass.ds(g * GW, GW)]).then_inc(g_loaded, 16)

                def load_dn(g):
                    sp.dma_start(draw[:], wd_v[:, bass.ds(g * GC, GC), :]).then_inc(d_loaded, 16)

                src.load(sp)
                load_gu(0)
                load_dn(0)
                with sp.Fori(1, GROUPS) as g:
                    sp.wait_ge(gl_ready, KC * g)
                    load_gu(g)
                    sp.wait_ge(dl_ready, DS * g)
                    load_dn(g)

            @block.gpsimd
            def _(pool):
                for t in range(NT):
                    src.rsqrt(pool, t)

            @block.scalar
            def _(act):
                def tile(g, t, more):
                    if t == NT - 1 and more:
                        split_gu_high(act, g + 1)
                    silu(act, g, t)
                    if t == 0:
                        split_dn_high(act, g)
                    hid_high(act, g, t)

                src.squares(act, 0)
                src.squares(act, 1)
                split_gu_high(act, 0)
                src.high(act, 0)
                for t in range(NT):
                    if t + 2 < NT:
                        src.squares(act, t + 2)
                    if t + 1 < NT:
                        src.high(act, t + 1)
                    tile(0, t, True)
                with act.Fori(1, GROUPS - 1) as g:
                    for t in range(NT):
                        tile(g, t, True)
                for t in range(NT):
                    tile(GROUPS - 1, t, False)

            @block.vector
            def _(dve):
                def tile(g, t, more, first):
                    if t == NT - 1 and more:
                        split_gu_low(dve, g + 1)
                    hidden(dve, g, t)
                    if not first:
                        if t:
                            residual(dve, g, t - 1)
                        else:
                            residual(dve, g - 1, NT - 1)
                    if t == 0:
                        split_dn_low(dve, g)
                    hid_low(dve, g, t)

                src.scaled(dve, 0)
                src.scaled(dve, 1)
                split_gu_low(dve, 0)
                src.low(dve, 0)
                for t in range(NT):
                    if t + 2 < NT:
                        src.scaled(dve, t + 2)
                    if t + 1 < NT:
                        src.low(dve, t + 1)
                    tile(0, t, True, t == 0)
                with dve.Fori(1, GROUPS - 1) as g:
                    for t in range(NT):
                        tile(g, t, True, False)
                for t in range(NT):
                    tile(GROUPS - 1, t, False, False)
                residual(dve, GROUPS - 1, NT - 1)

            @block.tensor
            def _(pe):
                src.turn(pe, 0)
                for t in range(NT):
                    if t + 1 < NT:
                        src.turn(pe, t + 1)
                    src.ready(pe, t)
                    up(pe, 0, t)
                    if t:
                        down(pe, 0, t - 1)
                    turn(pe, 0, t)

                def group(g):
                    for t in range(NT):
                        up(pe, g, t)
                        if t:
                            down(pe, g, t - 1)
                        else:
                            down(pe, g - 1, NT - 1)
                        turn(pe, g, t)
                with pe.Fori(1, GROUPS - 1) as g:
                    group(g)
                group(GROUPS - 1)
                down(pe, GROUPS - 1, NT - 1)


def final_block(nc, h, half, g_ap, y_of):
    with Phase(nc, "final") as ph:
        src = Norm(ph, h, g_ap, None, half, None, None, None)
        y = ph.sb("y", [P, 3, D])
        y_ready = ph.sem("y_ready")
        stored = [ph.sem(f"stored{i}") for i in range(3)]
        with nc.Block() as block:
            @block.sync
            def _(sp):
                src.load(sp)
                for t in range(NT):
                    sp.wait_ge(y_ready, t + 1)
                    sp.dma_start(y_of(t), y[:, t % 3, :]).then_inc(stored[t % 3], 16)
                for i in range(3):
                    sp.wait_ge(stored[i], 16 * (NT // 3))

            @block.gpsimd
            def _(pool):
                for t in range(NT):
                    src.rsqrt(pool, t)

            @block.scalar
            def _(act):
                for t in range(NT):
                    src.squares(act, t)

            @block.vector
            def _(dve):
                dve.wait_ge(src.g_loaded, 16)
                for t in range(NT):
                    dve.wait_ge(src.rs_ready, t + 1)
                    if t >= 3:
                        dve.wait_ge(stored[t % 3], 16 * (t // 3))
                    dve.scalar_tensor_tensor(y[:, t % 3, :], h[:, t, :], src.rs[:, t:t + 1], src.g[:],
                                             ALU.mult, ALU.mult).then_inc(y_ready, 1)


def build(nc, a, o):
    (y_p, y_s, ak_p, av_p, lf_p, bk_p, bv_p, ak_s, av_s, lf_s, bk_s, bv_s) = o

    def flat(ap, pattern):
        return ap.rearrange(pattern)

    x_p = a["x_prompt"][0]
    x_s = flat(a["x_sample"], "b t d -> (b t) d")
    y_p, y_s = y_p[0], flat(y_s, "b t d -> (b t) d")
    akp, avp = (flat(x[0, 0], "t h d -> t (h d)") for x in (ak_p, av_p))
    aks, avs = (flat(x[0], "b t h d -> (b t) (h d)") for x in (ak_s, av_s))
    lfp, lfs = lf_p[0, 0], flat(lf_s[0], "b t h -> (b t) h")
    bkp, bvp = (flat(x[0], "t h d -> t (h d)") for x in (bk_p, bv_p))
    bks, bvs = (flat(x, "b t h d -> b t (h d)") for x in (bk_s, bv_s))
    cak, cav = (flat(a[n][0], "b t h d -> b t (h d)") for n in ("cache_a_k", "cache_a_v"))
    cbk, cbv = (flat(a[n], "b t h d -> b t (h d)") for n in ("cache_b_k", "cache_b_v"))

    def scratch(name, shape):
        return nc.dram_tensor(name, shape, F32, kind="Internal").ap()

    qh_d, ql_d = scratch("q_high", (HEADS, P, TOK)), scratch("q_low", (HEADS, P, TOK))
    ks_d = scratch("k_split", (HEADS, P, KT * P))
    vb_d = scratch("band_v", (TOK, D))
    at_d = scratch("attn_turned", (D, TOK))
    negcum = scratch("negcum", (HEADS, KT * P))
    line = scratch("distances", (HEADS, TOEP))
    toep = scratch("band_bias", (HEADS, P, TOEP - P)), scratch("stream_bias", (HEADS, P, CACHED + NEW))

    def weights(w, at=0):
        v = w.rearrange("(c p) n -> p c n", p=P)
        return lambda n: v[:, :, bass.ds(n * WC + at, WC)]

    def turned_stores(kind, i, t, high, low):
        if kind == "q":
            to = [(qh_d, u * HD, t, high) for u in range(2)] + [(ql_d, u * HD, t, low) for u in range(2)]
        else:
            to = split_to(high, low, t)
        return place(i, to)

    def split_to(high, low, t):
        return [(ks_d, 0, t, high), (ks_d, HD, t, low)]

    def place(i, to):
        out = []
        for dst, row, t, src in to:
            for hh in range(2):
                heads = dst[i * 8:(i + 1) * 8].rearrange("(j x) r n -> x r j n", x=2)[hh]
                out.append((heads[row:row + HD, :, t * P:(t + 1) * P],
                            None if src is None else
                            src[hh * HD:(hh + 1) * HD, :].rearrange("r (j n) -> r j n", n=P)))
        return out

    def cached_stores(i, b, high, low):
        return place(i, split_to(high, low, QT + b))

    def new_key_tile(kind, t):
        return KT - 1 if kind == "k" and t == QT else t

    def fox_turned(kind, i, t, high, low):
        return turned_stores(kind, i, new_key_tile(kind, t), high, low)

    def fox_stage(kind, i, t, s):
        prompt, sample = (akp, aks) if kind == "k" else (avp, avs)
        dst = prompt[t * P:(t + 1) * P] if t < QT else sample
        return [(dst[:, i * WC:(i + 1) * WC], s)]

    def band_stage(kind, i, t, s):
        full, kept_p, kept_s = (None, bkp, bks) if kind == "k" else (vb_d, bvp, bvs)
        cols = slice(i * WC, (i + 1) * WC)
        out = [(full[t * P:(t + 1) * P, cols], s)] if kind == "v" else []
        if t == QT:
            out.append((kept_s[:, CACHED - NEW:, cols], s))
        elif t >= QT // 2:
            out.append((kept_p[(t - QT // 2) * P:(t - QT // 2 + 1) * P, cols], s))
        return out

    def parts(prompt, cached, new):
        return [(0, QT, lambda c: prompt[:, c].rearrange("(t p) n -> p t n", p=P)),
                (QT, STREAMS, lambda c: cached[:, :, c].rearrange("b p n -> p b n")),
                (QT + STREAMS, 1, lambda c: new[:, c].rearrange("(o p) n -> p o n", o=1))]

    with Phase(nc, "all") as al:
        h = al.sb("h", [P, NT, D])
        ident = al.sb("ident", [P, P])
        half = al.sb("half", [P, 1])
        cq = al.sb("cq", [P, NT, HEADS])
        x_in = [al.sem(f"x_in{t}") for t in range(NT)]
        kept = al.sem("kept")

        def load_x(sp, t0, t1):
            for t in range(t0, t1):
                sp.dma_start(h[:, t, :], x_p[t * P:(t + 1) * P, :] if t < QT else x_s).then_inc(x_in[t], 16)
            if t0:
                for dst, src in ((bks, cbk), (bvs, cbv)):
                    sp.dma_start(dst[:, 0:CACHED - NEW, :], src[:, NEW:, :]).then_inc(kept, 16)

        setup_block(nc, ident, half)
        w_in = a["w_a_in"][0]
        dense_block(nc, "qkv", h, ident, half, weights(w_in), "qqkkvv", g_ap=a["g_attn"][0],
                    stage_stores=fox_stage, turned_stores=fox_turned,
                    cached=lambda i, b: cak[b, :, i * WC:(i + 1) * WC], cached_stores=cached_stores,
                    x_in=x_in, load_x=load_x,
                    gate=lambda xh, xl: gate_block(nc, xh, xl, ident, w_in[:, 3 * D:], a["b_a_f"][0],
                                                   a["cache_a_logf"][0], lfp, lfs, negcum, cq))
        attention_block(nc, "fox", ident, ks_d, qh_d, ql_d, parts(avp, cav, avs), at_d, cq=cq, negcum=negcum)
        dense_block(nc, "aout", h, ident, half, weights(a["w_a_out"][0]), ("add", "add"), turned_src=at_d)
        ffn_block(nc, "ffn0", h, ident, half, a["g_ffn"][0], a["w_gate_up"][0], a["w_down"][0])
        w_kv = weights(a["w_kv"])
        dense_block(nc, "kv", h, ident, half, lambda n: w_kv((n + 2) % 4), "vvkk", g_ap=a["g_kv"],
                    stage_stores=band_stage, turned_stores=fox_turned,
                    cached=lambda i, b: cbk[b, :, i * WC:(i + 1) * WC], cached_stores=cached_stores)
        dense_block(nc, "bq", h, ident, half, weights(a["w_b_q"][0]), "qq", g_ap=a["g_attn"][1],
                    turned_stores=fox_turned)
        distances_block(nc, a["rel_bias"][0], line, toep)
        attention_block(nc, "band", ident, ks_d, qh_d, ql_d, parts(vb_d[0:QT * P], cbv, vb_d[QT * P:]), at_d,
                        toep=toep)
        dense_block(nc, "bout", h, ident, half, weights(a["w_b_out"][0]), ("add", "add"), turned_src=at_d)
        ffn_block(nc, "ffn1", h, ident, half, a["g_ffn"][1], a["w_gate_up"][1], a["w_down"][1])
        final_block(nc, h, half, a["g_final"], lambda t: y_p[t * P:(t + 1) * P, :] if t < QT else y_s)
        with nc.Block() as block:
            @block.sync
            def _(sp):
                sp.wait_ge(kept, 32)


OUTPUTS = [(1, 1024, 1024), (8, 16, 1024), (1, 1, 1024, 16, 64), (1, 1, 1024, 16, 64), (1, 1, 1024, 16),
           (1, 512, 16, 64), (1, 512, 16, 64), (1, 8, 16, 16, 64), (1, 8, 16, 16, 64), (1, 8, 16, 16),
           (8, 128, 16, 64), (8, 128, 16, 64)]
INPUTS = ["x_prompt", "x_sample", "cache_a_k", "cache_a_v", "cache_a_logf", "cache_b_k", "cache_b_v", "g_attn",
          "w_a_in", "b_a_f", "w_a_out", "w_b_q", "rel_bias", "w_b_out", "g_kv", "w_kv", "g_ffn", "w_gate_up",
          "w_down", "g_final"]


def kernel(**inputs):
    import numpy as np
    import concourse.bacc as bacc
    from concourse.bass_utils import run_bass_kernel_spmd

    nc = bacc.Bacc("TRN2", target_bir_lowering=False, num_devices=1)
    arrays, aps = {}, {}
    for name in INPUTS:
        x = np.ascontiguousarray(inputs[name])
        arrays[f"in_{name}"] = x
        aps[name] = nc.dram_tensor(f"in_{name}", x.shape, F32, kind="ExternalInput").ap()
    outs = [nc.dram_tensor(f"out_{i}", s, F32, kind="ExternalOutput").ap() for i, s in enumerate(OUTPUTS)]
    build(nc, aps, outs)
    r = run_bass_kernel_spmd(nc, [arrays], core_ids=[0])
    return tuple(r.results[0][f"out_{i}"] for i in range(len(OUTPUTS)))
```

```python
from contextlib import ExitStack

import concourse.bass as bass
from concourse import mybir

F32 = mybir.dt.float32
F32R = mybir.dt.float32r
ALU = mybir.AluOpType
ACT = mybir.ActivationFunctionType

P = 128
D = 1024
KC = D // P
HEADS = 16
HD = 64
PAIRS = HEADS // 2
QT = 8
NT = QT + 1
TOK = NT * P
STREAMS = 8
NEW = 16
CACHED = 128
KT = QT + STREAMS + 1
DFF = 2816
GW = 256
GROUPS = DFF // GW
GC = GW // P
PIECES = 4
WC = 512
EPS = 1e-6
NEG = -1e30
BIG = 3.0e38
SCALE = HD ** -0.5
BAND_TILES = 4
REL = 128
NREL = 2 * REL + 1
TOEP = (BAND_TILES + 1) * P + P


def f32(ap):
    return ap.bitcast(F32)


def wait(eng, sem, count):
    if isinstance(count, int) and count <= 0:
        return
    eng.wait_ge(sem, count)


class Phase:

    def __init__(self, nc, name):
        self.nc, self.name, self.ctx, self.sems = nc, name, ExitStack(), []

    def sem(self, what):
        self.sems.append(self.nc.alloc_semaphore(f"{self.name}_{what}"))
        return self.sems[-1]

    def sb(self, what, shape, dt=F32):
        return self.ctx.enter_context(self.nc.sbuf_tensor(f"{self.name}_{what}", shape, dt))

    def ps(self, what, shape):
        return self.ctx.enter_context(self.nc.psum_tensor(f"{self.name}_{what}", shape, F32))

    def __enter__(self):
        return self

    def __exit__(self, *e):
        if self.sems and not any(e):
            self.nc.clear_and_free_semaphores(self.sems)
            self.nc.all_engine_barrier()
        return self.ctx.__exit__(*e)


def setup_block(nc, ident, half, load_gains):
    with Phase(nc, "setup") as ph:
        made = ph.sem("made")
        with nc.Block() as block:
            @block.sync
            def _(sp):
                load_gains(sp)

            @block.gpsimd
            def _(pool):
                pool.memset(half[:], -0.5).then_inc(made, 1)
                pool.memset(ident[:], 0.0).then_inc(made, 1)
                pool.wait_ge(made, 2)
                pool.affine_select(out=ident[:], in_=ident[:], compare_op=ALU.not_equal, fill=1.0,
                                   base=0, pattern=[[-1, P]], channel_multiplier=1).then_inc(made, 1)


def stream_mask(pool, one, out, made):
    pool.memset(one[:], 0.0).then_inc(made, 1)
    pool.memset(out[:], NEG).then_inc(made, 1)
    pool.wait_ge(made, 2)
    for view, width, fill in ((one[:], NEW, 1.0), (out[:, 0:STREAMS * CACHED], CACHED, 0.0),
                              (out[:, STREAMS * CACHED:], NEW, 0.0)):
        view = view.rearrange("p (b k) -> p b k", b=STREAMS)
        pool.affine_select(out=view, in_=view, compare_op=ALU.not_equal, fill=fill, base=0,
                           pattern=[[-1, STREAMS], [0, width]], channel_multiplier=1).then_inc(made, 1)


class Norm:

    def __init__(self, ph, h, ident, half, xh, xl, ptr, x_in=None):
        self.ph, self.h, self.ident, self.half = ph, h, ident, half
        self.xh, self.xl, self.ptr, self.x_in = xh, xl, ptr, x_in
        self.sq = ph.sb("sq", [P, D], mybir.dt.bfloat16)
        self.ss = ph.sb("ss", [P, NT])
        self.ms = ph.sb("ms", [P, NT])
        self.rs = ph.sb("rs", [P, NT])
        self.xn = ph.sb("xn", [P, 2, D])
        self.squared, self.mean_ready, self.rs_ready = ph.sem("squared"), ph.sem("mean_ready"), ph.sem("rs_ready")
        self.xn_ready, self.turned = ph.sem("xn_ready"), ph.sem("turned")
        self.high_ready, self.low_ready = ph.sem("high_ready"), ph.sem("low_ready")

    def squares(self, act, t):
        if self.x_in:
            act.wait_ge(self.x_in[t], 16)
        if t:
            act.wait_ge(self.squared, t)
        act.activation(self.sq[:], self.h[:, t, :], ACT.Square,
                       accum_out=self.ss[:, t:t + 1]).then_inc(self.squared, 1)

    def rsqrt(self, pool, t):
        pool.wait_ge(self.squared, t + 1)
        pool.tensor_scalar(self.ms[:, t:t + 1], self.ss[:, t:t + 1], 1.0 / D, EPS,
                           ALU.mult, ALU.add).then_inc(self.mean_ready, 1)
        pool.wait_ge(self.mean_ready, t + 1)
        pool.tensor_tensor(out=self.rs[:, t:t + 1], in0=self.ms[:, t:t + 1], in1=self.half[:],
                           op=ALU.pow).then_inc(self.rs_ready, 1)

    def scaled(self, dve, t):
        dve.wait_ge(self.rs_ready, t + 1)
        if t >= 2:
            dve.wait_ge(self.turned, 2 * (t - 1))
        dve.tensor_scalar(self.xn[:, t % 2, :], self.h[:, t, :], self.rs[:, t:t + 1], None,
                          ALU.mult).then_inc(self.xn_ready, 1)

    def turn(self, pe, t):
        pe.wait_ge(self.xn_ready, t + 1)
        if t:
            pe.wait_ge(self.low_ready, 2 * t)
        for half in range(2):
            for j in range(4):
                c = 4 * half + j
                last = pe.transpose(self.ptr[:, half, j * P:(j + 1) * P],
                                    self.xn[:, t % 2, c * P:(c + 1) * P], self.ident[:])
            last.then_inc(self.turned, 1)

    def views(self, half, t):
        cols = slice(t * P, (t + 1) * P)
        src = self.ptr[:, half, :].rearrange("p (c n) -> p c n", c=4)
        return self.xh[:, 4 * half:4 * half + 4, cols], self.xl[:, 4 * half:4 * half + 4, cols], src

    def high(self, act, t):
        for half in range(2):
            xh, _, src = self.views(half, t)
            act.wait_ge(self.turned, 2 * t + half + 1)
            act.activation(xh, src, ACT.Copy).then_inc(self.high_ready, 1)

    def low(self, dve, t):
        for half in range(2):
            xh, xl, src = self.views(half, t)
            dve.wait_ge(self.high_ready, 2 * t + half + 1)
            dve.tensor_tensor(xl, src, f32(xh), ALU.subtract).then_inc(self.low_ready, 1)

    def ready(self, pe, t):
        pe.wait_ge(self.low_ready, 2 * t + 2)


class Turned:

    def __init__(self, ph, src, xh, xl):
        self.src, self.xh, self.xl = src, xh, xl
        self.raw = ph.sb("at", [P, 2, KC, P])
        self.loaded = [ph.sem(f"at_loaded{i}") for i in range(2)]
        self.high_ready, self.low_ready = ph.sem("high_ready"), ph.sem("low_ready")

    def squares(self, act, t):
        pass

    def rsqrt(self, pool, t):
        pass

    def scaled(self, dve, t):
        pass

    def turn(self, pe, t):
        pass

    def fetch(self, sp, t):
        if t >= 2:
            sp.wait_ge(self.low_ready, t - 1)
        sp.dma_start(self.raw[:, t % 2], self.src[:, t * P:(t + 1) * P].rearrange("(c p) n -> p c n", p=P)
                     ).then_inc(self.loaded[t % 2], 16)

    def high(self, act, t):
        act.wait_ge(self.loaded[t % 2], 16 * (t // 2 + 1))
        act.activation(self.xh[:, :, t * P:(t + 1) * P], self.raw[:, t % 2], ACT.Copy).then_inc(self.high_ready, 1)

    def low(self, dve, t):
        dve.wait_ge(self.high_ready, t + 1)
        dve.tensor_tensor(self.xl[:, :, t * P:(t + 1) * P], self.raw[:, t % 2],
                          f32(self.xh[:, :, t * P:(t + 1) * P]), ALU.subtract).then_inc(self.low_ready, 1)

    def ready(self, pe, t):
        pe.wait_ge(self.low_ready, t + 1)


def split_high(act, high, raw, gain, c):
    if gain is None:
        return act.activation(high, raw, ACT.Copy)
    return act.activation(high, raw, ACT.Copy, scale=gain[:, c:c + 1])


def split_low(dve, low, raw, high, gain, c):
    if gain is None:
        return dve.tensor_tensor(low, raw, f32(high), ALU.subtract)
    return dve.scalar_tensor_tensor(low, raw, gain[:, c:c + 1], f32(high), ALU.mult, ALU.subtract)


def product(pe, out, xh, xl, wh, wl, first, last):
    pe.matmul(out, xh, wh, start=first, stop=False)
    pe.matmul(out, xh, wl, start=False, stop=False)
    return pe.matmul(out, xl, wh, start=False, stop=last)


class Chunk:

    def __init__(self, n, kind, before):
        self.n, self.kind, self.before = n, kind, before


def dense_block(nc, name, h, ident, half, w_of, kinds, gain_of=lambda n: None, turned_src=None,
                stage_stores=None, turned_stores=None, cached=None, cached_stores=None, x_in=None, load_x=None,
                gains_loaded=None, gate=None, aside=None):
    chunks = len(kinds)
    NS, NTS, NCS = 3, 3, 2

    def dmas_of(kind):
        stage = [0] * NS
        turned = [0] * NTS
        cach = [0] * NCS
        for t in range(NT):
            if kind in ("v", "k"):
                stage[t % NS] += len(stage_stores(kind, 0, t, None))
            if kind in ("q", "k"):
                turned[t % NTS] += len(turned_stores(kind, 0, t, None, None))
            if kind == "k" and t < STREAMS:
                cach[t % NCS] += len(cached_stores(0, t, None, None))
        return {"stage": stage, "turned": turned, "cached": cach, "craw": [STREAMS // 2] * 2 if kind == "k" else [0, 0],
                "turns": [NT if kind in ("q", "k") else 0], "cturns": [STREAMS if kind == "k" else 0]}

    def chunks_of(eng, body):
        before = {k: [0] * len(v) for k, v in dmas_of("add").items()}
        for n, kind in enumerate(kinds):
            per = dmas_of(kind)
            body(Chunk(n, kind, before))
            before = {k: [b + per[k][x] for x, b in enumerate(v)] for k, v in before.items()}

    storing = "add" not in kinds
    turning = "q" in kinds or "k" in kinds
    with Phase(nc, name) as ph:
        xh = ph.sb("xh", [P, KC, TOK], F32R)
        xl = ph.sb("xl", [P, KC, TOK], F32R)
        with Phase(nc, name + "w") as pw:
            wraw = pw.sb("raw", [P, KC, WC])
            wh = pw.sb("h", [P, KC, WC], F32R)
            wl = pw.sb("l", [P, KC, WC], F32R)
            acc = pw.ps("acc", [P, 3, WC])
            ptr = pw.ps("ptr", [P, 2, WC])
            if turned_src is not None:
                src = Turned(pw, turned_src, xh, xl)
            else:
                src = Norm(pw, h, ident, half, xh, xl, ptr, x_in)
            raw_loaded = pw.sem("raw_loaded")
            piece_loaded = [pw.sem(f"piece_loaded{i}") for i in range(PIECES)]
            wh_ready, wl_ready, w_used = pw.sem("wh_ready"), pw.sem("wl_ready"), pw.sem("w_used")
            acc_ready, acc_used = pw.sem("acc_ready"), pw.sem("acc_used")
            if storing:
                stage = pw.sb("stage", [P, NS, WC])
                stored = [pw.sem(f"stored{i}") for i in range(NS)]
            if turning:
                kt = pw.ps("kt", [P, WC])
                th = pw.sb("th", [P, NTS, WC])
                tl = pw.sb("tl", [P, NTS, WC])
                t_done, th_done, tl_done = pw.sem("t_done"), pw.sem("th_done"), pw.sem("tl_done")
                t_stored = [pw.sem(f"t_stored{i}") for i in range(NTS)]
            if "k" in kinds:
                ct = pw.ps("ct", [P, WC])
                craw = pw.sb("craw", [P, NCS, WC])
                ch = pw.sb("ch", [P, NCS, WC])
                cl = pw.sb("cl", [P, NCS, WC])
                c_loaded = [pw.sem(f"c_loaded{i}") for i in range(NCS)]
                c_done, ch_done, cl_done = pw.sem("c_done"), pw.sem("ch_done"), pw.sem("cl_done")
                c_stored = [pw.sem(f"c_stored{i}") for i in range(NCS)]

            def chunk_high(act, n, between=None):
                if n:
                    act.wait_ge(raw_loaded, 16 * n)
                elif gains_loaded:
                    act.wait_ge(*gains_loaded)
                for c in range(KC):
                    if n:
                        if c < KC - 1:
                            act.wait_ge(w_used, (KC - 1) * (n - 1) + c + 1)
                        else:
                            act.wait_ge(acc_ready, NT * n)
                    elif c % (KC // PIECES) == 0:
                        act.wait_ge(piece_loaded[c // (KC // PIECES)], 16)
                    split_high(act, wh[:, c, :], wraw[:, c, :], gain_of(n), c).then_inc(wh_ready, 1)
                    if between and c == 1:
                        between()

            def chunk_low(dve, n, between=None):
                for c in range(KC):
                    dve.wait_ge(wh_ready, KC * n + c + 1)
                    split_low(dve, wl[:, c, :], wraw[:, c, :], wh[:, c, :], gain_of(n), c).then_inc(wl_ready, 1)
                    if between and c == 1:
                        between()

            def multiply(pe, n, t):
                if t >= 3 or n:
                    pe.wait_ge(acc_used, NT * n + t - 2)
                rows = slice(t * P, (t + 1) * P)
                for c in range(KC):
                    if t == 0:
                        pe.wait_ge(wl_ready, KC * n + c + 1)
                    last = product(pe, acc[:, t % 3, :], xh[:, c, rows], xl[:, c, rows],
                                   wh[:, c, :], wl[:, c, :], c == 0, c == KC - 1)
                    if t == NT - 1 and c < KC - 1:
                        last.then_inc(w_used, 1)
                last.then_inc(acc_ready, 1)

            def empty(eng, ck, t):
                n = ck.n
                eng.wait_ge(acc_ready, NT * n + t + 1)
                if storing:
                    before = ck.before["stage"][t % NS]
                    here = 0
                    if ck.kind in ("v", "k"):
                        here = sum(len(stage_stores(ck.kind, 0, u, None)) for u in range(t % NS, t, NS))
                    wait(eng, stored[t % NS], 16 * (before + here))
                    if turning:
                        before = ck.before["turns"][0]
                        wait(eng, t_done, before + (t - NS + 1 if ck.kind != "v" else 0))
                    eng.activation(stage[:, t % NS, :], acc[:, t % 3, :], ACT.Copy,
                                   scale=SCALE if ck.kind == "q" else 1.0).then_inc(acc_used, 1)
                else:
                    part = h[:, t, n * WC:(n + 1) * WC]
                    eng.tensor_tensor(part, acc[:, t % 3, :], part, ALU.add).then_inc(acc_used, 1)

            def turn_tile(pe, ck, t):
                before = ck.before["turns"][0]
                pe.wait_ge(acc_used, NT * ck.n + t + 1)
                wait(pe, tl_done, before + t)
                for j in range(4):
                    last = pe.transpose(kt[:, j * P:(j + 1) * P], stage[:, t % NS, j * P:(j + 1) * P], ident[:])
                last.then_inc(t_done, 1)

            def turned_high(act, ck, t):
                before = ck.before["turns"][0]
                wait(act, t_done, before + t + 1)
                wait_turned_slot(act, ck, t)
                act.activation(th[:, t % NTS, :].bitcast(F32R), kt[:], ACT.Copy).then_inc(th_done, 1)

            def wait_turned_slot(eng, ck, t):
                before = ck.before["turned"][t % NTS]
                if t >= 0:
                    here = sum(len(turned_stores(ck.kind, 0, u, None, None)) for u in range(t % NTS, t, NTS))
                else:
                    here = -len(turned_stores(kinds[ck.n - 1], 0, NT - 1, None, None))
                wait(eng, t_stored[t % NTS], 16 * (before + here))

            def turned_low(dve, ck, t):
                before = ck.before["turns"][0]
                wait(dve, th_done, before + t + 1)
                dve.tensor_tensor(tl[:, t % NTS, :].bitcast(F32R), kt[:], th[:, t % NTS, :],
                                  ALU.subtract).then_inc(tl_done, 1)

            def turn_cached(pe, ck, t):
                before = ck.before["cturns"][0]
                craw_before = ck.before["craw"][t % NCS]
                pe.wait_ge(c_loaded[t % NCS], 16 * (craw_before + t // NCS + 1))
                wait(pe, cl_done, before + t)
                for j in range(4):
                    last = pe.transpose(ct[:, j * P:(j + 1) * P], craw[:, t % NCS, j * P:(j + 1) * P], ident[:])
                last.then_inc(c_done, 1)

            def cached_high(act, ck, t):
                before = ck.before["cturns"][0]
                wait(act, c_done, before + t + 1)
                before = ck.before["cached"][t % NCS]
                here = sum(len(cached_stores(0, u, None, None)) for u in range(t % NCS, t, NCS))
                wait(act, c_stored[t % NCS], 16 * (before + here))
                act.activation(ch[:, t % NCS, :].bitcast(F32R), ct[:], ACT.Copy).then_inc(ch_done, 1)

            def cached_low(dve, ck, t):
                before = ck.before["cturns"][0]
                wait(dve, ch_done, before + t + 1)
                dve.tensor_tensor(cl[:, t % NCS, :].bitcast(F32R), ct[:], ch[:, t % NCS, :],
                                  ALU.subtract).then_inc(cl_done, 1)

            def turned_before(ck):
                return ck.n > 0 and kinds[ck.n - 1] in ("q", "k")

            def after_tile(eng, ck, t, turned_part, cached_part):
                if t == 0:
                    if turned_before(ck):
                        turned_part(eng, ck, -1)
                elif ck.kind in ("q", "k"):
                    turned_part(eng, ck, t - 1)
                    if ck.kind == "k":
                        cached_part(eng, ck, t - 1)

            def leftover(eng, turned_part):
                if kinds[-1] in ("q", "k"):
                    before = {k: [sum(dmas_of(x)[k][i] for x in kinds) for i in range(len(v))]
                              for k, v in dmas_of("add").items()}
                    turned_part(eng, Chunk(chunks, "v", before), -1)

            with nc.Block() as block:
                @block.sync
                def _(sp):
                    if load_x:
                        load_x(sp, 0, 2)
                    if turned_src is not None:
                        src.fetch(sp, 0)
                    for i in range(PIECES):
                        part = slice(i * KC // PIECES, (i + 1) * KC // PIECES)
                        sp.dma_start(wraw[:, part, :], w_of(0)[:, part, :]).then_inc(piece_loaded[i], 16)
                    if load_x:
                        load_x(sp, 2, NT)
                    if turned_src is not None:
                        for t in range(1, NT):
                            src.fetch(sp, t)
                    seen = {}

                    def store_turned(kind, i, t, turns):
                        sp.wait_ge(tl_done, turns)
                        for dst, s in turned_stores(kind, i, t, th[:, t % NTS, :], tl[:, t % NTS, :]):
                            sp.dma_start(dst, s).then_inc(t_stored[t % NTS], 16)

                    turns = cturns = 0
                    pending = None
                    for n, kind in enumerate(kinds):
                        i = seen.setdefault(kind, 0)
                        seen[kind] += 1
                        if kind == "k":
                            for t in range(NCS):
                                sp.dma_start(craw[:, t, :], cached(i, t)).then_inc(c_loaded[t], 16)
                        if n + 1 < chunks:
                            sp.wait_ge(wl_ready, KC * (n + 1))
                            sp.dma_start(wraw[:], w_of(n + 1)).then_inc(raw_loaded, 16)
                        for t in range(NT):
                            if kind in ("v", "k"):
                                sp.wait_ge(acc_used, NT * n + t + 1)
                                for dst, s in stage_stores(kind, i, t, stage[:, t % NS, :]):
                                    sp.dma_start(dst, s).then_inc(stored[t % NS], 16)
                            if pending:
                                turns += 1
                                store_turned(*pending, turns)
                                pending = None
                            if kind == "k" and t:
                                u = t - 1
                                cturns += 1
                                sp.wait_ge(cl_done, cturns)
                                for dst, s in cached_stores(i, u, ch[:, u % NCS, :], cl[:, u % NCS, :]):
                                    sp.dma_start(dst, s).then_inc(c_stored[u % NCS], 16)
                                if u + NCS < STREAMS:
                                    sp.dma_start(craw[:, u % NCS, :], cached(i, u + NCS)).then_inc(c_loaded[u % NCS], 16)
                            if kind in ("q", "k"):
                                pending = (kind, i, t)
                    if pending:
                        turns += 1
                        store_turned(*pending, turns)
                    if aside:
                        aside.sync(sp)
                    totals = {k: [sum(dmas_of(x)[k][i] for x in kinds) for i in range(len(v))]
                              for k, v in dmas_of("add").items()}
                    if storing:
                        for i in range(NS):
                            if totals["stage"][i]:
                                sp.wait_ge(stored[i], 16 * totals["stage"][i])
                    if turning:
                        for i in range(NTS):
                            sp.wait_ge(t_stored[i], 16 * totals["turned"][i])
                    if "k" in kinds:
                        for i in range(NCS):
                            sp.wait_ge(c_stored[i], 16 * totals["cached"][i])

                @block.gpsimd
                def _(pool):
                    for t in range(NT):
                        src.rsqrt(pool, t)

                @block.scalar
                def _(act):
                    src.squares(act, 0)
                    src.squares(act, 1)
                    chunk_high(act, 0, lambda: src.high(act, 0))

                    def chunk(ck):
                        first = ck.n == 0
                        for t in range(NT):
                            if first:
                                if t:
                                    src.high(act, t)
                                if t + 2 < NT:
                                    src.squares(act, t + 2)
                            if t == NT - 1 and ck.n < chunks - 1:
                                chunk_high(act, ck.n + 1)
                            if storing and not (first and t == 0):
                                empty(act, ck, t - 1 if first else t)
                                if first and t == NT - 1:
                                    after_tile(act, ck, t - 1, turned_high, cached_high)
                                    empty(act, ck, t)
                                after_tile(act, ck, t - 1 if first and t < NT - 1 else t, turned_high, cached_high)

                    chunks_of(act, chunk)
                    leftover(act, turned_high)
                    if aside:
                        aside.act(act)

                @block.vector
                def _(dve):
                    src.scaled(dve, 0)
                    src.scaled(dve, 1)
                    chunk_low(dve, 0, lambda: src.low(dve, 0))

                    def chunk(ck):
                        first = ck.n == 0
                        for t in range(NT):
                            if first and storing:
                                if t:
                                    src.low(dve, t)
                                if t + 2 < NT:
                                    src.scaled(dve, t + 2)
                            elif first:
                                if t + 1 < NT:
                                    src.low(dve, t + 1)
                            if t == NT - 1 and ck.n < chunks - 1:
                                chunk_low(dve, ck.n + 1)
                            if not storing:
                                empty(dve, ck, t)
                            elif first:
                                if t:
                                    after_tile(dve, ck, t - 1, turned_low, cached_low)
                                if t == NT - 1:
                                    after_tile(dve, ck, t, turned_low, cached_low)
                            else:
                                after_tile(dve, ck, t, turned_low, cached_low)

                    chunks_of(dve, chunk)
                    leftover(dve, turned_low)

                @block.tensor
                def _(pe):
                    def chunk(ck):
                        first = ck.n == 0
                        for t in range(NT):
                            if first:
                                if t == 0:
                                    src.turn(pe, 0)
                                if t + 1 < NT:
                                    src.turn(pe, t + 1)
                                src.ready(pe, t)
                            multiply(pe, ck.n, t)
                            if first and storing:
                                if t:
                                    after_tile(pe, ck, t - 1, turn_tile, turn_cached)
                                if t == NT - 1:
                                    after_tile(pe, ck, t, turn_tile, turn_cached)
                            elif storing:
                                after_tile(pe, ck, t, turn_tile, turn_cached)

                    chunks_of(pe, chunk)
                    leftover(pe, turn_tile)
        if gate:
            gate(xh, xl)


def gate_block(nc, xh, xl, ident, gain, wf_ap, bf_ap, clf_ap, lf_p, lf_s, negcum, cq):
    with Phase(nc, "gate") as ph:
        wraw = ph.sb("wraw", [P, KC, HEADS])
        wh = ph.sb("wh", [P, KC, HEADS], F32R)
        wl = ph.sb("wl", [P, KC, HEADS], F32R)
        bf = ph.sb("bf", [HEADS, 1])
        clf = ph.sb("clf", [P, STREAMS, HEADS])
        tri = ph.sb("tri", [P, P])
        trib = ph.sb("trib", [P, P])
        z = ph.sb("z", [HEADS, TOK])
        zt, u, w, e = (ph.sb(n, [P, NT * HEADS]) for n in ("zt", "u", "w", "e"))
        lf = ph.sb("lf", [P, NT, HEADS])
        cum = ph.sb("cum", [HEADS, KT * P])
        ncum = ph.sb("ncum", [HEADS, KT * P])
        pf = ph.ps("pf", [P, 3, WC])
        pc = ph.ps("pc", [P, 5, WC])
        loaded, split, made = ph.sem("loaded"), ph.sem("split"), ph.sem("made")
        f_ready, biased, chain, lnd = ph.sem("f_ready"), ph.sem("biased"), ph.sem("chain"), ph.sem("lnd")
        turned, summed, cq_turned, cq_ready = (ph.sem(s) for s in ("turned", "summed", "cq_turned", "cq_ready"))
        stored = ph.sem("stored")
        spans = [(0, WC), (WC, WC), (2 * WC, TOK - 2 * WC)]
        with nc.Block() as block:
            @block.sync
            def _(sp):
                with nc.allow_non_contiguous_dma("small"):
                    sp.dma_start(wraw[:], wf_ap.rearrange("(c p) n -> p c n", p=P)).then_inc(loaded, 16)
                    sp.dma_start(bf[:], bf_ap.rearrange("(h o) -> h o", o=1)).then_inc(loaded, 16)
                    sp.dma_start(clf[:], clf_ap.rearrange("b k h -> k b h")).then_inc(loaded, 16)
                    sp.wait_ge(chain, 7)
                    sp.dma_start(lf_p.rearrange("(t p) h -> p t h", p=P), lf[:, 0:QT, :]).then_inc(stored, 16)
                    sp.dma_start(lf_s, lf[:, QT, :]).then_inc(stored, 16)
                    sp.wait_ge(chain, 7 + QT + 3)
                    sp.dma_start(negcum, ncum[:]).then_inc(stored, 16)
                    sp.wait_ge(stored, 48)

            @block.gpsimd
            def _(pool):
                pool.memset(tri[:], 1.0).then_inc(made, 1)
                pool.wait_ge(made, 1)
                pool.affine_select(out=tri[:], in_=tri[:], compare_op=ALU.is_ge, fill=0.0, base=0,
                                   pattern=[[1, P]], channel_multiplier=-1).then_inc(made, 1)
                pool.wait_ge(made, 2)
                pool.affine_select(out=trib[:].rearrange("p (b n) -> p b n", b=STREAMS),
                                   in_=tri[:].rearrange("p (b n) -> p b n", b=STREAMS),
                                   compare_op=ALU.is_ge, fill=0.0, base=0,
                                   pattern=[[-NEW, STREAMS], [0, NEW]], channel_multiplier=1).then_inc(made, 1)

            @block.scalar
            def _(act):
                act.wait_ge(split, 1)
                act.activation(wh[:], wraw[:], ACT.Copy).then_inc(split, 1)
                act.wait_ge(chain, 2)
                act.activation(u[:], u[:], ACT.Exp, scale=-1.0).then_inc(lnd, 1)
                act.wait_ge(chain, 3)
                act.activation(w[:], w[:], ACT.Ln).then_inc(lnd, 1)
                act.wait_ge(cq_turned, 1)
                act.activation(cq[:], pf[:, 1, 0:NT * HEADS].rearrange("p (t h) -> p t h", t=NT),
                               ACT.Copy).then_inc(cq_ready, 1)

            @block.vector
            def _(dve):
                steps = [0]

                def link(ins):
                    steps[0] += 1
                    ins.then_inc(chain, 1)
                    dve.wait_ge(chain, steps[0])

                dve.wait_ge(loaded, 48)
                dve.tensor_tensor(wraw[:], wraw[:], gain.rearrange("p (c o) -> p c o", o=1)
                                  .to_broadcast([P, KC, HEADS]), ALU.mult).then_inc(split, 1)
                dve.wait_ge(split, 2)
                dve.tensor_tensor(wl[:], wraw[:], f32(wh[:]), ALU.subtract).then_inc(split, 1)
                dve.wait_ge(f_ready, 1)
                dve.tensor_scalar(z[:], pf[0:HEADS, :, :].rearrange("p a n -> p (a n)")[:, 0:TOK],
                                  bf[:, 0:1], None, ALU.add).then_inc(biased, 1)
                dve.wait_ge(turned, 1)
                link(dve.tensor_copy(zt[:], pf[:, 0, 0:NT * HEADS]))
                link(dve.scalar_tensor_tensor(u[:], zt[:], -1.0, zt[:], ALU.mult, ALU.max))
                dve.wait_ge(lnd, 1)
                link(dve.tensor_scalar(w[:], u[:], 1.0, None, ALU.add))
                link(dve.tensor_scalar(e[:], u[:], 1.0, None, ALU.add))
                link(dve.scalar_tensor_tensor(e[:], e[:], 1.0, u[:], ALU.subtract, ALU.subtract))
                dve.wait_ge(lnd, 2)
                link(dve.scalar_tensor_tensor(zt[:], zt[:], 0.0, w[:], ALU.min, ALU.subtract))
                link(dve.tensor_tensor(lf[:].rearrange("p t h -> p (t h)"), zt[:], e[:], ALU.add))
                dve.wait_ge(summed, 1)
                for t in range(QT):
                    cols = slice(t * P, (t + 1) * P)
                    src = pc[0:HEADS, t // 4, (t % 4) * P:(t % 4 + 1) * P]
                    if t == 0:
                        link(dve.tensor_copy(cum[:, cols], src))
                    else:
                        link(dve.tensor_scalar(cum[:, cols], src, cum[:, t * P - 1:t * P], None, ALU.add))
                link(dve.tensor_copy(cum[:, QT * P:(KT - 1) * P],
                                     pc[0:HEADS, 2:4, :].rearrange("p a n -> p (a n)")))
                past = cum[:, QT * P:(KT - 1) * P].rearrange("p (b k) -> p b k", b=STREAMS)
                link(dve.tensor_tensor(cum[:, (KT - 1) * P:].rearrange("p (b n) -> p b n", b=STREAMS),
                                       pc[0:HEADS, 4, 0:P].rearrange("p (b n) -> p b n", b=STREAMS),
                                       past[:, :, CACHED - 1:CACHED].to_broadcast([HEADS, STREAMS, NEW]), ALU.add))
                link(dve.tensor_scalar(ncum[:], cum[:], -1.0, None, ALU.mult))

            @block.tensor
            def _(pe):
                pe.wait_ge(split, 3)
                for s, (at, width) in enumerate(spans):
                    for c in range(KC):
                        last = product(pe, pf[0:HEADS, s, 0:width], wh[:, c, :], wl[:, c, :],
                                       xh[:, c, at:at + width], xl[:, c, at:at + width], c == 0, c == KC - 1)
                last.then_inc(f_ready, 1)
                pe.wait_ge(biased, 1)
                for t in range(NT):
                    last = pe.transpose(pf[:, 0, t * HEADS:(t + 1) * HEADS], z[:, t * P:(t + 1) * P],
                                        ident[0:HEADS, 0:HEADS])
                last.then_inc(turned, 1)
                pe.wait_ge(made, 3)
                for b in range(STREAMS):
                    pe.matmul(pc[0:HEADS, 2 + b // 4, (b % 4) * P:(b % 4 + 1) * P], clf[:, b, :], tri[:],
                              start=True, stop=True)
                pe.wait_ge(chain, 7)
                for t in range(QT):
                    pe.matmul(pc[0:HEADS, t // 4, (t % 4) * P:(t % 4 + 1) * P], lf[:, t, :], tri[:],
                              start=True, stop=True)
                pe.matmul(pc[0:HEADS, 4, 0:P], lf[:, QT, :], trib[:], start=True, stop=True).then_inc(summed, 1)
                pe.wait_ge(chain, 7 + QT + 2)
                for t in range(NT):
                    at = t * P if t < QT else (KT - 1) * P
                    last = pe.transpose(pf[:, 1, t * HEADS:(t + 1) * HEADS], cum[:, at:at + P],
                                        ident[0:HEADS, 0:HEADS])
                last.then_inc(cq_turned, 1)


def attention_block(nc, name, ident, ks_d, qh_d, ql_d, v_parts, out_d, cq=None, negcum=None, toep=None):
    fox = negcum is not None
    S = QT

    def width(i):
        return STREAMS + 1 if i == S else (i + 1 if fox else min(i, BAND_TILES) + 1)

    def first_key(i):
        return QT if i == S else i + 1 - width(i)

    by_turns = list(range(QT))
    order = [(0, S)] + [(0, i) for i in by_turns] + [(1, by_turns[0]), (1, S)] + [(1, i) for i in by_turns[1:]]
    U = len(order)
    groups = []
    for hh in (0, 1):
        groups += [(hh, (S,))] + [(hh, (i, i + 1)) for i in by_turns[0::2]]
    G = len(groups)
    GH = G // 2
    last_unit = [max(order.index((hh, i)) for i in tiles) for hh, tiles in groups]
    group_of = {(hh, i): g for g, (hh, tiles) in enumerate(groups) for i in tiles}
    last_of_head = [max(n for n, (hh, _) in enumerate(order) if hh == x) for x in (0, 1)]
    first_of_head = [min(n for n, (hh, _) in enumerate(order) if hh == x) for x in (0, 1)]

    rounds_of, r = [], 0
    for hh, i in order:
        mine = [(j, min(4, width(i) - j)) for j in range(0, width(i), 4)]
        rounds_of.append((r, mine))
        r += len(mine)
    R = r
    TB = 3
    SMALL = 6
    VSLICES = [(0, 6), (6, 12), (12, KT)]
    NV = len(VSLICES)
    vslice_at = {step + k: (hh, k) for hh, step in ((0, 2), (1, 7)) for k in range(NV)}
    assert last_unit == sorted(last_unit) and G % 2 == 0 and R % TB == 0 and U % SMALL == 0
    assert all(n % 2 == 0 for n, (_, i) in enumerate(order) if i == S)

    def rounds_through(n):
        return rounds_of[n][0] + len(rounds_of[n][1])

    MAX, EXP, NORM, TURN, FIRST, OTHERS, VALUES, OUT = 1, 2, 3, 4, 4, 5, 6, 7
    wide = (STREAMS + 1) * P
    fives = U % 4
    slot_of = [x for run in [4] * ((U - 5 * fives) // 4) + [5] * fives for x in range(run)]
    assert len(slot_of) == U
    prompt_groups = [g for g, (_, tiles) in enumerate(groups) if tiles != (S,)]
    sample_groups = [g for g, (_, tiles) in enumerate(groups) if tiles == (S,)]
    assert len(prompt_groups) % 2 == 0

    def through_before(g):
        kin, apart = (prompt_groups, 2) if g in prompt_groups else (sample_groups, 1)
        k = kin.index(g) - apart
        return kin[k] + 1 if k >= 0 else kin[k] + 1 - G
    samples = [n for n, (_, i) in enumerate(order) if i == S]
    values_step = [n + VALUES + ((n + VALUES) % U in samples) for n in last_unit]
    out_step = [v + OUT - VALUES for v in values_step]
    assert all(b > a for a, b in zip(values_step, values_step[1:])) and values_step[-1] < values_step[0] + U

    with Phase(nc, name) as ph:
        vraw = ph.sb("vraw", [P, KT, P])
        ks = [ph.sb(f"ks{i}", [P, KT * P], F32R) for i in range(2)]
        vs = [ph.sb(f"vs{i}", [P, KT, P], F32R) for i in range(2)]
        qh = [ph.sb(f"qh{i}", [P, TOK], F32R) for i in range(2)]
        ql = [ph.sb(f"ql{i}", [P, TOK], F32R) for i in range(2)]
        group_wide = 2 * P * (QT if fox else BAND_TILES + 2)
        pth = ph.sb("pth", [P, 2, group_wide], F32R)
        ptl = ph.sb("ptl", [P, 2, group_wide], F32R)
        sth = ph.sb("sth", [P, wide], F32R)
        stl = ph.sb("stl", [P, wide], F32R)
        pr = [ph.sb(f"pr{i}", [P, wide]) for i in range(5 if fives else 4)]
        mneg = ph.sb("mneg", [P, SMALL])
        rowsum = ph.sb("rowsum", [P, SMALL])
        inv = ph.sb("inv", [P, SMALL])
        half_out = ph.sb("half_out", [HD, 2 * P])
        att = ph.sb("att", [P, TOK])
        own_raw = ph.sb("own_raw", [P, P])
        own = ph.sb("own", [P, P], F32R)
        others = ph.sb("others", [P, wide], F32R)
        if fox:
            ncb = [ph.sb(f"ncb{i}", [P, KT * P]) for i in range(2)]
            diag = ph.sb("diag", [P, QT, P])
            bias = [ph.sb(f"bias{i}", [P, wide]) for i in range(2)]
            cqh = [ph.sb(f"cqh{i}", [P, NT]) for i in range(2)]
            cq_done, samp_chain = ph.sem("cq_done"), ph.sem("samp_chain")
        else:
            toe = [ph.sb(f"toe{i}", [P, TOEP - P]) for i in range(2)]
            toes = [ph.sb(f"toes{i}", [P, CACHED + NEW]) for i in range(2)]
            bs = [ph.sb(f"bs{i}", [P, wide]) for i in range(2)]
            spread_done = ph.sem("spread_done")
        sp_wide = ph.ps("sp_wide", [P, 3 * WC])
        sp_slim = ph.ps("sp_slim", [P, 2 * WC])
        tp = ph.ps("tp", [P, TB, WC])
        scores = [sp_wide, sp_slim]
        op = sp_wide[:, 3 * WC - 2 * P:3 * WC]

        kq_loaded = [ph.sem(f"kq_loaded{i}") for i in range(2)]
        b_loaded = [ph.sem(f"b_loaded{i}") for i in range(2)]
        v_loaded = ph.sem("v_loaded")
        t_done, th_done, tl_done = ph.sem("t_done"), ph.sem("th_done"), ph.sem("tl_done")
        vh_done, vl_done = ph.sem("vh_done"), ph.sem("vl_done")
        qk_done, max_done, exp_done, inv_done, norm_done = (ph.sem(s) for s in
            ("qk_done", "max_done", "exp_done", "inv_done", "norm_done"))
        bias_done, diag_made = ph.sem("bias_done"), ph.sem("diag_made")
        mask_made, mask_ready = ph.sem("mask_made"), ph.sem("mask_ready")
        pv_done, half_done, o_done = (ph.sem(s) for s in ("pv_done", "half_done", "o_done"))
        att_stored = [ph.sem(f"att_stored{i}") for i in range(2)]
        waited = {e: ph.sem(e + "_waited") for e in ("pool", "dve")}

        def settle(eng, which="pool"):
            eng.sem_inc(waited[which], 1)

        def stage_units(p, first, step, lag):
            n = step - lag
            if n >= U:
                return
            if n >= 0:
                yield n, p
            elif not first:
                yield n + U, p - 1

        def pairs_loop(eng, steps):
            steps(0, range(U), True)
            with eng.Fori(1, PAIRS) as p:
                steps(p, range(U), False)
            steps(PAIRS - 1, range(U, out_step[-1] + 1), False)

        def groups_at(p, first, step, steps_of):
            for g, s in enumerate(steps_of):
                if s == step:
                    yield g, p
                elif s == step + U and not first:
                    yield g, p - 1

        def group_slots(g):
            if g in sample_groups:
                return sth[:], stl[:]
            k = prompt_groups.index(g) % 2
            return pth[:, k, :], ptl[:, k, :]

        def splits(n, part):
            hh, i = order[n]
            g = group_of[(hh, i)]
            tiles = groups[g][1]
            base, mine = rounds_of[n]
            for k, (j, cnt) in enumerate(mine):
                if (k == 0) != (part == FIRST):
                    continue
                out = []
                for buf in group_slots(g):
                    if i == S:
                        v = buf[:, j * P:(j + cnt) * P].rearrange("p (k q) -> p k q", q=P)
                    else:
                        kb = first_key(i) - first_key(tiles[0]) + j
                        off = (i - tiles[0]) * P
                        v = buf.rearrange("p (k q) -> p k q", q=2 * P)[:, kb:kb + cnt, off:off + P]
                    out.append(v)
                yield base + k, cnt, g, out[0], out[1]

        with nc.Block() as block:
            @block.sync
            def _(sp):
                def load_head(p, hh):
                    wait(sp, qk_done, (p - 1) * U + last_of_head[hh] + 1)
                    head = bass.ds(p * 2 + hh, 1)
                    for buf, src in ((ks, ks_d), (qh, qh_d), (ql, ql_d)):
                        sp.dma_start(f32(buf[hh][:]), src[head].rearrange("o p n -> (o p) n")
                                     ).then_inc(kq_loaded[hh], 16)
                    if fox:
                        wait(sp, bias_done, (p - 1) * U + last_of_head[hh] + 1)
                        sp.dma_start(ncb[hh][:], negcum[head, :].to_broadcast([P, KT * P])).then_inc(b_loaded[hh], 16)
                    else:
                        wait(sp, max_done, (p - 1) * U + last_of_head[hh] + 1)
                        for buf, src in ((toe, toep[0]), (toes, toep[1])):
                            sp.dma_start(buf[hh][:], src[head].rearrange("o p n -> (o p) n")
                                         ).then_inc(b_loaded[hh], 16)

                def load_values(p):
                    wait(sp, vl_done, 2 * NV * p)
                    for at, n, src in v_parts:
                        sp.dma_start(vraw[:, at:at + n, :], src(bass.ds(p * P, P))).then_inc(v_loaded, 16)

                def store_head(p, hh):
                    sp.wait_ge(o_done, p * G + (hh + 1) * GH)
                    sp.dma_start(out_d[bass.ds(p * P + hh * HD, HD), :], att[hh * HD:(hh + 1) * HD, :]
                                 ).then_inc(att_stored[hh], 16)

                load_head(0, 0)
                load_values(0)
                load_head(0, 1)
                with sp.Fori(0, PAIRS - 1) as p:
                    load_head(p + 1, 0)
                    store_head(p, 0)
                    load_values(p + 1)
                    load_head(p + 1, 1)
                    store_head(p, 1)
                store_head(PAIRS - 1, 0)
                store_head(PAIRS - 1, 1)
                for hh in range(2):
                    sp.wait_ge(att_stored[hh], 16 * PAIRS)

            @block.gpsimd
            def _(pool):
                def values_low(p, step):
                    if step - 1 in vslice_at:
                        hh, k = vslice_at[step - 1]
                        k0, k1 = VSLICES[k]
                        pool.wait_ge(vh_done, (2 * p + hh) * NV + k + 1)
                        settle(pool)
                        pool.tensor_tensor(out=vs[hh][:, k0:k1, HD:P], in0=vraw[:, k0:k1, hh * HD:(hh + 1) * HD],
                                           in1=f32(vs[hh][:, k0:k1, 0:HD]), op=ALU.subtract).then_inc(vl_done, 1)

                def diagonal(p, hh):
                    pool.wait_ge(b_loaded[hh], (p + 1) * 16)
                    wait(pool, bias_done, p * U + (first_of_head[1] if hh else 0))
                    settle(pool)
                    pool.affine_select(out=diag[:], in_=ncb[hh][:, 0:QT * P].rearrange("p (t k) -> p t k", t=QT),
                                       compare_op=ALU.is_ge, fill=NEG, base=0, pattern=[[0, QT], [-1, P]],
                                       channel_multiplier=1).then_inc(diag_made, 1)
                    pool.tensor_copy(cqh[hh][:], cq[:, :, bass.ds(p * 2 + hh, 1)].rearrange("p t o -> p (t o)")
                                     ).then_inc(cq_done, 1)
                    pool.wait_ge(cq_done, 2 * p + hh + 1)
                    pool.wait_ge(diag_made, 2 * p + hh + 1)

                def unit_bias(p, n):
                    hh, i = order[n]
                    wait(pool, max_done, p * U + n - 1)
                    settle(pool)
                    slot, cqs = bias[n % 2], cqh[hh]
                    if i == S:
                        pool.tensor_scalar(slot[:, 0:wide], ncb[hh][:, QT * P:], cqs[:, i:i + 1], 1.0,
                                           ALU.add, ALU.mult).then_inc(samp_chain, 1)
                        pool.wait_ge(samp_chain, 2 * p + hh + 1)
                        settle(pool)
                        new = slot[:, STREAMS * P:wide]
                        pool.affine_select(out=new, in_=new, compare_op=ALU.is_ge, fill=NEG, base=0,
                                           pattern=[[-1, P]], channel_multiplier=1).then_inc(bias_done, 1)
                    else:
                        if i:
                            pool.tensor_scalar(slot[:, 0:i * P], ncb[hh][:, 0:i * P], cqs[:, i:i + 1], 1.0,
                                               ALU.add, ALU.mult)
                        pool.tensor_scalar(slot[:, i * P:(i + 1) * P], diag[:, i, :], cqs[:, i:i + 1], 1.0,
                                           ALU.add, ALU.mult).then_inc(bias_done, 1)

                def band_bias(p, hh):
                    pool.wait_ge(b_loaded[hh], (p + 1) * 32)
                    wait(pool, max_done, (p - 1) * U + last_of_head[hh] + 1)
                    settle(pool)
                    for cols, base, mult in ((slice(TOEP - P - HD, TOEP - P), -HD, 1), (slice(0, HD), HD - 1, -1)):
                        last = pool.affine_select(out=toe[hh][:, cols], in_=toe[hh][:, cols], compare_op=ALU.is_ge,
                                                  fill=NEG, base=base, pattern=[[0, HD]], channel_multiplier=mult)
                    last.then_inc(bias_done, 1)

                def normalise(p, n):
                    w, s, m = width(order[n][1]) * P, slot_of[n], n % SMALL
                    pool.wait_ge(inv_done, p * U + n + 1)
                    settle(pool)
                    pool.tensor_scalar(pr[s][:, 0:w], pr[s][:, 0:w], inv[:, m:m + 1], 1.0,
                                       ALU.mult, ALU.mult).then_inc(norm_done, 1)

                stream_mask(pool, own_raw, pr[0], mask_made)

                def fox_pair(p, last=False):
                    for n in range(U):
                        hh = order[n][0]
                        if n in first_of_head:
                            diagonal(p, hh)
                        unit_bias(p, n)
                        values_low(p, n)

                def band_pair(p, last=False):
                    for n in range(U):
                        if n == first_of_head[1] - 4:
                            band_bias(p, 1)
                        if n == U - 4 and not last:
                            band_bias(p + 1, 0)
                        normalise(p, n)
                        values_low(p, n + NORM)

                pair = fox_pair if fox else band_pair
                if not fox:
                    band_bias(0, 0)
                pair(0)
                with pool.Fori(1, PAIRS - 1) as p:
                    pair(p)
                pair(PAIRS - 1, last=True)

            @block.scalar
            def _(act):
                def high(p, first, step, part):
                    for n, pp in stage_units(p, first, step, part):
                        for r, cnt, g, hi, _ in splits(n, part):
                            act.wait_ge(t_done, pp * R + r + 1)
                            wait(act, pv_done, pp * G + through_before(g))
                            act.activation(hi, tp[:, r % TB, 0:cnt * P].rearrange("p (k q) -> p k q", q=P),
                                           ACT.Copy).then_inc(th_done, 1)

                def values_high(p, step):
                    if step in vslice_at:
                        hh, k = vslice_at[step]
                        k0, k1 = VSLICES[k]
                        if (hh, k) == (0, 0):
                            act.wait_ge(v_loaded, (p + 1) * 16 * len(v_parts))
                        if k == 0:
                            wait(act, pv_done, (p - 1) * G + (hh + 1) * GH)
                        act.activation(vs[hh][:, k0:k1, 0:HD], vraw[:, k0:k1, hh * HD:(hh + 1) * HD], ACT.Copy
                                       ).then_inc(vh_done, 1)

                def spread(p, step):
                    for hh in range(2):
                        if step != samples[hh]:
                            continue
                        act.wait_ge(b_loaded[hh], (p + 1) * 32)
                        wait(act, max_done, (p - 1) * U + samples[hh] + 1)
                        for at, k0, k1 in ((0, 0, CACHED), (STREAMS * CACHED, CACHED, CACHED + NEW)):
                            last = act.activation(
                                bs[hh][:, at:at + STREAMS * (k1 - k0)].rearrange("p (b k) -> p b k", b=STREAMS),
                                toes[hh][:, k0:k1].rearrange("p (o k) -> p o k", o=1)
                                .to_broadcast([P, STREAMS, k1 - k0]), ACT.Copy)
                        last.then_inc(spread_done, 1)

                def steps(p, rng, first):
                    for step in rng:
                        high(p, first, step, OTHERS)
                        for n, pp in stage_units(p, first, step, EXP):
                            w, s, m = width(order[n][1]) * P, slot_of[n], n % SMALL
                            act.wait_ge(max_done, pp * U + n + 1)
                            act.activation(pr[s][:, 0:w], pr[s][:, 0:w], ACT.Exp, bias=mneg[:, m:m + 1],
                                           scale=-1.0, accum_out=rowsum[:, m:m + 1]).then_inc(exp_done, 1)
                        for g, pp in groups_at(p, first, step, out_step):
                            w = P * len(groups[g][1])
                            act.wait_ge(pv_done, pp * G + g + 1)
                            wait(act, o_done, pp * G + g)
                            act.activation(half_out[:, 0:w], op[HD:P, 0:w], ACT.Copy).then_inc(half_done, 1)
                        high(p, first, step, FIRST)
                        values_high(p, step)
                        if not fox:
                            spread(p, step)

                act.wait_ge(mask_made, 5)
                act.activation(own[:], own_raw[:], ACT.Copy).then_inc(mask_ready, 1)
                act.activation(others[:], pr[0][:], ACT.Copy).then_inc(mask_ready, 1)
                pairs_loop(act, steps)

            @block.vector
            def _(dve):
                def low(p, first, step, part):
                    for n, pp in stage_units(p, first, step, part):
                        for r, cnt, g, hi, lo in splits(n, part):
                            dve.wait_ge(th_done, pp * R + r + 1)
                            dve.tensor_tensor(lo, tp[:, r % TB, 0:cnt * P].rearrange("p (k q) -> p k q", q=P),
                                              f32(hi), ALU.subtract).then_inc(tl_done, 1)

                def steps(p, rng, first):
                    for step in rng:
                        for n, pp in stage_units(p, first, step, NORM):
                            w, s, m = width(order[n][1]) * P, slot_of[n], n % SMALL
                            dve.wait_ge(exp_done, pp * U + n + 1)
                            dve.reciprocal(inv[:, m:m + 1], rowsum[:, m:m + 1]).then_inc(inv_done, 1)
                            if fox:
                                dve.wait_ge(inv_done, pp * U + n + 1)
                                dve.tensor_scalar(pr[s][:, 0:w], pr[s][:, 0:w], inv[:, m:m + 1], None,
                                                  ALU.mult).then_inc(norm_done, 1)
                        low(p, first, step, OTHERS)
                        for n, pp in stage_units(p, first, step, MAX):
                            hh, i = order[n]
                            w, s, m = width(i) * P, slot_of[n], n % SMALL
                            dve.wait_ge(qk_done, pp * U + n + 1)
                            if fox:
                                dve.wait_ge(bias_done, pp * U + n + 1)
                                b = bias[n % 2][:, 0:w]
                            else:
                                dve.wait_ge(*((spread_done, pp * 2 + hh + 1) if i == S else (bias_done, pp * 2 + hh + 1)))
                                b = bs[hh][:, 0:w] if i == S else toe[hh][:, TOEP - P - w:TOEP - P]
                            wait(dve, t_done, pp * R + (rounds_through(n - 4) if n >= 4 else rounds_through(n - 4 + U) - R))
                            if not isinstance(pp, int):
                                settle(dve, "dve")
                            dve.tensor_tensor_reduce(out=pr[s][:, 0:w], in0=scores[n % 2][:, 0:w], in1=b,
                                                     scale=-1.0, scalar=BIG, op0=ALU.add, op1=ALU.min,
                                                     accum_out=mneg[:, m:m + 1]).then_inc(max_done, 1)
                        for g, pp in groups_at(p, first, step, out_step):
                            hh, tiles = groups[g]
                            w = P * len(tiles)
                            dve.wait_ge(half_done, pp * G + g + 1)
                            if g % GH == 0:
                                wait(dve, att_stored[hh], 16 * pp)
                            dve.tensor_tensor(att[hh * HD:(hh + 1) * HD, tiles[0] * P:tiles[0] * P + w],
                                              op[0:HD, 0:w], half_out[:, 0:w], ALU.add).then_inc(o_done, 1)
                        low(p, first, step, FIRST)

                pairs_loop(dve, steps)

            @block.tensor
            def _(pe):
                def score(p, n):
                    hh, i = order[n]
                    if n in first_of_head:
                        pe.wait_ge(kq_loaded[hh], (p + 1) * 48)
                    wait(pe, max_done, p * U + n - 1)
                    if i == S:
                        wait(pe, o_done, p * G + sum(v < n for v in values_step)
                             - sum(v >= U + n for v in values_step))
                    q = slice(i * P, (i + 1) * P)
                    for j in range(0, width(i), 4):
                        cnt = min(4, width(i) - j)
                        keys = slice((first_key(i) + j) * P, (first_key(i) + j + cnt) * P)
                        out = scores[n % 2][:, j * P:(j + cnt) * P]
                        pe.matmul(out, qh[hh][:, q], ks[hh][:, keys], start=True, stop=False)
                        last = pe.matmul(out, ql[hh][:, q], ks[hh][:, keys], start=False, stop=i != S)
                        if i == S:
                            last = pe.matmul(out, own[:], others[:, j * P:(j + cnt) * P], start=False, stop=True)
                    last.then_inc(qk_done, 1)

                def values(p, g, scored):
                    hh, tiles = groups[g]
                    if g % GH == 0:
                        pe.wait_ge(vl_done, (2 * p + hh + 1) * NV)
                    wait(pe, o_done, p * G + g)
                    if scored is not None:
                        pe.wait_ge(max_done, scored)
                    pe.wait_ge(tl_done, p * R + rounds_through(last_unit[g]))
                    k0 = first_key(tiles[0])
                    todo = []
                    for kb in range(k0, first_key(tiles[-1]) + width(tiles[-1])):
                        inside = [x for x in range(len(tiles))
                                  if first_key(tiles[x]) <= kb < first_key(tiles[x]) + width(tiles[x])]
                        todo.append((len(inside) < len(tiles), kb, inside[0] * P, len(inside) * P))
                    todo.sort()
                    step = P * len(tiles)
                    for x, (_, kb, off, w) in enumerate(todo):
                        at = (kb - k0) * step + off
                        for y, buf in enumerate(group_slots(g)):
                            last = pe.matmul(op[:, off:off + w], vs[hh][:, kb, :], buf[:, at:at + w],
                                             start=x == 0 and y == 0, stop=x == len(todo) - 1 and y == 1)
                    last.then_inc(pv_done, 1)

                def turn(p, first, step):
                    for n, pp in stage_units(p, first, step, TURN):
                        base, mine = rounds_of[n]
                        pe.wait_ge(norm_done, pp * U + n + 1)
                        for k, (j, cnt) in enumerate(mine):
                            wait(pe, tl_done, pp * R + base + k - TB + 1)
                            for b in range(cnt):
                                last = pe.transpose(tp[:, (base + k) % TB, b * P:(b + 1) * P],
                                                    pr[slot_of[n]][:, (j + b) * P:(j + b + 1) * P], ident[:])
                            last.then_inc(t_done, 1)

                def steps(p, rng, first):
                    scored = None
                    for step in rng:
                        turn(p, first, step)
                        for n, pp in stage_units(p, first, step, 0):
                            score(pp, n)
                            if n in samples:
                                scored = pp * U + n + 1
                        for g, pp in groups_at(p, first, step, values_step):
                            values(pp, g, scored)
                            scored = None
                    assert scored is None

                pe.wait_ge(mask_ready, 2)
                pairs_loop(pe, steps)


def slid(rows_ap, start, rows, cols):
    return bass.AP(tensor=rows_ap.tensor, offset=start, ap=[[rows_ap.shape[1], rows_ap.shape[0]], [-1, rows], [1, cols]])


class Distances:

    def __init__(self, ph, rel_ap, line, toep):
        self.rel_ap, self.line, self.toep = rel_ap, line, toep
        self.rb = ph.sb("rb", [HEADS, NREL])
        self.row = ph.sb("row", [HEADS, TOEP])
        self.loaded, self.made = ph.sem("rel_loaded"), ph.sem("row_made")
        self.line_stored, self.bias_stored = ph.sem("line_stored"), ph.sem("bias_stored")

    def sync(self, sp):
        sp.dma_start(self.rb[:], self.rel_ap).then_inc(self.loaded, 16)
        sp.wait_ge(self.made, 2)
        sp.dma_start(self.line, self.row[:]).then_inc(self.line_stored, 16)
        sp.wait_ge(self.line_stored, 16)
        sp.dma_start(self.toep[0], slid(self.line, P - 1, P, TOEP - P)).then_inc(self.bias_stored, 16)
        for b in range(STREAMS):
            sp.dma_start(self.toep[1][:, b * NEW:(b + 1) * NEW, :],
                         slid(self.line, 4 * P - 1, NEW, CACHED + NEW)).then_inc(self.bias_stored, 16)
        sp.wait_ge(self.bias_stored, 16 * (1 + STREAMS))

    def act(self, act):
        far = TOEP - NREL
        act.wait_ge(self.loaded, 16)
        act.activation(self.row[:, far:], self.rb[:, ::-1], ACT.Copy).then_inc(self.made, 1)
        act.activation(self.row[:, 0:far], self.rb[:, NREL - 1:NREL].to_broadcast([HEADS, far]), ACT.Copy
                       ).then_inc(self.made, 1)


class Final:

    def __init__(self, ph, norm, h, g_ap, y_of):
        self.h, self.g_ap, self.y_of, self.norm = h, g_ap, y_of, norm
        self.g = ph.sb("g_final", [P, D])
        self.g_loaded, self.y_ready = ph.sem("g_final_loaded"), ph.sem("y_ready")
        self.stored = [ph.sem(f"y_stored{i}") for i in range(2)]

    def load(self, sp):
        sp.dma_start(self.g[:], self.g_ap.partition_broadcast(P)).then_inc(self.g_loaded, 16)

    def squares(self, act, t, done, before):
        act.wait_ge(done, before + t + 1)
        act.wait_ge(self.norm.squared, NT + t)
        act.activation(self.norm.sq[:], self.h[:, t, :], ACT.Square,
                       accum_out=self.norm.ss[:, t:t + 1]).then_inc(self.norm.squared, 1)

    def rsqrt(self, pool, t):
        n = self.norm
        pool.wait_ge(n.squared, NT + t + 1)
        pool.tensor_scalar(n.ms[:, t:t + 1], n.ss[:, t:t + 1], 1.0 / D, EPS,
                           ALU.mult, ALU.add).then_inc(n.mean_ready, 1)
        pool.wait_ge(n.mean_ready, NT + t + 1)
        pool.tensor_tensor(out=n.rs[:, t:t + 1], in0=n.ms[:, t:t + 1], in1=n.half[:],
                           op=ALU.pow).then_inc(n.rs_ready, 1)

    def scaled(self, dve, t):
        if t == 0:
            dve.wait_ge(self.g_loaded, 16)
        dve.wait_ge(self.norm.rs_ready, NT + t + 1)
        if t >= 2:
            dve.wait_ge(self.stored[t % 2], 16 * (t // 2))
        dve.scalar_tensor_tensor(self.norm.xn[:, t % 2, :], self.h[:, t, :], self.norm.rs[:, t:t + 1], self.g[:],
                                 ALU.mult, ALU.mult).then_inc(self.y_ready, 1)

    def store(self, sp, t):
        sp.wait_ge(self.y_ready, t + 1)
        sp.dma_start(self.y_of(t), self.norm.xn[:, t % 2, :]).then_inc(self.stored[t % 2], 16)

    def all_stored(self, sp):
        for i in range(2):
            sp.wait_ge(self.stored[i], 16 * ((NT + 1 - i) // 2))


def ffn_block(nc, name, h, ident, half, gain, wgu, wdn, final=None, aside=None):
    with Phase(nc, name) as ph:
        xh = ph.sb("xh", [P, KC, TOK], F32R)
        xl = ph.sb("xl", [P, KC, TOK], F32R)
        graw = ph.sb("graw", [P, KC, 2, GW])
        gh = ph.sb("gh", [P, KC, 2 * GW], F32R)
        gl = ph.sb("gl", [P, KC, 2 * GW], F32R)
        draw = ph.sb("draw", [P, GC, D])
        dh = ph.sb("dh", [P, GC, D], F32R)
        dl = ph.sb("dl", [P, GC, D], F32R)
        gu = ph.ps("gu", [P, 2, WC])
        ptr = ph.ps("ptr", [P, 2, WC])
        tps = ph.ps("tps", [P, WC])
        dn = ph.ps("dn", [P, 2, WC])
        gate = ph.sb("gate", [P, GW])
        hid = ph.sb("hid", [P, GW])
        hidh = ph.sb("hidh", [P, GC, P], F32R)
        hidl = ph.sb("hidl", [P, GC, P], F32R)
        src = Norm(ph, h, ident, half, xh, xl, ptr)
        end = Final(ph, src, h, *final) if final else None
        piece_loaded = [ph.sem(f"piece_loaded{i}") for i in range(PIECES)]
        g_loaded, d_loaded = ph.sem("gu_loaded"), ph.sem("dn_loaded")
        gh_ready, gl_ready, g_used = ph.sem("gh_ready"), ph.sem("gl_ready"), ph.sem("g_used")
        dh_ready, dl_ready = ph.sem("dh_ready"), ph.sem("dl_ready")
        gu_ready, gate_ready, hid_ready = ph.sem("gu_ready"), ph.sem("gate_ready"), ph.sem("hid_ready")
        hid_turned, hidh_ready, hidl_ready = ph.sem("hid_turned"), ph.sem("hidh_ready"), ph.sem("hidl_ready")
        dn_ready, dn_used = ph.sem("dn_ready"), ph.sem("dn_used")
        wg_v = wgu.rearrange("(c p) (u n) -> p c u n", p=P, u=2)
        wd_v = wdn.rearrange("(c p) n -> p c n", p=P)
        DS = GC * D // WC

        def is_first(g):
            return isinstance(g, int) and g == 0

        def split_gu_high(act, g, between=None):
            if not is_first(g):
                act.wait_ge(g_loaded, 16 * 2 * g)
            for c in range(KC):
                if is_first(g) and c % (KC // PIECES) == 0:
                    act.wait_ge(piece_loaded[c // (KC // PIECES)], 32)
                if not is_first(g):
                    if c < KC - 1:
                        act.wait_ge(g_used, (KC - 1) * (g - 1) + c + 1)
                    else:
                        act.wait_ge(gu_ready, NT * g)
                split_high(act, gh[:, c, :], graw[:, c].rearrange("p u n -> p (u n)"), gain, c).then_inc(gh_ready, 1)
                if between and c == 1:
                    between()

        def split_gu_low(dve, g, between=None):
            for c in range(KC):
                dve.wait_ge(gh_ready, KC * g + c + 1)
                split_low(dve, gl[:, c, :], graw[:, c].rearrange("p u n -> p (u n)"), gh[:, c, :],
                          gain, c).then_inc(gl_ready, 1)
                if between and c == 1:
                    between()

        def piece(buf, s):
            return buf[:, s // 2, (s % 2) * WC:(s % 2 + 1) * WC]

        def split_dn_high(act, g):
            act.wait_ge(d_loaded, 16 * (g + 1))
            if not is_first(g):
                act.wait_ge(dn_ready, NT * g)
            for s in range(DS):
                act.activation(piece(dh, s), piece(draw, s), ACT.Copy).then_inc(dh_ready, 1)

        def split_dn_low(dve, g):
            for s in range(DS):
                dve.wait_ge(dh_ready, DS * g + s + 1)
                dve.tensor_tensor(piece(dl, s), piece(draw, s), f32(piece(dh, s)),
                                  ALU.subtract).then_inc(dl_ready, 1)

        def up(pe, g, t):
            k = NT * g + t
            if not (is_first(g) and t < 2):
                pe.wait_ge(hid_ready, k - 1 if t else k)
            rows = slice(t * P, (t + 1) * P)
            for c in range(KC):
                if t == 0:
                    pe.wait_ge(gl_ready, KC * g + c + 1)
                last = product(pe, gu[:, t % 2, :], xh[:, c, rows], xl[:, c, rows], gh[:, c, :], gl[:, c, :],
                               c == 0, c == KC - 1)
                if t == NT - 1 and c < KC - 1:
                    last.then_inc(g_used, 1)
            last.then_inc(gu_ready, 1)

        def turn(pe, g, t):
            k = NT * g + t
            pe.wait_ge(hid_ready, k + 1)
            if not (is_first(g) and t == 0):
                pe.wait_ge(hidl_ready, k)
            for c in range(GC):
                last = pe.transpose(tps[:, c * P:(c + 1) * P], hid[:, c * P:(c + 1) * P], ident[:])
            last.then_inc(hid_turned, 1)

        def down(pe, g, t):
            k = NT * g + t
            pe.wait_ge(hidl_ready, k + 1)
            if t == 0:
                pe.wait_ge(dl_ready, DS * (g + 1))
            if not (is_first(g) and t == 0):
                pe.wait_ge(dn_used, k)
            for half_ in range(2):
                for c in range(GC):
                    w = slice(half_ * WC, (half_ + 1) * WC)
                    last = product(pe, dn[:, half_, :], hidh[:, c, :], hidl[:, c, :], dh[:, c, w], dl[:, c, w],
                                   c == 0, c == GC - 1)
            last.then_inc(dn_ready, 1)

        def silu(act, g, t):
            k = NT * g + t
            act.wait_ge(gu_ready, k + 1)
            if not (is_first(g) and t == 0):
                act.wait_ge(hid_ready, k)
            act.activation(gate[:], gu[:, t % 2, 0:GW], ACT.Silu).then_inc(gate_ready, 1)

        def hidden(dve, g, t):
            k = NT * g + t
            dve.wait_ge(gate_ready, k + 1)
            if not (is_first(g) and t == 0):
                dve.wait_ge(hid_turned, k)
            dve.tensor_tensor(hid[:], gu[:, t % 2, GW:2 * GW], gate[:], ALU.mult).then_inc(hid_ready, 1)

        def hid_high(act, g, t):
            k = NT * g + t
            act.wait_ge(hid_turned, k + 1)
            if not (is_first(g) and t == 0):
                act.wait_ge(dn_ready, k)
            act.activation(hidh[:].rearrange("p c n -> p (c n)"), tps[:, 0:GW], ACT.Copy).then_inc(hidh_ready, 1)

        def hid_low(dve, g, t):
            dve.wait_ge(hidh_ready, NT * g + t + 1)
            dve.tensor_tensor(hidl[:].rearrange("p c n -> p (c n)"), tps[:, 0:GW],
                              f32(hidh[:].rearrange("p c n -> p (c n)")), ALU.subtract).then_inc(hidl_ready, 1)

        def residual(dve, g, t):
            dve.wait_ge(dn_ready, NT * g + t + 1)
            dve.tensor_tensor(h[:, t, :], dn[:].rearrange("p a n -> p (a n)"), h[:, t, :],
                              ALU.add).then_inc(dn_used, 1)

        with nc.Block() as block:
            @block.sync
            def _(sp):
                def load_gu(g):
                    for u in range(2):
                        sp.dma_start(graw[:, :, u, :], wg_v[:, :, u, bass.ds(g * GW, GW)]).then_inc(g_loaded, 16)

                def load_dn(g):
                    sp.dma_start(draw[:], wd_v[:, bass.ds(g * GC, GC), :]).then_inc(d_loaded, 16)

                for i in range(PIECES):
                    part = slice(i * KC // PIECES, (i + 1) * KC // PIECES)
                    for u in range(2):
                        sp.dma_start(graw[:, part, u, :], wg_v[:, part, u, 0:GW]).then_inc(piece_loaded[i], 16)
                load_dn(0)
                if end:
                    end.load(sp)
                if aside:
                    sp.wait_ge(gl_ready, KC)
                    aside(sp)
                with sp.Fori(1, GROUPS) as g:
                    sp.wait_ge(gl_ready, KC * g)
                    load_gu(g)
                    sp.wait_ge(dl_ready, DS * g)
                    load_dn(g)
                if end:
                    for t in range(NT):
                        end.store(sp, t)
                    end.all_stored(sp)

            @block.gpsimd
            def _(pool):
                for t in range(NT):
                    src.rsqrt(pool, t)
                if end:
                    for t in range(NT):
                        end.rsqrt(pool, t)

            @block.scalar
            def _(act):
                def tile(g, t, more):
                    if t == NT - 1 and more:
                        split_gu_high(act, g + 1)
                    silu(act, g, t)
                    if t == 0:
                        split_dn_high(act, g)
                    hid_high(act, g, t)

                src.squares(act, 0)
                src.squares(act, 1)
                split_gu_high(act, 0, lambda: src.high(act, 0))
                for t in range(NT):
                    if t + 2 < NT:
                        src.squares(act, t + 2)
                    if t + 1 < NT:
                        src.high(act, t + 1)
                    tile(0, t, True)
                with act.Fori(1, GROUPS - 1) as g:
                    for t in range(NT):
                        tile(g, t, True)
                for t in range(NT):
                    tile(GROUPS - 1, t, False)
                    if end and t:
                        end.squares(act, t - 1, dn_used, NT * (GROUPS - 1))
                if end:
                    end.squares(act, NT - 1, dn_used, NT * (GROUPS - 1))

            @block.vector
            def _(dve):
                def tile(g, t, more, first):
                    if t == NT - 1 and more:
                        split_gu_low(dve, g + 1)
                    hidden(dve, g, t)
                    if not first:
                        if t:
                            residual(dve, g, t - 1)
                        else:
                            residual(dve, g - 1, NT - 1)
                    if t == 0:
                        split_dn_low(dve, g)
                    hid_low(dve, g, t)

                src.scaled(dve, 0)
                src.scaled(dve, 1)
                split_gu_low(dve, 0, lambda: src.low(dve, 0))
                for t in range(NT):
                    if t + 2 < NT:
                        src.scaled(dve, t + 2)
                    if t + 1 < NT:
                        src.low(dve, t + 1)
                    tile(0, t, True, t == 0)
                with dve.Fori(1, GROUPS - 1) as g:
                    for t in range(NT):
                        tile(g, t, True, False)
                for t in range(NT):
                    tile(GROUPS - 1, t, False, False)
                    if end and t > 1:
                        end.scaled(dve, t - 2)
                residual(dve, GROUPS - 1, NT - 1)
                if end:
                    for t in range(NT - 2, NT):
                        end.scaled(dve, t)

            @block.tensor
            def _(pe):
                src.turn(pe, 0)
                for t in range(NT):
                    if t + 1 < NT:
                        src.turn(pe, t + 1)
                    src.ready(pe, t)
                    up(pe, 0, t)
                    if t:
                        down(pe, 0, t - 1)
                    turn(pe, 0, t)

                def group(g):
                    for t in range(NT):
                        up(pe, g, t)
                        if t:
                            down(pe, g, t - 1)
                        else:
                            down(pe, g - 1, NT - 1)
                        turn(pe, g, t)
                with pe.Fori(1, GROUPS - 1) as g:
                    group(g)
                group(GROUPS - 1)
                down(pe, GROUPS - 1, NT - 1)


def build(nc, a, o):
    (y_p, y_s, ak_p, av_p, lf_p, bk_p, bv_p, ak_s, av_s, lf_s, bk_s, bv_s) = o

    def flat(ap, pattern):
        return ap.rearrange(pattern)

    x_p = a["x_prompt"][0]
    x_s = flat(a["x_sample"], "b t d -> (b t) d")
    y_p, y_s = y_p[0], flat(y_s, "b t d -> (b t) d")
    akp, avp = (flat(x[0, 0], "t h d -> t (h d)") for x in (ak_p, av_p))
    aks, avs = (flat(x[0], "b t h d -> (b t) (h d)") for x in (ak_s, av_s))
    lfp, lfs = lf_p[0, 0], flat(lf_s[0], "b t h -> (b t) h")
    bkp, bvp = (flat(x[0], "t h d -> t (h d)") for x in (bk_p, bv_p))
    bks, bvs = (flat(x, "b t h d -> b t (h d)") for x in (bk_s, bv_s))
    cak, cav = (flat(a[n][0], "b t h d -> b t (h d)") for n in ("cache_a_k", "cache_a_v"))
    cbk, cbv = (flat(a[n], "b t h d -> b t (h d)") for n in ("cache_b_k", "cache_b_v"))

    def scratch(name, shape):
        return nc.dram_tensor(name, shape, F32, kind="Internal").ap()

    qh_d, ql_d = scratch("q_high", (HEADS, P, TOK)), scratch("q_low", (HEADS, P, TOK))
    ks_d = scratch("k_split", (HEADS, P, KT * P))
    vb_d = scratch("band_v", (TOK, D))
    at_d = scratch("attn_turned", (D, TOK))
    negcum = scratch("negcum", (HEADS, KT * P))
    line = scratch("distances", (HEADS, TOEP))
    toep = scratch("band_bias", (HEADS, P, TOEP - P)), scratch("stream_bias", (HEADS, P, CACHED + NEW))

    def weights(w, at=0):
        v = w.rearrange("(c p) n -> p c n", p=P)
        return lambda n: v[:, :, bass.ds(n * WC + at, WC)]

    def turned_stores(kind, i, t, high, low):
        if kind == "q":
            to = [(qh_d, u * HD, t, high) for u in range(2)] + [(ql_d, u * HD, t, low) for u in range(2)]
        else:
            to = split_to(high, low, t)
        return place(i, to)

    def split_to(high, low, t):
        return [(ks_d, 0, t, high), (ks_d, HD, t, low)]

    def place(i, to):
        out = []
        for dst, row, t, src in to:
            for hh in range(2):
                heads = dst[i * 8:(i + 1) * 8].rearrange("(j x) r n -> x r j n", x=2)[hh]
                out.append((heads[row:row + HD, :, t * P:(t + 1) * P],
                            None if src is None else
                            src[hh * HD:(hh + 1) * HD, :].rearrange("r (j n) -> r j n", n=P)))
        return out

    def cached_stores(i, b, high, low):
        return place(i, split_to(high, low, QT + b))

    def new_key_tile(kind, t):
        return KT - 1 if kind == "k" and t == QT else t

    def fox_turned(kind, i, t, high, low):
        return turned_stores(kind, i, new_key_tile(kind, t), high, low)

    def fox_stage(kind, i, t, s):
        prompt, sample = (akp, aks) if kind == "k" else (avp, avs)
        dst = prompt[t * P:(t + 1) * P] if t < QT else sample
        return [(dst[:, i * WC:(i + 1) * WC], s)]

    def band_stage(kind, i, t, s):
        full, kept_p, kept_s = (None, bkp, bks) if kind == "k" else (vb_d, bvp, bvs)
        cols = slice(i * WC, (i + 1) * WC)
        out = [(full[t * P:(t + 1) * P, cols], s)] if kind == "v" else []
        if t == QT:
            out.append((kept_s[:, CACHED - NEW:, cols], s))
        elif t >= QT // 2:
            out.append((kept_p[(t - QT // 2) * P:(t - QT // 2 + 1) * P, cols], s))
        return out

    def parts(prompt, cached, new):
        return [(0, QT, lambda c: prompt[:, c].rearrange("(t p) n -> p t n", p=P)),
                (QT, STREAMS, lambda c: cached[:, :, c].rearrange("b p n -> p b n")),
                (QT + STREAMS, 1, lambda c: new[:, c].rearrange("(o p) n -> p o n", o=1))]

    with Phase(nc, "all") as al:
        h = al.sb("h", [P, NT, D])
        ident = al.sb("ident", [P, P])
        half = al.sb("half", [P, 1])
        cq = al.sb("cq", [P, NT, HEADS])
        x_in = [al.sem(f"x_in{t}") for t in range(NT)]
        kept = al.sem("kept")

        def load_x(sp, t0, t1):
            for t in range(t0, t1):
                sp.dma_start(h[:, t, :], x_p[t * P:(t + 1) * P, :] if t < QT else x_s).then_inc(x_in[t], 16)

        def keep_rows(sp):
            for dst, src in ((bks, cbk), (bvs, cbv)):
                sp.dma_start(dst[:, 0:CACHED - NEW, :], src[:, NEW:, :]).then_inc(kept, 16)

        names = ("attn0", "ffn0", "kv", "attn1", "ffn1")
        gains = al.sb("gains", [P, len(names), KC])
        gain = {n: gains[:, i, :] for i, n in enumerate(names)}
        gains_in = al.sem("gains_in")

        def load_gains(sp):
            with nc.allow_non_contiguous_dma("small"):
                for n, src in zip(names, (a["g_attn"][0], a["g_ffn"][0], a["g_kv"], a["g_attn"][1], a["g_ffn"][1])):
                    sp.dma_start(gain[n], src.rearrange("(c p) -> p c", p=P)).then_inc(gains_in, 16)

        setup_block(nc, ident, half, load_gains)
        w_in = a["w_a_in"][0]
        w_qkv = weights(w_in)
        dense_block(nc, "qkv", h, ident, half, lambda n: w_qkv((4, 0, 1, 2, 3, 5)[n]), "vqqkkv",
                    gain_of=lambda n: gain["attn0"], gains_loaded=(gains_in, 16 * len(names)),
                    stage_stores=fox_stage, turned_stores=fox_turned,
                    cached=lambda i, b: cak[b, :, i * WC:(i + 1) * WC], cached_stores=cached_stores,
                    x_in=x_in, load_x=load_x,
                    gate=lambda xh, xl: gate_block(nc, xh, xl, ident, gain["attn0"], w_in[:, 3 * D:], a["b_a_f"][0],
                                                   a["cache_a_logf"][0], lfp, lfs, negcum, cq))
        attention_block(nc, "fox", ident, ks_d, qh_d, ql_d, parts(avp, cav, avs), at_d, cq=cq, negcum=negcum)
        with Phase(nc, "dist") as dist:
            dense_block(nc, "aout", h, ident, half, weights(a["w_a_out"][0]), ("add", "add"), turned_src=at_d,
                        aside=Distances(dist, a["rel_bias"][0], line, toep))
        ffn_block(nc, "ffn0", h, ident, half, gain["ffn0"], a["w_gate_up"][0], a["w_down"][0], aside=keep_rows)
        w_kv, w_q = weights(a["w_kv"]), weights(a["w_b_q"][0])
        dense_block(nc, "band_in", h, ident, half, lambda n: w_q(n - 3) if n in (3, 4) else w_kv((2, 0, 1, 0, 0, 3)[n]),
                    "vkkqqv", gain_of=lambda n: gain["attn1" if n in (3, 4) else "kv"],
                    stage_stores=band_stage, turned_stores=fox_turned,
                    cached=lambda i, b: cbk[b, :, i * WC:(i + 1) * WC], cached_stores=cached_stores)
        attention_block(nc, "band", ident, ks_d, qh_d, ql_d, parts(vb_d[0:QT * P], cbv, vb_d[QT * P:]), at_d,
                        toep=toep)
        dense_block(nc, "bout", h, ident, half, weights(a["w_b_out"][0]), ("add", "add"), turned_src=at_d)
        ffn_block(nc, "ffn1", h, ident, half, gain["ffn1"], a["w_gate_up"][1], a["w_down"][1],
                  final=(a["g_final"], lambda t: y_p[t * P:(t + 1) * P, :] if t < QT else y_s))
        with nc.Block() as block:
            @block.sync
            def _(sp):
                sp.wait_ge(kept, 32)


OUTPUTS = [(1, 1024, 1024), (8, 16, 1024), (1, 1, 1024, 16, 64), (1, 1, 1024, 16, 64), (1, 1, 1024, 16),
           (1, 512, 16, 64), (1, 512, 16, 64), (1, 8, 16, 16, 64), (1, 8, 16, 16, 64), (1, 8, 16, 16),
           (8, 128, 16, 64), (8, 128, 16, 64)]
INPUTS = ["x_prompt", "x_sample", "cache_a_k", "cache_a_v", "cache_a_logf", "cache_b_k", "cache_b_v", "g_attn",
          "w_a_in", "b_a_f", "w_a_out", "w_b_q", "rel_bias", "w_b_out", "g_kv", "w_kv", "g_ffn", "w_gate_up",
          "w_down", "g_final"]


def kernel(**inputs):
    import numpy as np
    import concourse.bacc as bacc
    from concourse.bass_utils import run_bass_kernel_spmd

    nc = bacc.Bacc("TRN2", target_bir_lowering=False, num_devices=1)
    arrays, aps = {}, {}
    for name in INPUTS:
        x = np.ascontiguousarray(inputs[name])
        arrays[f"in_{name}"] = x
        aps[name] = nc.dram_tensor(f"in_{name}", x.shape, F32, kind="ExternalInput").ap()
    outs = [nc.dram_tensor(f"out_{i}", s, F32, kind="ExternalOutput").ap() for i, s in enumerate(OUTPUTS)]
    build(nc, aps, outs)
    r = run_bass_kernel_spmd(nc, [arrays], core_ids=[0])
    return tuple(r.results[0][f"out_{i}"] for i in range(len(OUTPUTS)))
```
